# Optimizing a Trainium2 kernel written in Bass

```python
import math
import jax, jax.numpy as jnp
from jax import lax
import numpy as np

D_MODEL = 1024
BATCH = 1
SEQ = 1024
DEPTH = 1

N_META = 16
DA_HEADS = 8
DA_HEAD_DIM = 64
DA_VDIM = 2 * DA_HEAD_DIM
DA_WIDTH = DA_HEADS * DA_VDIM
RET_HEADS = 4
RET_QK_DIM = D_MODEL // RET_HEADS
RET_V_DIM = 2 * D_MODEL // RET_HEADS
RET_WIDTH = RET_HEADS * RET_V_DIM
RET_CHUNK = 128
Q_BLOCK = 128
D_FF = 4 * D_MODEL
NORM_EPS = 1e-6

SPLITS = (
    DA_HEADS * 2 * DA_HEAD_DIM,
    DA_HEADS * 2 * DA_HEAD_DIM,
    DA_WIDTH,
    RET_HEADS * RET_QK_DIM,
    RET_HEADS * RET_QK_DIM,
    RET_WIDTH,
    RET_WIDTH,
    D_MODEL,
    D_MODEL,
)
D_IN = sum(SPLITS)
SPLIT_POINTS = tuple(int(c) for c in np.cumsum(SPLITS)[:-1])

kernel_name = "hybrid_diffattn_retention_gated_block"

def rmsnorm(x, g):
    xf = x.astype(jnp.float32)
    y = xf * lax.rsqrt(jnp.mean(xf * xf, axis=-1, keepdims=True) + NORM_EPS)
    return (y * g.astype(jnp.float32)).astype(x.dtype)

def head_rms(x):
    xf = x.astype(jnp.float32)
    return (xf * lax.rsqrt(jnp.mean(xf * xf, axis=-1, keepdims=True) + NORM_EPS)).astype(x.dtype)

def alibi_slopes(n):
    return 2.0 ** (-8.0 * (jnp.arange(n, dtype=jnp.float32) + 1.0) / n)

def lambda_init(layer):
    return 0.8 - 0.6 * math.exp(-0.3 * layer)

def diff_attention(q, k, v, lam, lam_init, head_g):
    B, L = q.shape[0], q.shape[1]
    scale = DA_HEAD_DIM ** -0.5
    slopes = alibi_slopes(DA_HEADS)
    pos = jnp.arange(L, dtype=jnp.int32)

    def attend(qb, qpos, kb, vb, kpos):
        s = jnp.einsum('bqhcd,bkhcd->bhcqk', qb, kb).astype(jnp.float32) * scale
        dist = (qpos[:, None] - kpos[None, :]).astype(jnp.float32)
        s = s - slopes[None, :, None, None, None] * dist
        s = jnp.where(dist >= 0, s, -jnp.inf)
        p = jax.nn.softmax(s, axis=-1)
        a = p[:, :, 0] - lam * p[:, :, 1]
        return jnp.einsum('bhqk,bkhd->bqhd', a.astype(vb.dtype), vb)

    o_meta = attend(q[:, :N_META], pos[:N_META], k[:, :N_META], v[:, :N_META], pos[:N_META])
    n_blk = (L - N_META) // Q_BLOCK
    q_real = q[:, N_META:].reshape(B, n_blk, Q_BLOCK, DA_HEADS, 2, DA_HEAD_DIM)
    q_real = jnp.moveaxis(q_real, 1, 0)

    def block_fn(args):
        qb, i = args
        qpos = N_META + i * Q_BLOCK + jnp.arange(Q_BLOCK, dtype=jnp.int32)
        return attend(qb, qpos, k, v, pos)

    o_real = lax.map(block_fn, (q_real, jnp.arange(n_blk, dtype=jnp.int32)))
    o_real = jnp.moveaxis(o_real, 0, 1).reshape(B, L - N_META, DA_HEADS, DA_VDIM)
    o = jnp.concatenate([o_meta, o_real], axis=1)
    o = rmsnorm(o, head_g) * (1.0 - lam_init)
    return o.reshape(B, L, DA_WIDTH)

def retention(q, k, v):
    B, L = q.shape[0], q.shape[1]
    log_gamma = jnp.log(1.0 - 2.0 ** (-5.0 - jnp.arange(RET_HEADS, dtype=jnp.float32)))
    k = k * (RET_QK_DIM ** -0.5)
    q, k, v = (jnp.transpose(t, (0, 2, 1, 3)) for t in (q, k, v))

    def intra_decay(n):
        i = jnp.arange(n, dtype=jnp.float32)
        diff = i[:, None] - i[None, :]
        dec = jnp.exp(jnp.maximum(diff, 0.0)[None] * log_gamma[:, None, None])
        return jnp.where(diff[None] >= 0, dec, 0.0)

    def end_decay(n):
        return jnp.exp((n - 1 - jnp.arange(n, dtype=jnp.float32))[None] * log_gamma[:, None])

    qm, km, vm = q[:, :, :N_META], k[:, :, :N_META], v[:, :, :N_META]
    o_meta = jnp.einsum('bhqk,bhke->bhqe',
                        jnp.einsum('bhqd,bhkd->bhqk', qm, km) * intra_decay(N_META), vm)
    state0 = jnp.einsum('bhkd,bhke->bhde', km * end_decay(N_META)[None, :, :, None], vm)

    n_chunk = (L - N_META) // RET_CHUNK
    def chunks(t):
        t = t[:, :, N_META:].reshape(B, RET_HEADS, n_chunk, RET_CHUNK, t.shape[-1])
        return jnp.moveaxis(t, 2, 0)

    d_c = intra_decay(RET_CHUNK)
    cross_dec = jnp.exp((jnp.arange(RET_CHUNK, dtype=jnp.float32) + 1.0)[None] * log_gamma[:, None])
    end_dec = end_decay(RET_CHUNK)
    chunk_dec = jnp.exp(RET_CHUNK * log_gamma)

    def step(S, inp):
        qc, kc, vc = inp
        inner = jnp.einsum('bhqk,bhke->bhqe', jnp.einsum('bhqd,bhkd->bhqk', qc, kc) * d_c, vc)
        cross = jnp.einsum('bhqd,bhde->bhqe', qc * cross_dec[None, :, :, None], S)
        S_new = S * chunk_dec[None, :, None, None] + jnp.einsum(
            'bhkd,bhke->bhde', kc * end_dec[None, :, :, None], vc)
        return S_new, inner + cross

    _, o_real = lax.scan(step, state0, (chunks(q), chunks(k), chunks(v)))
    o_real = jnp.moveaxis(o_real, 0, 2).reshape(B, RET_HEADS, L - N_META, RET_V_DIM)
    o = jnp.concatenate([o_meta, o_real], axis=2).astype(v.dtype)
    return jnp.transpose(o, (0, 2, 1, 3))

def setup_inputs(seed: int = 0) -> dict:
    key = jax.random.key(seed)
    ks = jax.random.split(key, 20)
    f = jnp.float32
    nrm = lambda k, shape, s: jax.random.normal(k, shape, f) * s
    return {
        "x": nrm(ks[0], (BATCH, SEQ, D_MODEL), 1.0),
        "meta_tokens": nrm(ks[1], (N_META, D_MODEL), 1.0),
        "norm_mix_g": 1.0 + nrm(ks[2], (DEPTH, D_MODEL), 0.02),
        "w_in": nrm(ks[3], (DEPTH, D_MODEL, D_IN), D_MODEL ** -0.5),
        "da_lambda_q1": nrm(ks[4], (DEPTH, DA_HEAD_DIM), 0.1),
        "da_lambda_k1": nrm(ks[5], (DEPTH, DA_HEAD_DIM), 0.1),
        "da_lambda_q2": nrm(ks[6], (DEPTH, DA_HEAD_DIM), 0.1),
        "da_lambda_k2": nrm(ks[7], (DEPTH, DA_HEAD_DIM), 0.1),
        "da_head_g": 1.0 + nrm(ks[8], (DEPTH, DA_VDIM), 0.02),
        "w_proj_da": nrm(ks[9], (DEPTH, DA_WIDTH, D_MODEL), DA_WIDTH ** -0.5),
        "w_proj_ret": nrm(ks[10], (DEPTH, RET_WIDTH, D_MODEL), RET_WIDTH ** -0.5),
        "w_out": nrm(ks[11], (DEPTH, D_MODEL, D_MODEL), D_MODEL ** -0.5),
        "norm_mlp_g": 1.0 + nrm(ks[12], (DEPTH, D_MODEL), 0.02),
        "w_up": nrm(ks[13], (DEPTH, D_MODEL, D_FF), D_MODEL ** -0.5),
        "w_down": nrm(ks[14], (DEPTH, D_FF, D_MODEL), D_FF ** -0.5),
        "final_norm_g": 1.0 + nrm(ks[15], (D_MODEL,), 0.02),
    }

def reference(x, meta_tokens, norm_mix_g, w_in, da_lambda_q1, da_lambda_k1, da_lambda_q2,
              da_lambda_k2, da_head_g, w_proj_da, w_proj_ret, w_out, norm_mlp_g, w_up,
              w_down, final_norm_g):
    B, S, D = x.shape
    L = S + N_META
    meta = jnp.broadcast_to(meta_tokens[None].astype(x.dtype), (B, N_META, D))
    h = jnp.concatenate([meta, x], axis=1)

    for layer in range(DEPTH):
        u = rmsnorm(h, norm_mix_g[layer])
        proj = u @ w_in[layer]
        qa, ka, va, qr, kr, vr, gr_out, g_a, g_r = jnp.split(proj, SPLIT_POINTS, axis=-1)

        lam_init = lambda_init(layer)
        lam = (jnp.exp(jnp.sum(da_lambda_q1[layer].astype(jnp.float32) * da_lambda_k1[layer].astype(jnp.float32)))
               - jnp.exp(jnp.sum(da_lambda_q2[layer].astype(jnp.float32) * da_lambda_k2[layer].astype(jnp.float32)))
               + lam_init)
        y_da = diff_attention(qa.reshape(B, L, DA_HEADS, 2, DA_HEAD_DIM),
                              ka.reshape(B, L, DA_HEADS, 2, DA_HEAD_DIM),
                              va.reshape(B, L, DA_HEADS, DA_VDIM),
                              lam, lam_init, da_head_g[layer])

        o_ret = retention(qr.reshape(B, L, RET_HEADS, RET_QK_DIM),
                          kr.reshape(B, L, RET_HEADS, RET_QK_DIM),
                          vr.reshape(B, L, RET_HEADS, RET_V_DIM))
        y_ret = head_rms(o_ret).reshape(B, L, RET_WIDTH) * jax.nn.silu(gr_out)

        merged = (jax.nn.sigmoid(g_a) * (y_da @ w_proj_da[layer])
                  + jax.nn.sigmoid(g_r) * (y_ret @ w_proj_ret[layer]))
        h = h + merged @ w_out[layer]

        u = rmsnorm(h, norm_mlp_g[layer])
        h = h + jnp.square(jax.nn.relu(u @ w_up[layer])) @ w_down[layer]

    out = rmsnorm(h, final_norm_g)
    return out[:, N_META:]


_drawn_inputs = setup_inputs


def setup_inputs(seed=0):
    import zlib

    import numpy as np

    out = dict(_drawn_inputs(seed))
    spreads = {}
    factors = {'norm_mix_g': 2.803,
     'da_lambda_k1': 4.238,
     'da_lambda_q2': 4.444,
     'da_head_g': 6.464,
     'norm_mlp_g': 3.403,
     'final_norm_g': 2.849}
    for name, (base, spread) in spreads.items():
        noise = np.random.default_rng([zlib.crc32(name.encode()), seed]).standard_normal(out[name].shape)
        drawn = base * np.exp(spread * noise) if base else spread * noise
        out[name] = __import__('jax').numpy.asarray(drawn.astype(out[name].dtype))
    for name, factor in factors.items():
        out[name] = (out[name] * factor).astype(out[name].dtype)
    return out
```

```python
import math
from contextlib import ExitStack, contextmanager

import numpy as np

import concourse.bass as bass
from concourse import mybir

F32 = mybir.dt.float32
F32R = mybir.dt.float32r
I32 = mybir.dt.int32
ALU = mybir.AluOpType
ACT = mybir.ActivationFunctionType
AX_X = mybir.AxisListType.X

P = 128
D = 1024
KT = D // P
META = 16
SEQ = 1024
L = META + SEQ
TT = SEQ // P
PAD = P - META
LP = PAD + L
BANK = 512
HALF = SEQ // 2
EPS = 1e-6
MAP_ORIGIN = 16512
MAP_SIZE = 53000

DA_HEADS = 8
DH = 64
LAM_INIT = 0.8 - 0.6 * math.exp(-0.3 * 0)
DA_SCALE = DH ** -0.5

RET_HEADS = 4
RDK = D // RET_HEADS
RDV = 2 * D // RET_HEADS
DKT = RDK // P
DVT = RDV // P

FF = 4 * D
FF_BLOCK = 4
N_BLOCKS = FF // P // FF_BLOCK

KV_PARTS = [(0, META + 3 * P), (META + 3 * P, META + 6 * P), (META + 6 * P, L)]
KV_TILES = [(0, 4), (4, 7), (7, 9)]
Q_PARTS = [(META, META + HALF), (META + HALF, L)]

T_DA = 3 * DA_HEADS
T_RET = 12 * RET_HEADS
T_RPROJ = 4 * RET_HEADS
T_RING = T_DA + T_RET + T_RPROJ + KT + 2 * KT + KT
T_ALL = T_RING + N_BLOCKS * 2 * FF_BLOCK
MLP_ORDER = [("up", 0), ("up", 1), ("down", 0), ("down", 1), ("up", 2), ("down", 2), ("up", 3), ("down", 3)]


class Tally:

    def __init__(self):
        self.n, self.turn, self.per = 0, None, 0

    def next(self, k=1):
        self.n += k
        return self.value()

    def value(self, back=0):
        v = self.n - back
        assert v > 0
        return v if self.turn is None else self.turn * self.per + v

    def value16(self):
        v = 16 * self.n
        assert v > 0
        return v if self.turn is None else self.turn * (16 * self.per) + v


class Tallies:

    def __init__(self):
        self.of = {}

    def __getitem__(self, name):
        return self.of.setdefault(name, Tally())

    @contextmanager
    def loop(self, eng, turns, per):
        before = {}
        with eng.Fori(0, turns) as turn:
            for name in per:
                t = self[name]
                before[name] = t.n
                t.turn, t.per = turn, per[name]
            frozen = {k: t.n for k, t in self.of.items() if k not in per}
            yield turn
            for k, t in self.of.items():
                if k in before:
                    assert t.n - before[k] in (0, per[k]), (k, t.n - before[k], per[k])
                else:
                    assert t.n == frozen.get(k, 0), (k, t.n - frozen.get(k, 0), "missing")
        for name in per:
            t = self[name]
            t.turn = None
            t.n = before[name] + per[name] * turns


CONST_IN = 16 * 5
DA_TURN = {
    "w_split": 6, "w_used": 6, "proj_full": 16, "proj_hi": 10, "proj_free0": 8, "proj_free1": 8,
    "tr_full": 38, "tr_hi": 34, "tr_free0": 19, "tr_free1": 19, "sc_full": 56, "sc_free": 56,
    "nb": 16, "expd": 32, "a_ready": 16, "pv_full": 16, "pv_low": 16, "pv_free": 16,
    "y_ready": 4, "y_out0": 2, "y_out1": 2, "dve": 114,
}
RET_TURN = {
    "w_split": 12, "w_used": 12, "proj_full": 30, "proj_hi": 10, "proj_free0": 15, "proj_free1": 15,
    "tr_full": 20, "tr_hi": 12, "tr_free0": 10, "tr_free1": 10, "sk_full": 9, "k_hi": 8,
    "k_ready": 8, "st_full": 8, "st_free": 8, "s_hi": 8, "s_ready": 8, "p_mul": 8, "p_hi": 8,
    "p_ready": 8, "o_full": 8, "o_sq": 8, "o_free": 8, "g_sig": 8, "ry_out0": 4, "ry_out1": 4,
    "g_out0": 4, "g_out1": 4, "dve": 96, "dec": 1,
}
MLP_TURN = {
    "w_split": 8, "w_used": 8, "proj_full": 24, "proj_free0": 12, "proj_free1": 12,
    "f_sq": 8, "f_hi": 8, "f_lo": 8,
}


SIGNALS = {
    "const_in": "a constant is in", "x_a": "meta tokens or a tile of the first four is in",
    "x_b": "a tile of the last four is in", "raw_in0": "a weight tile is in", "raw_in1": "",
    "y_out0": "attention output is stored", "y_out1": "", "ry_out0": "retention output is stored",
    "ry_out1": "", "g_out0": "retention gate is stored", "g_out1": "",
    "y_in0": "a branch's tile (or its gate) is back", "y_in1": "", "h_in": "tokens are in h2",
    "fin_in": "the final gain is in", "out0": "a result tile is stored", "out1": "",
    "w_hi": "Pool rounded a weight tile", "w_split": "Pool split a weight tile",
    "w_used": "PE is done with a weight tile", "down_used": "PE is done with a block's down rows",
    "proj_full": "PE filled a projection bank", "proj_hi": "ScalarE rounded a projection bank",
    "proj_free0": "a projection bank has been read", "proj_free1": "",
    "tr_full": "PE filled a transpose bank", "tr_hi": "ScalarE rounded a transpose bank",
    "tr_free0": "a transpose bank has been read", "tr_free1": "",
    "pads": "VectorE cleared zero columns", "lam": "lambda's exponents are there",
    "lam_e": "and their exponentials", "diag": "diag(1 / rms) of a group of token tiles is there",
    "act": "ScalarE wrote a sum of squares", "dve": "VectorE wrote what it reads next",
    "sc_full": "PE filled a bank of scores", "sc_free": "VectorE read a bank of scores",
    "nb": "minus the rows' maxima are there", "expd": "exponentials and their sum are there",
    "a_ready": "the two maps are combined", "pv_full": "PE summed the values",
    "pv_low": "ScalarE read the low half of that sum", "pv_free": "VectorE read the high half",
    "y_ready": "four query tiles are normalised",
    "dec": "this head's decay is in `dec`", "sk_full": "PE wrote scores and keys by token",
    "k_hi": "ScalarE rounded the decayed keys", "k_ready": "their rest is there too",
    "st_full": "PE wrote a chunk's k^T v", "st_free": "VectorE added it to the state",
    "s_hi": "ScalarE rounded the state", "s_ready": "its rest is there too",
    "p_mul": "VectorE decayed the scores", "p_hi": "ScalarE rounded them",
    "p_ready": "their rest is there too", "o_full": "PE wrote a chunk's output",
    "o_sq": "ScalarE summed its squares", "o_free": "VectorE normalised it",
    "g_sig": "the gate's sigmoid is there",
    "y_mul": "a retention tile is gated", "y_hi": "ScalarE rounded a branch's tile",
    "y_split": "its rest is there too", "gated": "VectorE gated or added half a tile of `acc`",
    "mrg_hi": "ScalarE rounded a quarter of `acc`", "mrg_lo": "its rest is there too",
    "f_sq": "VectorE squared the hidden features", "f_hi": "ScalarE rounded them",
    "f_lo": "their rest is there too", "fin": "a result tile is normalised",
}


def key_pieces(i):
    n = META + P * (i + 1)
    size = -(-n // -(-n // BANK) // META) * META
    return [(k, min(k + size, n)) for k in range(0, n, size)]


SC_PERIOD = 2 * 2 * sum(len(key_pieces(i)) for i in range(TT))


def score_bank(n):
    n %= SC_PERIOD
    return n % 3, (1 if n < 2 else 2)


DA_PEEL = 3


def y_group(s):
    return (s - 2) // 4 - 1


def block_groups(i):
    return [(k, min(k + 4, i + 2)) for k in range(0, i + 2, 4)]


def build(nc, t):
    ctx = ExitStack()
    with ctx:
        ctx.enter_context(nc.sbuf_tensor("map", [P, MAP_SIZE], F32))

        def at(name, offset, shape, dtype=F32):
            size = int(np.prod(shape))
            assert offset + size <= MAP_SIZE, (name, offset + size)
            return nc.alloc_sbuf_tensor_at(name, [P, *shape], dtype, offset=MAP_ORIGIN + 4 * offset)

        class Area:
            def __init__(self, start):
                self.at = start

            def take(self, name, shape, dtype=F32):
                here = self.at
                self.at += (int(np.prod(shape)) + 7) // 8 * 8
                return at(name, here, shape, dtype)

        keep = Area(0)
        ident = keep.take("ident", [P])
        ident_r = keep.take("ident_r", [P], F32R)
        vecs = keep.take("vecs", [2 * KT + 1])
        lamv = keep.take("lamv", [4, DH])
        small = keep.take("small", [96])
        decay = keep.take("decay", [RET_HEADS, P + 3])
        dec = keep.take("dec", [P + 3])
        raw = keep.take("raw", [2, D])
        w_hi = keep.take("w_hi", [2, D], F32R)
        w_lo = keep.take("w_lo", [2, D], F32R)
        u_at = keep.at
        u_hi = keep.take("u_hi", [KT, L], F32R)
        u_lo = keep.take("u_lo", [KT, L], F32R)
        work = keep.at

        ss = small[:, 0:9]
        rs = small[:, 9:18]
        ms = small[:, 18:27]
        nt = small[:, 27:36]
        mx = small[:, 36:42].rearrange("p (c j) -> p c j", c=2)
        mxc = small[:, 42:44]
        nb = small[:, 44:46]
        sums = small[:, 46:50].rearrange("p (b c) -> p b c", b=2)
        rec = small[:, 50:54].rearrange("p (b c) -> p b c", b=2)
        cf = small[:, 54:55]
        lam = small[:, 55:61]
        neglam = small[:, 61:62]
        g_head = small[:, 62:63]
        rsq = small[:, 63:64]

        a = Area(work)
        x_in = a.take("x_in", [TT, D])
        x_meta = a.take("x_meta", [D])
        junk0 = a.take("junk0", [D])
        diag0 = a.take("diag0", [TT, P])
        diag_m = a.take("diag_m", [P])

        a = Area(work)
        q_hi = a.take("q_hi", [2, SEQ], F32R)
        q_lo = a.take("q_lo", [2, SEQ], F32R)
        k_hi = a.take("k_hi", [2, L], F32R)
        k_lo = a.take("k_lo", [2, L], F32R)
        v_da = a.take("v_da", [2, 9, 2, P], F32R)
        at_hi = a.take("at_hi", [9, P], F32R)
        at_lo = a.take("at_lo", [9, P], F32R)
        z = a.take("z", [2, 2, LP])
        bias = a.take("bias", [L])
        vt = a.take("vt", [LP])
        y_low = a.take("y_low", [2, P])
        y_q = a.take("y_q", [2, 4, P])
        y_st = a.take("y_st", [2, BANK])
        junk1 = a.take("junk1", [P])

        a = Area(work)
        rq_hi = a.take("rq_hi", [DKT, SEQ], F32R)
        rq_lo = a.take("rq_lo", [DKT, SEQ], F32R)
        rk_hi = a.take("rk_hi", [DKT, LP], F32R)
        rk_lo = a.take("rk_lo", [DKT, LP], F32R)
        rv_hi = a.take("rv_hi", [9, RDV], F32R)
        rv_lo = a.take("rv_lo", [9, RDV], F32R)
        kt_hi = a.take("kt_hi", [RDK], F32R)
        kt_lo = a.take("kt_lo", [RDK], F32R)
        s_hi = a.take("s_hi", [DKT, RDV], F32R)
        s_lo = a.take("s_lo", [DKT, RDV], F32R)
        p_hi = a.take("p_hi", [P], F32R)
        p_lo = a.take("p_lo", [P], F32R)
        state = a.take("state", [DKT, RDV])
        p_f = a.take("p_f", [P])
        o_n = a.take("o_n", [2, RDV])
        junk3 = a.take("junk3", [RDV])
        rvt = a.take("rvt", [LP])
        ry_st = a.take("ry_st", [2, DVT, P])
        sg = a.take("sg", [BANK])
        g_st = a.take("g_st", [2, BANK])

        a = Area(work)
        y_hi = a.take("y_hi", [KT, SEQ], F32R)
        y_lo = a.take("y_lo", [KT, SEQ], F32R)
        acc = a.take("acc", [KT, SEQ])
        y_in = a.take("y_in", [2, SEQ])
        g_in = a.take("g_in", [2, SEQ])
        gate = at("gate", a.at - 2 * SEQ, [2, BANK])

        h2 = at("h2", u_at, [TT, D])
        wd_hi = at("wd_hi", u_at + 8192, [FF_BLOCK, D], F32R)
        wd_lo = at("wd_lo", u_at + 8192 + 4096, [FF_BLOCK, D], F32R)
        f_at = work + 2 * KT * SEQ
        f_hi = at("f_hi", f_at, [FF_BLOCK, SEQ], F32R)
        f_lo = at("f_lo", f_at + 4096, [FF_BLOCK, SEQ], F32R)
        a = Area(f_at + 8192)
        o_st = a.take("o_st", [2, BANK])
        diag2 = a.take("diag2", [TT, P])
        f_r = a.take("f_r", [2, BANK])
        f_s = a.take("f_s", [2, BANK])
        g_fin = at("g_fin", work, [D])
        out_st = at("out_st", work + D, [2, D])

        psum = ctx.enter_context(nc.psum_tensor("psum", [P, 8, BANK], F32))
        PROJ, TR, SC, PV = 0, 2, 4, 7
        SK, ST, OUT = 4, 5, 7

        S = {name: ctx.enter_context(nc.semaphore(name)) for name in SIGNALS}
        block = ctx.enter_context(nc.Block())

        @block.sync
        def _(sp):
            for i in range(2):
                sp.dma_start(raw[:, i, :], t["w"][i]).then_inc(S[f"raw_in{i}"], 16)
            with sp.Fori(1, T_ALL // 2) as pair:
                for i in range(2):
                    sp.wait_ge(S["w_split"], pair * 2 + i - 1)
                    sp.dma_start(raw[:, i, :], t["w"][pair * 2 + i]).then_inc(S[f"raw_in{i}"], 16)

        @block.gpsimd
        def _(pool):
            def split(slot, landed, n, hi, lo, apart=True):
                pool.wait_ge(S[f"raw_in{slot}"], landed)
                if apart:
                    pool.nop(nofuse=True)
                nc.gpsimd.tensor_copy(hi, raw[:, slot, :]).then_inc(S["w_hi"], 1)
                pool.wait_ge(S["w_hi"], n)
                nc.gpsimd.tensor_tensor(lo, raw[:, slot, :], hi.bitcast(F32), ALU.subtract)\
                    .then_inc(S["w_split"], 1)

            for i in range(2):
                split(i, 16, i + 1, w_hi[:, i, :], w_lo[:, i, :], apart=False)
            with pool.Fori(1, T_RING // 2) as pair:
                for i in range(2):
                    pool.wait_ge(S["w_used"], pair * 2 + i - 1)
                    split(i, pair * 16 + 16, pair * 2 + i + 1, w_hi[:, i, :], w_lo[:, i, :])

            def mlp_block(b):
                for n, (kind, j) in enumerate(MLP_ORDER):
                    if kind == "up":
                        hi, lo = w_hi[:, j % 2, :], w_lo[:, j % 2, :]
                        pool.wait_ge(S["w_used"], b * FF_BLOCK + (T_RING + j - 1))
                    else:
                        hi, lo = wd_hi[:, j, :], wd_lo[:, j, :]
                        if isinstance(b, int):
                            pool.wait_ge(S["w_used"], T_RING - KT // 2)
                        else:
                            pool.wait_ge(S["down_used"], b)
                    split(n % 2, b * 64 + 16 * ((T_RING + n) // 2 + 1), b * 8 + (T_RING + n + 1), hi, lo,
                          apart=not isinstance(b, int))

            mlp_block(0)
            with pool.Fori(1, N_BLOCKS) as b:
                mlp_block(b)

        @block.tensor
        def _(pe):
            seen = Tallies()
            turn = [0, 0, 0]

            def product(out, st_hi, st_lo, mv_hi, mv_lo, first, last):
                nc.tensor.matmul(out, st_hi, mv_hi, start=first, stop=False)
                nc.tensor.matmul(out, st_hi, mv_lo, start=False, stop=False)
                return nc.tensor.matmul(out, st_lo, mv_hi, start=False, stop=last)

            def next_weights():
                pe.wait_ge(S["w_split"], seen["w_split"].next())

            def take_proj():
                b = turn[0] % 2
                turn[0] += 1
                free = seen[f"proj_free{b}"]
                if free.n:
                    pe.wait_ge(S[f"proj_free{b}"], free.value())
                free.next()
                return PROJ + b

            def take_tr():
                b = turn[1] % 2
                turn[1] += 1
                free = seen[f"tr_free{b}"]
                if free.n:
                    pe.wait_ge(S[f"tr_free{b}"], free.value())
                free.next()
                return TR + b

            def project(slot, mv_h, mv_l, part, first_use, between=None):
                c0, c1 = part
                b = take_proj()
                for k in range(KT):
                    if between and k == KT // 2:
                        between()
                    cols = slice(k * P, (k + 1) * P)
                    mm = nc.tensor.matmul(psum[:, b, 0:c1 - c0], w_hi[:, slot, cols], mv_h[:, k, c0:c1],
                                          start=k == 0, stop=False)
                    if first_use and k == 0:
                        mm.then_inc(S[first_use], 1)
                    nc.tensor.matmul(psum[:, b, 0:c1 - c0], w_hi[:, slot, cols], mv_l[:, k, c0:c1],
                                     start=False, stop=False)
                    mm = nc.tensor.matmul(psum[:, b, 0:c1 - c0], w_lo[:, slot, cols], mv_h[:, k, c0:c1],
                                          start=False, stop=k == KT - 1)
                mm.then_inc(S["proj_full"], 1)

            def all_free(name):
                for b in range(2):
                    pe.wait_ge(S[f"{name}{b}"], seen[f"{name}{b}"].value())

            pe.wait_ge(S["const_in"], CONST_IN)
            for part in range(2):
                pe.wait_ge(S["diag"], part + 1)
                for m in range(KT):
                    b = take_tr()
                    for j in range(4):
                        mm = nc.tensor.matmul(psum[:, b, j * P:(j + 1) * P],
                                              x_in[:, 4 * part + j, m * P:(m + 1) * P],
                                              diag0[:, 4 * part + j, :], start=True, stop=True)
                    mm.then_inc(S["tr_full"], 1)
                if part == 0:
                    b = take_tr()
                    for m in range(KT):
                        mm = nc.tensor.matmul(psum[:, b, m * META:(m + 1) * META],
                                              x_meta[0:META, m * P:(m + 1) * P],
                                              diag_m[0:META, 0:META], start=True, stop=True)
                    mm.then_inc(S["tr_full"], 1)
            all_free("tr_free")
            pe.wait_ge(S["pads"], 2)

            tile = [0]

            def da_group(g, between=None):
                if g in (0, 3, 6):
                    next_weights()
                    tile[0] += 1
                first = "w_used" if g in (0, 3, 6) and tile[0] > 1 else None
                part = KV_PARTS[g % 3] if g < 6 else Q_PARTS[g - 6]
                project((tile[0] - 1) % 2, u_hi, u_lo, part, first, between)

            def da_values(part):
                last = (turn[0] - 2) % 2
                pe.wait_ge(S[f"proj_free{last}"], seen[f"proj_free{last}"].value())
                b = take_tr()
                for j, tok in enumerate(range(*KV_TILES[part])):
                    mm = nc.tensor.transpose(psum[:, b, j * P:(j + 1) * P],
                                             vt[:, tok * P:(tok + 1) * P], ident[:, :])
                mm.then_inc(S["tr_full"], 1)

            def da_scores(s):
                i, p = s % TT, (s // TT) % 2
                if i == 0:
                    pe.wait_ge(S["proj_free0"], seen["proj_free0"].value())
                for c in range(2):
                    rows = slice(c * DH, (c + 1) * DH)
                    q = slice(i * P, (i + 1) * P)
                    for k0, k1 in key_pieces(i):
                        bank, back = score_bank(turn[2])
                        turn[2] += 1
                        free = seen["sc_free"]
                        if free.n > back:
                            pe.wait_ge(S["sc_free"], free.value(back))
                        free.next()
                        product(psum[:, SC + bank, 0:k1 - k0], q_hi[rows, p, q], q_lo[rows, p, q],
                                k_hi[rows, p, k0:k1], k_lo[rows, p, k0:k1], True, True)\
                            .then_inc(S["sc_full"], 1)

            def da_turn_probs(s, g0, g1):
                b = take_tr()
                for j in range(g0, g1):
                    mm = nc.tensor.transpose(psum[:, b, (j - g0) * P:(j - g0 + 1) * P],
                                             z[:, s % 2, 0, j * P:(j + 1) * P], ident[:, :])
                mm.then_inc(S["tr_full"], 1)

            def da_turn_y(par):
                pe.wait_ge(S["y_ready"], seen["y_ready"].next())
                b = take_tr()
                for j in range(4):
                    mm = nc.tensor.transpose(psum[:, b, j * P:(j + 1) * P], y_q[:, par, j, :],
                                             ident[:, :])
                mm.then_inc(S["tr_full"], 1)

            def da_values_sum(s):
                p, i = (s // TT) % 2, s % TT
                all_free("tr_free")
                free = seen["pv_free"]
                if free.n:
                    pe.wait_ge(S["pv_free"], free.value())
                free.next()
                for j in range(i + 2):
                    nc.tensor.matmul(psum[:, PV, 0:2 * P], at_hi[:, j, :], v_da[:, p, j, :, :],
                                     start=j == 0, stop=False)
                    mm = nc.tensor.matmul(psum[:, PV, 0:P], at_lo[:, j, :], v_da[:, p, j, 0, :],
                                          start=False, stop=j == i + 1)
                mm.then_inc(S["pv_full"], 1)

            def da_step(s, more=True):
                i = s % TT
                da_scores(s)
                blocks = block_groups((s - 1) % TT) if s else []
                if s:
                    pe.wait_ge(S["a_ready"], seen["a_ready"].next())
                for g0, g1 in blocks[:2]:
                    da_turn_probs(s - 1, g0, g1)

                def middle():
                    for g0, g1 in blocks[2:]:
                        da_turn_probs(s - 1, g0, g1)
                    if i in (2, 6) and s > 4:
                        da_turn_y(y_group(s) % 2)
                    if more and i in (1, 2, 3):
                        da_values(i - 1)

                if more:
                    da_group(i, middle)
                else:
                    middle()
                if s:
                    da_values_sum(s - 1)

            for g in range(8):
                da_group(g)
                if g in (1, 2, 3):
                    da_values(g - 1)
            for s in range(DA_PEEL):
                da_step(s)
            with seen.loop(pe, 3, DA_TURN):
                for s in range(DA_PEEL, DA_PEEL + 2 * TT):
                    da_step(s)
            for s in range(DA_PEEL + 6 * TT, 8 * TT):
                da_step(s, more=s < 7 * TT)
            pe.wait_ge(S["a_ready"], seen["a_ready"].next())
            for n, (g0, g1) in enumerate(block_groups(TT - 1)):
                da_turn_probs(8 * TT - 1, g0, g1)
            da_values_sum(8 * TT - 1)
            da_turn_y(y_group(8 * TT + 2) % 2)

            def ret_values(m, part):
                last = (turn[0] - 2) % 2
                pe.wait_ge(S[f"proj_free{last}"], seen[f"proj_free{last}"].value())
                b = take_tr()
                for j, tok in enumerate(range(*KV_TILES[part])):
                    mm = nc.tensor.transpose(psum[:, b, j * P:(j + 1) * P],
                                             rvt[:, tok * P:(tok + 1) * P], ident[:, :])
                mm.then_inc(S["tr_full"], 1)

            def ret_turn_y(c):
                pe.wait_ge(S["o_free"], seen["o_free"].value())
                b = take_tr()
                for j in range(DVT):
                    mm = nc.tensor.transpose(psum[:, b, j * P:(j + 1) * P],
                                             o_n[:, c % 2, j * P:(j + 1) * P], ident[:, :])
                mm.then_inc(S["tr_full"], 1)

            def ret_scores(c):
                cols = slice((c + 1) * P, (c + 2) * P)
                if seen["k_ready"].n:
                    pe.wait_ge(S["k_ready"], seen["k_ready"].value())
                if c >= 0:
                    q = slice(c * P, (c + 1) * P)
                    for d in range(DKT):
                        mm = product(psum[:, SK, 0:P], rk_hi[:, d, cols], rk_lo[:, d, cols],
                                     rq_hi[:, d, q], rq_lo[:, d, q], d == 0, d == DKT - 1)
                if c < TT - 1:
                    for d in range(DKT):
                        out = psum[:, SK, (d + 1) * P:(d + 2) * P]
                        nc.tensor.matmul(out, rk_hi[:, d, cols], ident_r[:, :], start=True, stop=False)
                        mm = nc.tensor.matmul(out, rk_lo[:, d, cols], ident_r[:, :], start=False, stop=True)
                mm.then_inc(S["sk_full"], 1)

            def ret_state(c):
                pe.wait_ge(S["k_ready"], seen["k_ready"].next())
                if seen["st_free"].n:
                    pe.wait_ge(S["st_free"], seen["st_free"].value())
                seen["st_free"].next()
                for d in range(DKT):
                    cols = slice(d * P, (d + 1) * P)
                    mm = product(psum[:, ST + d, :], kt_hi[:, cols], kt_lo[:, cols],
                                 rv_hi[:, c + 1, :], rv_lo[:, c + 1, :], True, True)
                mm.then_inc(S["st_full"], 1)

            def ret_out(c):
                q = slice(c * P, (c + 1) * P)
                if seen["o_free"].n:
                    pe.wait_ge(S["o_free"], seen["o_free"].value())
                seen["o_free"].next()
                pe.wait_ge(S["s_ready"], seen["s_ready"].next())
                for d in range(DKT):
                    product(psum[:, OUT, :], rq_hi[:, d, q], rq_lo[:, d, q], s_hi[:, d, :],
                            s_lo[:, d, :], d == 0, False)
                pe.wait_ge(S["p_ready"], seen["p_ready"].next())
                product(psum[:, OUT, :], p_hi[:, :], p_lo[:, :], rv_hi[:, c + 1, :],
                        rv_lo[:, c + 1, :], False, True).then_inc(S["o_full"], 1)

            pe.wait_ge(S["pads"], 3)
            with seen.loop(pe, RET_HEADS, RET_TURN):
                late = []
                for m in range(DVT):
                    next_weights()
                    for part in range(3):
                        project(m % 2, u_hi, u_lo, KV_PARTS[part], "w_used" if part == 0 else None)
                        for m1, p1 in late:
                            ret_values(m1, p1)
                        late = [(m, part)]
                for d in range(DKT):
                    next_weights()
                    for part in range(3):
                        project(d % 2, u_hi, u_lo, KV_PARTS[part], "w_used" if part == 0 else None)
                        for m1, p1 in late:
                            ret_values(m1, p1)
                        late = []
                for d in range(DKT):
                    next_weights()
                    for part in range(2):
                        project(d % 2, u_hi, u_lo, Q_PARTS[part], "w_used" if part == 0 else None)
                all_free("proj_free")
                all_free("tr_free")
                ret_scores(-1)
                ret_state(-1)
                for c in range(TT):
                    ret_scores(c)
                    if c % 2 == 0:
                        next_weights()

                    def middle(c=c):
                        ret_out(c)
                        if c < TT - 1:
                            ret_state(c)

                    project((c // 2) % 2, u_hi, u_lo, Q_PARTS[c % 2], None if c % 2 else "w_used", middle)
                    if c:
                        ret_turn_y(c - 1)
                ret_turn_y(TT - 1)

            def operand_ready(n):
                pe.wait_ge(S["y_split"], seen["y_split"].next(n))

            for hr in range(RET_HEADS):
                operand_ready(DVT)
                k0 = DVT * (hr % 2)
                for mp in range(4):
                    next_weights()
                    slot = mp % 2
                    for m2 in range(2):
                        for half in range(2):
                            b = take_proj()
                            tok = slice(half * HALF, (half + 1) * HALF)
                            for k in range(DVT):
                                cols = slice((m2 * DVT + k) * P, (m2 * DVT + k + 1) * P)
                                mm = nc.tensor.matmul(psum[:, b, :], w_hi[:, slot, cols],
                                                      y_hi[:, k0 + k, tok], start=k == 0, stop=False)
                                if (m2, half, k) == (0, 0, 0):
                                    mm.then_inc(S["w_used"], 1)
                                nc.tensor.matmul(psum[:, b, :], w_hi[:, slot, cols],
                                                 y_lo[:, k0 + k, tok], start=False, stop=False)
                                mm = nc.tensor.matmul(psum[:, b, :], w_lo[:, slot, cols],
                                                      y_hi[:, k0 + k, tok], start=False,
                                                      stop=k == DVT - 1)
                            mm.then_inc(S["proj_full"], 1)

            HALVES = [(0, HALF), (HALF, SEQ)]
            with seen.loop(pe, KT // 2, {"w_split": 2, "w_used": 2, "proj_free0": 2, "proj_free1": 2}):
                for m in range(2):
                    next_weights()
                    for half in range(2):
                        project(m, u_hi, u_lo, Q_PARTS[half], None if half else "w_used")
            operand_ready(KT)
            with seen.loop(pe, KT, {"w_split": 2, "w_used": 2, "proj_free0": 2, "proj_free1": 2}):
                next_weights()
                for half in range(2):
                    project(0, u_hi, u_lo, Q_PARTS[half], None if half else "w_used")
                next_weights()
                for half in range(2):
                    project(1, y_hi, y_lo, HALVES[half], None if half else "w_used")

            def turn_o(g):
                last = (turn[0] - 1 - g) % 2
                b = take_tr()
                for j in range(4):
                    mm = nc.tensor.transpose(psum[:, b, j * P:(j + 1) * P],
                                             o_st[:, last, j * P:(j + 1) * P], ident[:, :])
                mm.then_inc(S["tr_full"], 1)

            def out_group(m, half, late=True):
                project(m % 2, y_hi, y_lo, HALVES[half], None if half else "w_used")
                if late:
                    b = turn[0] % 2
                    pe.wait_ge(S[f"proj_free{b}"], seen[f"proj_free{b}"].value())
                    turn_o(1)

            next_weights()
            pe.wait_ge(S["mrg_lo"], 2)
            out_group(0, 0, late=False)
            pe.wait_ge(S["mrg_lo"], 4)
            out_group(0, 1)
            for m in range(1, KT):
                next_weights()
                for half in range(2):
                    out_group(m, half)
            all_free("proj_free")
            turn_o(0)

            all_free("tr_free")
            pe.wait_ge(S["diag"], 3)
            for half in range(2):
                for m in range(KT):
                    b = take_tr()
                    for j in range(4):
                        mm = nc.tensor.matmul(psum[:, b, j * P:(j + 1) * P],
                                              h2[:, 4 * half + j, m * P:(m + 1) * P],
                                              diag2[:, 4 * half + j, :], start=True, stop=True)
                    mm.then_inc(S["tr_full"], 1)
            all_free("tr_free")

            def mlp(first):
                for j in range(FF_BLOCK):
                    pe.wait_ge(S["w_split"], seen["w_split"].next((1, 1, 3, 2)[j]))
                    before = "w_used" if first or j else "down_used"
                    for half in range(2):
                        project(j % 2, y_hi, y_lo, HALVES[half], None if half else before)
                def down(b, tok, half, ks):
                    out = slice(half * BANK, (half + 1) * BANK)
                    st = slice(tok * P, (tok + 1) * P)
                    for k in ks:
                        mm = nc.tensor.matmul(psum[:, b, :], f_hi[:, k, st], wd_hi[:, k, out],
                                              start=k == 0, stop=False)
                        if (tok, half, k) == (0, 0, 0):
                            mm.then_inc(S["w_used"], 1)
                        nc.tensor.matmul(psum[:, b, :], f_hi[:, k, st], wd_lo[:, k, out],
                                         start=False, stop=False)
                        mm = nc.tensor.matmul(psum[:, b, :], f_lo[:, k, st], wd_hi[:, k, out],
                                              start=False, stop=k == FF_BLOCK - 1)
                    return mm

                pe.wait_ge(S["w_split"], seen["w_split"].next())
                pe.wait_ge(S["f_lo"], seen["f_lo"].next(2 * (FF_BLOCK - 1)))
                banks = []
                for half in range(2):
                    banks.append(take_proj())
                    down(banks[half], 0, half, range(FF_BLOCK - 1))
                pe.wait_ge(S["f_lo"], seen["f_lo"].next(2))
                for half in range(2):
                    down(banks[half], 0, half, [FF_BLOCK - 1]).then_inc(S["proj_full"], 1)
                for tok in range(1, TT):
                    for half in range(2):
                        down(take_proj(), tok, half, range(FF_BLOCK)).then_inc(S["proj_full"], 1)

            mlp(True)
            with seen.loop(pe, N_BLOCKS - 2, MLP_TURN):
                mlp(False)
            mlp(False)

        @block.scalar
        def _(act):
            seen = Tallies()
            turn = [0, 0]

            def wait(name, k=1):
                act.wait_ge(S[name], seen[name].next(k))

            def bank_proj():
                b = turn[0] % 2
                turn[0] += 1
                seen["proj_full"].next()
                seen[f"proj_free{b}"].next()
                return PROJ + b

            def bank_tr():
                b = turn[1] % 2
                turn[1] += 1
                seen["tr_full"].next()
                seen[f"tr_free{b}"].next()
                return TR + b

            def filled(name):
                act.wait_ge(S[name], seen[name].value())

            def free(b):
                return S[f"proj_free{b}" if b < TR else f"tr_free{b - TR}"]

            def step(ins):
                ins.then_inc(S["act"], 1)
                seen["act"].next()

            def settle():
                act.wait_ge(S["act"], seen["act"].value())

            for name in ("y_out0", "y_out1", "ry_out0", "ry_out1", "g_out0", "g_out1"):
                act.sem_inc(S[name], 16)
                seen[name].n = 1
            for dst, src in ((ident[:, :], t["ident"]), (bias[:, :], t["dist"]), (vecs[:, :], t["vecs"]),
                             (lamv[:, :, :], t["lamv"]), (decay[:, :, :], t["decay"])):
                act.dma_start(dst, src).then_inc(S["const_in"], 16)
            act.dma_start(x_meta[0:META, :], t["meta"]).then_inc(S["x_a"], 16)
            for j in range(TT):
                act.dma_start(x_in[:, j, :], t["x"][j * P:(j + 1) * P, :])\
                    .then_inc(S["x_a" if j < 4 else "x_b"], 16)

            act.wait_ge(S["pads"], 1)
            act.wait_ge(S["const_in"], CONST_IN)
            act.wait_ge(S["x_a"], 5 * 16)
            step(nc.scalar.activation(junk0[0:META, :], x_meta[0:META, :], ACT.Square,
                                      accum_out=ss[0:META, 0:1]))
            for part in range(2):
                if part:
                    act.wait_ge(S["x_b"], 4 * 16)
                for j in range(4 * part, 4 * part + 4):
                    settle()
                    step(nc.scalar.activation(junk0[:, :], x_in[:, j, :], ACT.Square,
                                              accum_out=ss[:, j + 1:j + 2]))
            act.wait_ge(S["lam"], 1)
            nc.scalar.activation(lam[:, 2:4], lam[:, 0:2], ACT.Exp).then_inc(S["lam_e"], 1)

            def norm_turned(g0, dst, c0, groups):
                for m in groups:
                    b = bank_tr()
                    filled("tr_full")
                    nc.scalar.activation(dst[:, m, c0:c0 + BANK], psum[:, b, :], ACT.Copy,
                                         scale=vecs[:, g0 + m:g0 + m + 1]).then_inc(S["tr_hi"], 1)

            norm_turned(0, u_hi, META, range(KT))
            b = bank_tr()
            filled("tr_full")
            for m in range(KT):
                last = nc.scalar.activation(u_hi[:, m, 0:META], psum[:, b, m * META:(m + 1) * META],
                                            ACT.Copy, scale=vecs[:, m:m + 1])
            last.then_inc(S["tr_hi"], 1)
            norm_turned(0, u_hi, META + BANK, range(KT))

            def da_group(g, p):
                b = bank_proj()
                filled("proj_full")
                if g < 3:
                    c0, c1 = KV_PARTS[g]
                    nc.scalar.activation(vt[:, PAD + c0:PAD + c1], psum[:, b, 0:c1 - c0], ACT.Copy)\
                        .then_inc(free(b), 1)
                else:
                    c0, c1 = KV_PARTS[g - 3] if g < 6 else ((g - 6) * HALF, (g - 5) * HALF)
                    dst = k_hi if g < 6 else q_hi
                    nc.scalar.activation(dst[:, p, c0:c1], psum[:, b, 0:c1 - c0], ACT.Copy)\
                        .then_inc(S["proj_hi"], 1)

            def da_values(part, p):
                b = bank_tr()
                filled("tr_full")
                t0, t1 = KV_TILES[part]
                nc.scalar.activation(v_da[:, p, t0:t1, 0, :],
                                     psum[:, b, 0:(t1 - t0) * P].rearrange("p (t n) -> p t n", n=P),
                                     ACT.Copy).then_inc(S["tr_hi"], 1)

            def da_turned(g0, g1):
                b = bank_tr()
                filled("tr_full")
                nc.scalar.activation(at_hi[:, g0:g1, :],
                                     psum[:, b, 0:(g1 - g0) * P].rearrange("p (t n) -> p t n", n=P),
                                     ACT.Copy).then_inc(S["tr_hi"], 1)

            stores = [0]

            def da_y(head, half):
                b = bank_tr()
                filled("tr_full")
                slot = stores[0] % 2
                stores[0] += 1
                out = seen[f"y_out{slot}"]
                act.wait_ge(S[f"y_out{slot}"], out.value16())
                sem_b = free(b)
                nc.scalar.activation(y_st[:, slot, :], psum[:, b, :], ACT.Copy, scale=g_head)\
                    .then_inc(sem_b, 1)
                act.wait_ge(sem_b, seen[f"tr_free{b - TR}"].value())
                out.next()
                act.dma_start(t["yd"][head, :, half * HALF:(half + 1) * HALF], y_st[:, slot, :])\
                    .then_inc(S[f"y_out{slot}"], 16)

            def da_exp(s):
                wait("nb")
                nk = META + P * (s % TT + 1)
                for c in range(2):
                    zc = z[:, s % 2, c, PAD:PAD + nk]
                    nc.scalar.activation(zc, zc, ACT.Exp, bias=nb[:, c:c + 1], scale=DA_SCALE,
                                         accum_out=sums[:, s % 2, c:c + 1]).then_inc(S["expd"], 1)

            def da_low(s):
                wait("pv_full")
                nc.scalar.activation(y_low[:, s % 2, :], psum[:, PV, P:2 * P], ACT.Copy,
                                     scale=rec[:, s % 2, 0:1]).then_inc(S["pv_low"], 1)

            def da_step(s, head, more=True):
                i = s % TT
                blocks = block_groups((s - 1) % TT) if s else []
                for g0, g1 in blocks[:2]:
                    da_turned(g0, g1)
                if s > 1:
                    da_low(s - 2)
                da_exp(s)
                for g0, g1 in blocks[2:]:
                    da_turned(g0, g1)
                if i in (2, 6) and s > 4:
                    da_y(head - (1 if i == 2 else 0), 1 if i == 2 else 0)
                if more and i in (1, 2, 3):
                    da_values(i - 1, (s // TT + 1) % 2)
                if more:
                    da_group(i, (s // TT + 1) % 2)

            for g in range(8):
                da_group(g, 0)
                if g in (1, 2, 3):
                    da_values(g - 1, 0)
            for s in range(DA_PEEL):
                da_step(s, 0)
            with seen.loop(act, 3, DA_TURN) as pair:
                for s in range(DA_PEEL, DA_PEEL + 2 * TT):
                    da_step(s, pair * 2 + s // TT)
            for s in range(DA_PEEL + 6 * TT, 8 * TT):
                da_step(s, s // TT, more=s < 7 * TT)
            for g0, g1 in block_groups(TT - 1):
                da_turned(g0, g1)
            da_low(8 * TT - 2)
            da_low(8 * TT - 1)
            da_y(7, 1)
            for slot in range(2):
                act.wait_ge(S[f"y_out{slot}"], seen[f"y_out{slot}"].value16())

            def ret_values(m, part):
                b = bank_tr()
                filled("tr_full")
                t0, t1 = KV_TILES[part]
                nc.scalar.activation(rv_hi[:, t0:t1, m * P:(m + 1) * P],
                                     psum[:, b, 0:(t1 - t0) * P].rearrange("p (t n) -> p t n", n=P),
                                     ACT.Copy).then_inc(S["tr_hi"], 1)

            def ret_hi(dst):
                b = bank_proj()
                filled("proj_full")
                nc.scalar.activation(dst, psum[:, b, 0:dst.shape[-1]], ACT.Copy)\
                    .then_inc(S["proj_hi"], 1)

            def ret_keys(head):
                nc.scalar.activation(kt_hi[:, :], psum[:, SK, P:P + RDK], ACT.Copy,
                                     scale=dec[:, P + 1:P + 2]).then_inc(S["k_hi"], 1)

            def ret_state():
                wait("st_free")
                nc.scalar.activation(s_hi[:, :, :], state[:, :, :], ACT.Copy).then_inc(S["s_hi"], 1)

            def ret_y(head, c):
                b = bank_tr()
                filled("tr_full")
                slot = c % 2
                out = seen[f"ry_out{slot}"]
                act.wait_ge(S[f"ry_out{slot}"], out.value16())
                sem_b = free(b)
                nc.scalar.activation(ry_st[:, slot, :, :],
                                     psum[:, b, :].rearrange("p (t n) -> p t n", n=P), ACT.Copy)\
                    .then_inc(sem_b, 1)
                act.wait_ge(sem_b, seen[f"tr_free{b - TR}"].value())
                out.next()
                act.dma_start(t["yr"][head, :, :, c * P:(c + 1) * P], ry_st[:, slot, :, :])\
                    .then_inc(S[f"ry_out{slot}"], 16)

            with seen.loop(act, RET_HEADS, RET_TURN) as head:
                late = []
                for m in range(DVT):
                    for part in range(3):
                        b = bank_proj()
                        filled("proj_full")
                        c0, c1 = KV_PARTS[part]
                        nc.scalar.activation(rvt[:, PAD + c0:PAD + c1], psum[:, b, 0:c1 - c0], ACT.Copy)\
                            .then_inc(free(b), 1)
                        for m1, p1 in late:
                            ret_values(m1, p1)
                        late = [(m, part)]
                for d in range(DKT):
                    for part in range(3):
                        c0, c1 = KV_PARTS[part]
                        ret_hi(rk_hi[:, d, PAD + c0:PAD + c1])
                        for m1, p1 in late:
                            ret_values(m1, p1)
                        late = []
                for d in range(DKT):
                    for part in range(2):
                        ret_hi(rq_hi[:, d, part * HALF:(part + 1) * HALF])
                wait("dec")
                wait("sk_full")
                ret_keys(head)
                ret_state()
                for c in range(TT):
                    wait("p_mul")
                    seen["sk_full"].next()
                    nc.scalar.activation(p_hi[:, :], p_f[:, :], ACT.Copy).then_inc(S["p_hi"], 1)
                    if c < TT - 1:
                        ret_keys(head)
                    wait("o_full")
                    nc.scalar.activation(junk3[:, :], psum[:, OUT, :], ACT.Square,
                                         scale=dec[:, P:P + 1],
                                         accum_out=ss[:, c % 2:c % 2 + 1]).then_inc(S["o_sq"], 1)
                    if c < TT - 1:
                        ret_state()
                    b = bank_proj()
                    filled("proj_full")
                    nc.scalar.activation(sg[:, :], psum[:, b, :], ACT.Sigmoid).then_inc(S["g_sig"], 1)
                    act.wait_ge(free(b), seen[f"proj_free{b}"].value())
                    m, half = c // 2, c % 2
                    act.dma_start(t["gr"][head, :, m, half * HALF:(half + 1) * HALF], g_st[:, c % 2, :])\
                        .then_inc(S[f"g_out{c % 2}"], 16)
                    seen[f"g_out{c % 2}"].next()
                    if c:
                        ret_y(head, c - 1)
                ret_y(head, TT - 1)
            for slot in range(2):
                act.wait_ge(S[f"ry_out{slot}"], seen[f"ry_out{slot}"].value16())
                act.wait_ge(S[f"g_out{slot}"], seen[f"g_out{slot}"].value16())

            tiles = [0]

            def load(n):
                slot = n % 2
                if n >= 2:
                    act.wait_ge(S["y_split"], n - 1)
                act.dma_start(y_in[:, slot, :], t["yr"][n // 4, :, n % 4, :]).then_inc(S[f"y_in{slot}"], 16)
                act.dma_start(g_in[:, slot, :], t["gr"][n // 4, :, n % 4, :]).then_inc(S[f"y_in{slot}"], 16)

            def load_da(n):
                k = n - 16
                act.wait_ge(S["y_split"], n - 1)
                act.dma_start(y_in[:, n % 2, :], t["yd"][k]).then_inc(S[f"y_in{n % 2}"], 16)

            base_proj = seen["proj_full"].n

            def split_ret(n):
                if n + 1 < 16:
                    load(n + 1)
                wait("y_mul")
                if n >= 8:
                    act.wait_ge(S["proj_full"], base_proj + 16 * (n // 4 - 1))
                nc.scalar.activation(y_hi[:, n % 8, :], y_in[:, n % 2, :], ACT.Copy)\
                    .then_inc(S["y_hi"], 1)

            load(0)
            for n in range(4):
                split_ret(n)
            for hr in range(RET_HEADS):
                for n in range(4 * hr + 4, min(4 * hr + 8, 16)):
                    split_ret(n)
            for _ in range(16 * RET_HEADS):
                bank_proj()

            def gate_half(half):
                b = bank_proj()
                filled("proj_full")
                if seen["gated"].n > 1:
                    act.wait_ge(S["gated"], seen["gated"].value(1))
                seen["gated"].next()
                nc.scalar.activation(gate[:, half, :], psum[:, b, :], ACT.Sigmoid).then_inc(free(b), 1)

            act.wait_ge(S["proj_full"], seen["proj_full"].value())
            load_da(16)
            for m in range(KT):
                for half in range(2):
                    gate_half(half)
                n = 16 + m
                if m < KT - 1:
                    load_da(n + 1)
                act.wait_ge(S[f"y_in{n % 2}"], 16 * 2 * 8 + 16 * (m // 2 + 1))
                nc.scalar.activation(y_hi[:, m, :], y_in[:, n % 2, :], ACT.Copy).then_inc(S["y_hi"], 1)
            for m in range(KT):
                for half in range(2):
                    gate_half(half)
                if m == KT - 1:
                    act.dma_start(h2[:, :, :], t["x"].rearrange("(t p) d -> p t d", p=P))\
                        .then_inc(S["h_in"], 16)
                for half in range(2):
                    bank_proj()
            act.wait_ge(S["proj_full"], seen["proj_full"].value())
            act.wait_ge(S["gated"], 4 * KT)
            for q in range(4):
                tok = slice(q * 256, (q + 1) * 256)
                nc.scalar.activation(y_hi[:, :, tok], acc[:, :, tok], ACT.Copy).then_inc(S["mrg_hi"], 1)

            for g in range(2 * KT):
                b = bank_proj()
                filled("proj_full")
                nc.scalar.activation(o_st[:, b, :], psum[:, b, :], ACT.Copy).then_inc(free(b), 1)
            for g in range(2 * KT):
                b = bank_tr()
            for b in range(2):
                act.wait_ge(S[f"tr_free{b}"], seen[f"tr_free{b}"].value())
            for j in range(TT):
                if j:
                    settle()
                step(nc.scalar.activation(f_r[:, :, :], h2[:, j, :].rearrange("p (a n) -> p a n", a=2), ACT.Square,
                                          accum_out=ss[:, j:j + 1]))
            for half in range(2):
                norm_turned(KT, y_hi, half * HALF, range(KT))

            def mlp():
                for g in range(2 * FF_BLOCK):
                    b = bank_proj()
                    filled("proj_full")
                    nc.scalar.activation(f_r[:, b, :], psum[:, b, :], ACT.Relu).then_inc(free(b), 1)
                    wait("f_sq")
                    nc.scalar.activation(f_hi[:, g // 2, (g % 2) * HALF:(g % 2 + 1) * HALF],
                                         f_s[:, b, :], ACT.Copy).then_inc(S["f_hi"], 1)
                for _ in range(2 * TT):
                    bank_proj()

            mlp()
            with seen.loop(act, N_BLOCKS - 2, MLP_TURN):
                mlp()
            mlp()

            act.wait_ge(S["proj_full"], seen["proj_full"].value(2 * TT - 1))
            act.dma_start(g_fin[:, :], t["g_fin"]).then_inc(S["fin_in"], 16)

            def store_out(j):
                act.wait_ge(S["fin"], j + 1)
                act.dma_start(t["out"][0, j * P:(j + 1) * P, :], out_st[:, j % 2, :])\
                    .then_inc(S[f"out{j % 2}"], 16)

            for j in range(TT):
                for b in range(2):
                    act.wait_ge(S[f"proj_free{b}"], seen[f"proj_free{b}"].value(TT - 1 - j))
                if j:
                    settle()
                step(nc.scalar.activation(f_r[:, :, :], h2[:, j, :].rearrange("p (a n) -> p a n", a=2),
                                          ACT.Square, accum_out=ss[:, j:j + 1]))
                if j:
                    store_out(j - 1)
            store_out(TT - 1)
            for slot in range(2):
                act.wait_ge(S[f"out{slot}"], 16 * TT // 2)

        @block.vector
        def _(dve):
            seen = Tallies()
            turn = [0, 0, 0]
            for slot in range(2):
                seen[f"g_out{slot}"].n = 1

            def wait(name, k=1):
                dve.wait_ge(S[name], seen[name].next(k))

            def bank_proj():
                b = turn[0] % 2
                turn[0] += 1
                seen["proj_full"].next()
                seen[f"proj_free{b}"].next()
                return PROJ + b

            def bank_tr():
                b = turn[1] % 2
                turn[1] += 1
                seen["tr_full"].next()
                seen[f"tr_free{b}"].next()
                return TR + b

            def filled(name):
                dve.wait_ge(S[name], seen[name].value())

            def free(b):
                return S[f"proj_free{b}" if b < TR else f"tr_free{b - TR}"]

            def link(ins):
                ins.then_inc(S["dve"], 1)
                dve.wait_ge(S["dve"], seen["dve"].next())

            def rsqrt(c0, c1, n):
                x, y, w = ms[:, c0:c1], rs[:, c0:c1], nt[:, c0:c1]
                link(nc.vector.tensor_scalar(x, ss[:, c0:c1], 1.0 / n, EPS, ALU.mult, ALU.add))
                link(nc.vector.tensor_scalar(w.bitcast(I32), x.bitcast(I32), 1, None,
                                             ALU.logical_shift_right))
                link(nc.vector.tensor_scalar(y.bitcast(I32), w.bitcast(I32), -1.0, float(0x5F3759DF),
                                             ALU.mult, ALU.add))
                for _ in range(3):
                    link(nc.vector.tensor_tensor(w, y, y, ALU.mult))
                    link(nc.vector.scalar_tensor_tensor(w, w, -0.5, x, ALU.mult, ALU.mult))
                    link(nc.vector.scalar_tensor_tensor(y, w, 1.5, y, ALU.add, ALU.mult))

            def low(dst, b, hi, n):
                src = psum[:, b, 0:n]
                if len(dst.shape) == 3:
                    src = src.rearrange("p (t n) -> p t n", n=P)
                return nc.vector.tensor_tensor(dst, src, hi.bitcast(F32), ALU.subtract)

            nc.vector.memset(small[:, :], 0.0).then_inc(S["pads"], 1)
            dve.wait_ge(S["pads"], 1)
            dve.wait_ge(S["const_in"], CONST_IN)
            nc.vector.tensor_copy(ident_r[:, :], ident[:, :])
            for j in range(2):
                last = nc.vector.tensor_tensor_reduce(lamv[:, 2 * j, :], lamv[:, 2 * j, :], lamv[:, 2 * j + 1, :],
                                                      1.0, 0.0, ALU.mult, ALU.add, lam[:, j:j + 1])
            last.then_inc(S["lam"], 1)
            dve.wait_ge(S["lam_e"], 1)
            link(nc.vector.tensor_tensor(lam[:, 4:5], lam[:, 3:4], lam[:, 2:3], ALU.subtract))
            nc.vector.tensor_scalar(neglam, lam[:, 4:5], -LAM_INIT, None, ALU.add)
            link(nc.vector.tensor_scalar(g_head, vecs[:, 2 * KT:2 * KT + 1], 1.0 - LAM_INIT, None, ALU.mult))
            for part in range(2):
                dve.wait_ge(S["act"], 5 + 4 * part)
                c0, c1 = (0, 5) if part == 0 else (5, 9)
                rsqrt(c0, c1, D)
                if part == 0:
                    nc.vector.tensor_scalar(diag_m[:, :], ident[:, :], rs[:, 0:1], None, ALU.mult)
                for j in range(4 * part, 4 * part + 4):
                    last = nc.vector.tensor_scalar(diag0[:, j, :], ident[:, :], rs[:, j + 1:j + 2], None,
                                                   ALU.mult)
                last.then_inc(S["diag"], 1)

            def norm_turned(g0, hi, lo, c0):
                for m in range(KT):
                    b = bank_tr()
                    wait("tr_hi")
                    nc.vector.scalar_tensor_tensor(lo[:, m, c0:c0 + BANK], psum[:, b, :],
                                                   vecs[:, g0 + m:g0 + m + 1],
                                                   hi[:, m, c0:c0 + BANK].bitcast(F32),
                                                   ALU.mult, ALU.subtract).then_inc(free(b), 1)

            norm_turned(0, u_hi, u_lo, META)
            b = bank_tr()
            wait("tr_hi")
            for m in range(KT):
                last = nc.vector.scalar_tensor_tensor(u_lo[:, m, 0:META], psum[:, b, m * META:(m + 1) * META],
                                                      vecs[:, m:m + 1], u_hi[:, m, 0:META].bitcast(F32),
                                                      ALU.mult, ALU.subtract)
            last.then_inc(free(b), 1)
            norm_turned(0, u_hi, u_lo, META + BANK)

            for par in range(2):
                nc.vector.memset(z[:, par, 0, 0:PAD], 0.0)
            nc.vector.memset(vt[:, 0:PAD], 0.0).then_inc(S["pads"], 1)

            def da_group(g, p):
                b = bank_proj()
                if g < 3:
                    return
                wait("proj_hi")
                c0, c1 = KV_PARTS[g - 3] if g < 6 else ((g - 6) * HALF, (g - 5) * HALF)
                hi, lo = (k_hi, k_lo) if g < 6 else (q_hi, q_lo)
                low(lo[:, p, c0:c1], b, hi[:, p, c0:c1], c1 - c0).then_inc(free(b), 1)

            def da_values(part, p):
                b = bank_tr()
                wait("tr_hi")
                t0, t1 = KV_TILES[part]
                low(v_da[:, p, t0:t1, 1, :], b, v_da[:, p, t0:t1, 0, :], (t1 - t0) * P)\
                    .then_inc(free(b), 1)

            def da_logits(s):
                i = s % TT
                pieces = key_pieces(i)
                for c in range(2):
                    for j, (k0, k1) in enumerate(pieces):
                        b = SC + score_bank(turn[2])[0]
                        turn[2] += 1
                        wait("sc_full")
                        off = k0 + P * (TT - 1 - i)
                        dve.nop(nofuse=True)
                        nc.vector.tensor_tensor_reduce(z[:, s % 2, c, PAD + k0:PAD + k1], psum[:, b, 0:k1 - k0],
                                                       bias[:, off:off + k1 - k0], 1.0, -3e38,
                                                       ALU.add, ALU.max, mx[:, c, j:j + 1])\
                            .then_inc(S["sc_free"], 1)
                        seen["sc_free"].next()
                dve.wait_ge(S["sc_free"], seen["sc_free"].value())
                link(nc.vector.tensor_reduce(mxc[:, :], mx[:, :, 0:len(pieces)], AX_X, ALU.max))
                nc.vector.tensor_scalar(nb[:, :], mxc[:, :], -DA_SCALE, None, ALU.mult).then_inc(S["nb"], 1)
                seen["nb"].next()

            def da_turned(g0, g1):
                b = bank_tr()
                wait("tr_hi")
                low(at_lo[:, g0:g1, :], b, at_hi[:, g0:g1, :], (g1 - g0) * P).then_inc(free(b), 1)

            def da_combine(s):
                par = s % 2
                wait("expd", 2)
                link(nc.vector.reciprocal(rec[:, par, :], sums[:, par, :]))
                link(nc.vector.tensor_scalar(cf, sums[:, par, 0:1], neglam, rec[:, par, 1:2],
                                             ALU.mult, ALU.mult))
                nk = META + P * (s % TT + 1)
                z0, z1 = z[:, par, 0, PAD:PAD + nk], z[:, par, 1, PAD:PAD + nk]
                nc.vector.scalar_tensor_tensor(z0, z1, cf, z0, ALU.mult, ALU.add).then_inc(S["a_ready"], 1)

            def da_y(s):
                j, par = s % 4, (s // 4) % 2
                wait("pv_low")
                seen["pv_free"].next()
                y = y_q[:, par, j, :]
                nc.vector.scalar_tensor_tensor(y, psum[:, PV, 0:P], rec[:, s % 2, 0:1],
                                               y_low[:, s % 2, :], ALU.mult, ALU.add)\
                    .then_inc(S["pv_free"], 1)
                dve.wait_ge(S["pv_free"], seen["pv_free"].value())
                link(nc.vector.tensor_tensor_reduce(junk1[:, :], y, y, 1.0, 0.0, ALU.mult, ALU.add,
                                                    ss[:, j:j + 1]))
                if j == 3:
                    rsqrt(0, 4, P)
                    for j in range(4):
                        y = y_q[:, par, j, :]
                        last = nc.vector.tensor_scalar(y, y, rs[:, j:j + 1], None, ALU.mult)
                    last.then_inc(S["y_ready"], 1)

            def next_slope():
                link(nc.vector.tensor_scalar(bias[:, :], bias[:, :], 0.5, None, ALU.mult))

            def da_step(s, more=True):
                i = s % TT
                blocks = block_groups((s - 1) % TT) if s else []
                da_logits(s)
                for g0, g1 in blocks[:2]:
                    da_turned(g0, g1)
                if s > 1:
                    da_y(s - 2)
                for g0, g1 in blocks[2:]:
                    da_turned(g0, g1)
                if i in (2, 6) and s > 4:
                    bank_tr()
                if more and i in (1, 2, 3):
                    da_values(i - 1, (s // TT + 1) % 2)
                da_combine(s)
                if more:
                    da_group(i, (s // TT + 1) % 2)
                if i == TT - 1 and more:
                    next_slope()

            next_slope()
            for g in range(8):
                da_group(g, 0)
                if g in (1, 2, 3):
                    da_values(g - 1, 0)
            for s in range(DA_PEEL):
                da_step(s)
            with seen.loop(dve, 3, DA_TURN):
                for s in range(DA_PEEL, DA_PEEL + 2 * TT):
                    da_step(s)
            for s in range(DA_PEEL + 6 * TT, 8 * TT):
                da_step(s, more=s < 7 * TT)
            for g0, g1 in block_groups(TT - 1):
                da_turned(g0, g1)
            da_y(8 * TT - 2)
            da_y(8 * TT - 1)
            bank_tr()

            for slot in range(2):
                dve.wait_ge(S[f"y_out{slot}"], 16 * (1 + DA_HEADS))
            for x in (rk_hi, rk_lo):
                for d in range(DKT):
                    nc.vector.memset(x[:, d, 0:PAD].bitcast(F32), 0.0)
            nc.vector.memset(rvt[:, 0:PAD], 0.0).then_inc(S["pads"], 1)

            def ret_values(m, part):
                b = bank_tr()
                wait("tr_hi")
                t0, t1 = KV_TILES[part]
                cols = slice(m * P, (m + 1) * P)
                low(rv_lo[:, t0:t1, cols], b, rv_hi[:, t0:t1, cols], (t1 - t0) * P).then_inc(free(b), 1)

            def ret_low(hi, lo):
                b = bank_proj()
                wait("proj_hi")
                low(lo, b, hi, lo.shape[-1]).then_inc(free(b), 1)

            def ret_keys(head):
                wait("k_hi")
                nc.vector.scalar_tensor_tensor(kt_lo[:, :], psum[:, SK, P:P + RDK], dec[:, P + 1:P + 2],
                                               kt_hi[:, :].bitcast(F32), ALU.mult, ALU.subtract)\
                    .then_inc(S["k_ready"], 1)

            def ret_state(head, first):
                wait("st_full")
                flat = state[:, :, :].rearrange("p d n -> p (d n)")
                src = psum[:, ST:ST + DKT, :].rearrange("p d n -> p (d n)")
                if first:
                    ins = nc.vector.tensor_copy(flat, src)
                else:
                    ins = nc.vector.scalar_tensor_tensor(flat, flat, dec[:, P + 2:P + 3], src,
                                                         ALU.mult, ALU.add)
                seen["st_free"].next()
                ins.then_inc(S["st_free"], 1)
                wait("s_hi")
                nc.vector.tensor_tensor(s_lo[:, :, :], state[:, :, :], s_hi[:, :, :].bitcast(F32),
                                        ALU.subtract).then_inc(S["s_ready"], 1)

            with seen.loop(dve, RET_HEADS, RET_TURN) as head:
                nc.vector.tensor_copy(dec[:, :], decay[:, head, :]).then_inc(S["dec"], 1)
                seen["dec"].next()
                dve.wait_ge(S["dec"], seen["dec"].value())
                late = []
                for m in range(DVT):
                    for part in range(3):
                        bank_proj()
                        for m1, p1 in late:
                            ret_values(m1, p1)
                        late = [(m, part)]
                for d in range(DKT):
                    for part in range(3):
                        c0, c1 = KV_PARTS[part]
                        ret_low(rk_hi[:, d, PAD + c0:PAD + c1], rk_lo[:, d, PAD + c0:PAD + c1])
                        for m1, p1 in late:
                            ret_values(m1, p1)
                        late = []
                for d in range(DKT):
                    for part in range(2):
                        cols = slice(part * HALF, (part + 1) * HALF)
                        ret_low(rq_hi[:, d, cols], rq_lo[:, d, cols])
                seen["sk_full"].next()
                ret_keys(head)
                ret_state(head, True)
                for c in range(TT):
                    wait("sk_full")
                    nc.vector.tensor_tensor(p_f[:, :], psum[:, SK, 0:P], dec[:, 0:P], ALU.mult)\
                        .then_inc(S["p_mul"], 1)
                    wait("p_hi")
                    nc.vector.tensor_tensor(p_lo[:, :], p_f[:, :], p_hi[:, :].bitcast(F32), ALU.subtract)\
                        .then_inc(S["p_ready"], 1)
                    if c < TT - 1:
                        ret_keys(head)
                    wait("o_sq")
                    rsqrt(c % 2, c % 2 + 1, RDV)
                    nc.vector.tensor_scalar(o_n[:, c % 2, :], psum[:, OUT, :], dec[:, P:P + 1],
                                            rs[:, c % 2:c % 2 + 1], ALU.mult, ALU.mult)\
                        .then_inc(S["o_free"], 1)
                    if c < TT - 1:
                        ret_state(head, False)
                    b = bank_proj()
                    wait("g_sig")
                    out = seen[f"g_out{c % 2}"]
                    dve.wait_ge(S[f"g_out{c % 2}"], out.value16())
                    out.next()
                    nc.vector.tensor_tensor(g_st[:, c % 2, :], psum[:, b, :], sg[:, :], ALU.mult)\
                        .then_inc(free(b), 1)
                    bank_tr()
                dve.wait_ge(S["o_free"], seen["o_free"].next(TT))

            for slot in range(2):
                dve.wait_ge(S[f"ry_out{slot}"], 16 * (1 + 4 * RET_HEADS))
                dve.wait_ge(S[f"g_out{slot}"], seen[f"g_out{slot}"].value16())

            def split_ret(n):
                slot = n % 2
                dve.wait_ge(S[f"y_in{slot}"], 32 * (n // 2 + 1))
                nc.vector.tensor_tensor(y_in[:, slot, :], y_in[:, slot, :], g_in[:, slot, :], ALU.mult)\
                    .then_inc(S["y_mul"], 1)
                split_low(n)

            def split_low(n):
                wait("y_hi")
                nc.vector.tensor_tensor(y_lo[:, n % 8, :], y_in[:, n % 2, :], y_hi[:, n % 8, :].bitcast(F32),
                                        ALU.subtract).then_inc(S["y_split"], 1)

            def ret_add(hr, g):
                m, half = g // 2, g % 2
                b = bank_proj()
                filled("proj_full")
                a = acc[:, m, half * HALF:(half + 1) * HALF]
                if hr == 0:
                    nc.vector.tensor_copy(a, psum[:, b, :]).then_inc(free(b), 1)
                else:
                    dve.wait_ge(free(b), seen[f"proj_free{b}"].value(1))
                    nc.vector.tensor_tensor(a, a, psum[:, b, :], ALU.add).then_inc(free(b), 1)

            for n in range(4):
                split_ret(n)
            for hr in range(RET_HEADS):
                for q in range(4):
                    for g in range(4 * q, 4 * q + 4):
                        ret_add(hr, g)
                    if hr < RET_HEADS - 1:
                        split_ret(4 * hr + 4 + q)

            def gate_wait(b):
                dve.wait_ge(free(b), seen[f"proj_free{b}"].value())

            for m in range(KT):
                for half in range(2):
                    b = bank_proj()
                    gate_wait(b)
                    a = acc[:, m, half * HALF:(half + 1) * HALF]
                    nc.vector.tensor_tensor(a, a, gate[:, half, :], ALU.mult).then_inc(S["gated"], 1)
                    seen["gated"].next()
                split_low(16 + m)
            for m in range(KT):
                for half in range(2):
                    b = bank_proj()
                    gate_wait(b)
                for half in range(2):
                    b = bank_proj()
                    filled("proj_full")
                    a = acc[:, m, half * HALF:(half + 1) * HALF]
                    g = gate[:, half, :]
                    sem_b = free(b)
                    nc.vector.tensor_tensor(g, psum[:, b, :], g, ALU.mult).then_inc(sem_b, 1)
                    dve.wait_ge(sem_b, seen[f"proj_free{b}"].value())
                    dve.wait_ge(S["gated"], seen["gated"].value())
                    nc.vector.tensor_tensor(a, a, g, ALU.add).then_inc(S["gated"], 1)
                    seen["gated"].next()
            for q in range(4):
                tok = slice(q * 256, (q + 1) * 256)
                wait("mrg_hi")
                nc.vector.tensor_tensor(y_lo[:, :, tok], acc[:, :, tok], y_hi[:, :, tok].bitcast(F32),
                                        ALU.subtract).then_inc(S["mrg_lo"], 1)

            dve.wait_ge(S["h_in"], 16)
            for g in range(2 * KT):
                m, half = g // 2, g % 2
                bank_proj()
                b = bank_tr()
                filled("tr_full")
                h = h2[:, 4 * half:4 * half + 4, m * P:(m + 1) * P]
                nc.vector.tensor_tensor(h, h, psum[:, b, :].rearrange("p (t n) -> p t n", n=P), ALU.add)\
                    .then_inc(free(b), 1)

            dve.wait_ge(S["act"], 9 + TT)
            rsqrt(0, TT, D)
            for j in range(TT):
                last = nc.vector.tensor_scalar(diag2[:, j, :], ident[:, :], rs[:, j:j + 1], None, ALU.mult)
            last.then_inc(S["diag"], 1)
            for half in range(2):
                norm_turned(KT, y_hi, y_lo, half * HALF)

            def mlp(then=None):
                for g in range(2 * FF_BLOCK):
                    b = bank_proj()
                    dve.wait_ge(free(b), seen[f"proj_free{b}"].value())
                    nc.vector.tensor_tensor(f_s[:, b, :], f_r[:, b, :], f_r[:, b, :], ALU.mult)\
                        .then_inc(S["f_sq"], 1)
                    wait("f_hi")
                    seen["f_sq"].next()
                    tok = slice((g % 2) * HALF, (g % 2 + 1) * HALF)
                    nc.vector.tensor_tensor(f_lo[:, g // 2, tok], f_s[:, b, :],
                                            f_hi[:, g // 2, tok].bitcast(F32), ALU.subtract)\
                        .then_inc(S["f_lo"], 1)
                    seen["f_lo"].next()
                for tok in range(TT):
                    for half in range(2):
                        b = bank_proj()
                        filled("proj_full")
                        dve.wait_ge(free(b), seen[f"proj_free{b}"].value(1))
                        h = h2[:, tok, half * BANK:(half + 1) * BANK]
                        nc.vector.tensor_tensor(h, h, psum[:, b, :], ALU.add).then_inc(free(b), 1)
                    if then and tok:
                        then(tok - 1)

            def finish(j):
                if j == 0:
                    dve.wait_ge(S["fin_in"], 16)
                dve.wait_ge(S["act"], 9 + TT + j + 1)
                rsqrt(j, j + 1, D)
                if j >= 2:
                    dve.wait_ge(S[f"out{j % 2}"], 16 * (j // 2))
                nc.vector.scalar_tensor_tensor(out_st[:, j % 2, :], h2[:, j, :], rs[:, j:j + 1],
                                               g_fin[:, :], ALU.mult, ALU.mult).then_inc(S["fin"], 1)

            mlp()
            with seen.loop(dve, N_BLOCKS - 2, MLP_TURN):
                mlp()
            mlp(then=finish)
            finish(TT - 1)


def feature_tiles(w):
    k, m = w.shape
    return w.reshape(k // P, P, m // P, P).transpose(2, 1, 0, 3).reshape(m // P, P, k)


def weight_stream(w_in, w_da, w_ret, w_out, w_up, w_down):
    tiles = feature_tiles(w_in)
    qa, ka, va, qr, kr, vr, gr, g_a, g_r = 0, 8, 16, 24, 32, 40, 56, 72, 80
    order = []
    for h in range(DA_HEADS):
        order += [va + h, ka + h, qa + h]
    for h in range(RET_HEADS):
        order += [vr + DVT * h + j for j in range(DVT)]
        order += [kr + DKT * h + j for j in range(DKT)] + [qr + DKT * h + j for j in range(DKT)]
        order += [gr + DVT * h + j for j in range(DVT)]
    ret = w_ret.reshape(RET_HEADS, DVT, P, 4, 2, P).transpose(0, 3, 2, 4, 1, 5).reshape(16, P, D)
    gate_r, gate_a, da = tiles[g_r:g_r + KT], tiles[g_a:g_a + KT], feature_tiles(w_da)
    both = np.stack([gate_a, da], axis=1).reshape(2 * KT, P, D)
    up, down = feature_tiles(w_up), w_down.reshape(FF // P, P, D)
    both_mlp = {"up": up.reshape(N_BLOCKS, FF_BLOCK, P, D), "down": down.reshape(N_BLOCKS, FF_BLOCK, P, D)}
    mlp = np.stack([both_mlp[kind][:, j] for kind, j in MLP_ORDER], axis=1)
    return np.concatenate([tiles[np.array(order)], ret, gate_r, both, feature_tiles(w_out),
                           mlp.reshape(-1, P, D)])


def decay_tables():
    j, i = np.arange(P, dtype=np.float64)[:, None], np.arange(P, dtype=np.float64)[None, :]
    out = np.zeros((P, RET_HEADS, P + 3))
    for h in range(RET_HEADS):
        g = 1.0 - 2.0 ** (-5.0 - h)
        out[:, h, 0:P] = np.where(i >= j, g ** -(j + 1.0), 0.0) * RDK ** -0.5
        out[:, h, P] = g ** (j[:, 0] + 1.0)
        out[:, h, P + 1] = g ** (P - 1.0 - j[:, 0]) * RDK ** -0.5
        out[:, h, P + 2] = g ** P
    return out.astype(np.float32)


def distance_table():
    q, k = np.arange(P)[:, None] + META + SEQ - P, np.arange(L)[None, :]
    return np.where(k <= q, (k - q) / DA_SCALE, -1e30).astype(np.float32)


def kernel(x, meta_tokens, norm_mix_g, w_in, da_lambda_q1, da_lambda_k1, da_lambda_q2, da_lambda_k2,
           da_head_g, w_proj_da, w_proj_ret, w_out, norm_mlp_g, w_up, w_down, final_norm_g):
    import concourse.bacc as bacc
    from concourse.bass_utils import run_bass_kernel_spmd

    np_in = {
        "x": np.asarray(x)[0],
        "meta": np.asarray(meta_tokens),
        "w": weight_stream(np.asarray(w_in)[0], np.asarray(w_proj_da)[0], np.asarray(w_proj_ret)[0],
                           np.asarray(w_out)[0], np.asarray(w_up)[0], np.asarray(w_down)[0]),
        "vecs": np.concatenate([np.asarray(norm_mix_g)[0].reshape(KT, P),
                                np.asarray(norm_mlp_g)[0].reshape(KT, P),
                                np.asarray(da_head_g)[0].reshape(1, P)]).T,
        "lamv": np.broadcast_to(np.stack([np.asarray(v)[0] for v in (
            da_lambda_q1, da_lambda_k1, da_lambda_q2, da_lambda_k2)])[None], (P, 4, DH)),
        "g_fin": np.broadcast_to(np.asarray(final_norm_g)[None], (P, D)),
        "ident": np.eye(P, dtype=np.float32),
        "dist": distance_table(),
        "decay": decay_tables(),
    }
    nc = bacc.Bacc("TRN2", target_bir_lowering=False, num_devices=1)
    arrays, t = {}, {}
    for name, a in np_in.items():
        a = np.ascontiguousarray(a)
        arrays[f"in_{name}"] = a
        t[name] = nc.dram_tensor(f"in_{name}", a.shape, mybir.dt.from_np(a.dtype), kind="ExternalInput").ap()
    t["out"] = nc.dram_tensor("out_0", (1, SEQ, D), F32, kind="ExternalOutput").ap()
    t["yd"] = nc.dram_tensor("y_da_scratch", (DA_HEADS, P, SEQ), F32, kind="Internal").ap()
    t["yr"] = nc.dram_tensor("y_ret_scratch", (RET_HEADS, P, DVT, SEQ), F32, kind="Internal").ap()
    t["gr"] = nc.dram_tensor("gate_scratch", (RET_HEADS, P, DVT, SEQ), F32, kind="Internal").ap()
    build(nc, t)
    r = run_bass_kernel_spmd(nc, [arrays], core_ids=[0])
    return r.results[0]["out_0"]
```

```python
import math
from contextlib import ExitStack, contextmanager

import numpy as np

import concourse.bass as bass
from concourse import mybir

F32 = mybir.dt.float32
F32R = mybir.dt.float32r
I32 = mybir.dt.int32
ALU = mybir.AluOpType
ACT = mybir.ActivationFunctionType
AX_X = mybir.AxisListType.X

P = 128
D = 1024
KT = D // P
META = 16
SEQ = 1024
L = META + SEQ
TT = SEQ // P
PAD = P - META
LP = PAD + L
BANK = 512
HALF = SEQ // 2
EPS = 1e-6
MAP_ORIGIN = 16512
MAP_SIZE = 53200

DA_HEADS = 8
DH = 64
LAM_INIT = 0.8 - 0.6 * math.exp(-0.3 * 0)
DA_SCALE = DH ** -0.5

RET_HEADS = 4
RDK = D // RET_HEADS
RDV = 2 * D // RET_HEADS
DKT = RDK // P
DVT = RDV // P

FF = 4 * D
FF_BLOCK = 4
N_BLOCKS = FF // P // FF_BLOCK

KV_PARTS = [(0, META + 3 * P), (META + 3 * P, META + 6 * P), (META + 6 * P, L)]
KV_TILES = [(0, 4), (4, 7), (7, 9)]
Q_PARTS = [(META, META + HALF), (META + HALF, L)]

T_DA = 3 * DA_HEADS
T_RET = DVT + 12 * RET_HEADS
T_BRANCH = 2 * KT + KT // 2 + 4 * RET_HEADS
T_RING = T_DA + T_RET + T_BRANCH + KT
T_ALL = T_RING + N_BLOCKS * 2 * FF_BLOCK
MLP_ORDER = [("up", 0), ("up", 1), ("down", 0), ("down", 1), ("up", 2), ("down", 2), ("up", 3), ("down", 3)]


class Tally:

    def __init__(self):
        self.n, self.turn, self.per = 0, None, 0

    def next(self, k=1):
        self.n += k
        return self.value()

    def value(self, back=0):
        v = self.n - back
        assert v > 0
        return v if self.turn is None else self.turn * self.per + v

    def value16(self):
        v = 16 * self.n
        assert v > 0
        return v if self.turn is None else self.turn * (16 * self.per) + v


class Tallies:

    def __init__(self):
        self.of = {}

    def __getitem__(self, name):
        return self.of.setdefault(name, Tally())

    @contextmanager
    def loop(self, eng, turns, per):
        before = {}
        with eng.Fori(0, turns) as turn:
            for name in per:
                t = self[name]
                before[name] = t.n
                t.turn, t.per = turn, per[name]
            frozen = {k: t.n for k, t in self.of.items() if k not in per}
            yield turn
            for k, t in self.of.items():
                if k in before:
                    assert t.n - before[k] in (0, per[k]), (k, t.n - before[k], per[k])
                else:
                    assert t.n == frozen.get(k, 0), (k, t.n - frozen.get(k, 0), "missing")
        for name in per:
            t = self[name]
            t.turn = None
            t.n = before[name] + per[name] * turns


CONST_IN = 16 * 5
DA_TURN = {
    "w_split": 6, "w_used": 6, "proj_full": 16, "proj_hi": 10, "proj_free0": 8, "proj_free1": 8,
    "tr_full": 38, "tr_hi": 34, "tr_free0": 19, "tr_free1": 19, "sc_full": 56, "sc_free": 56,
    "nb": 16, "expd": 32, "a_ready": 16, "pv_full": 16, "pv_low": 16, "pv_free": 16,
    "y_ready": 4, "y_out0": 2, "y_out1": 2, "dve": 114,
}
RET_TURN = {
    "w_split": 12, "w_used": 12, "proj_full": 30, "proj_hi": 10, "proj_free0": 15, "proj_free1": 15,
    "tr_full": 20, "tr_hi": 12, "tr_free0": 10, "tr_free1": 10, "sk_full": 9, "k_hi": 8,
    "k_ready": 8, "st_full": 8, "st_free": 8, "s_hi": 8, "s_ready": 8, "p_mul": 8, "p_hi": 8,
    "p_ready": 8, "o_full": 8, "o_sq": 8, "o_free": 8, "o_diag": 8, "ry_out0": 4, "ry_out1": 4,
    "g_out0": 4, "g_out1": 4, "dve": 96, "dec": 1,
}
MLP_TURN = {
    "w_split": 8, "w_used": 8, "proj_full": 24, "proj_free0": 12, "proj_free1": 12,
    "f_sq": 8, "f_hi": 8, "f_lo": 8,
}


SIGNALS = {
    "const_in": "a constant is in", "x_a": "meta tokens or a tile of the first four is in",
    "x_b": "a tile of the last four is in", "raw_in0": "a weight tile is in", "raw_in1": "",
    "y_out0": "attention output is stored", "y_out1": "", "ry_out0": "retention output is stored",
    "ry_out1": "", "g_out0": "retention gate is stored", "g_out1": "",
    "y_in0": "a branch's tile (or its gate) is back", "y_in1": "", "h_in": "tokens are in h2",
    "fin_in": "the final gain is in", "out0": "a result tile is stored", "out1": "",
    "w_hi": "Pool rounded a weight tile", "w_split": "Pool split a weight tile",
    "w_used": "PE is done with a weight tile", "down_used": "PE is done with a block's down rows",
    "proj_full": "PE filled a projection bank", "proj_hi": "ScalarE rounded a projection bank",
    "proj_free0": "a projection bank has been read", "proj_free1": "",
    "tr_full": "PE filled a transpose bank", "tr_hi": "ScalarE rounded a transpose bank",
    "tr_free0": "a transpose bank has been read", "tr_free1": "",
    "pads": "VectorE cleared zero columns", "lam": "lambda's exponents are there",
    "lam_e": "and their exponentials", "diag": "diag(1 / rms) of a group of token tiles is there",
    "act": "ScalarE wrote a sum of squares", "dve": "VectorE wrote what it reads next",
    "sc_full": "PE filled a bank of scores", "sc_free": "VectorE read a bank of scores",
    "nb": "minus the rows' maxima are there", "expd": "exponentials and their sum are there",
    "a_ready": "the two maps are combined", "pv_full": "PE summed the values",
    "pv_low": "ScalarE read the low half of that sum", "pv_free": "VectorE read the high half",
    "y_ready": "four query tiles are normalised",
    "dec": "this head's decay is in `dec`", "sk_full": "PE wrote scores and keys by token",
    "k_hi": "ScalarE rounded the decayed keys", "k_ready": "their rest is there too",
    "st_full": "PE wrote a chunk's k^T v", "st_free": "VectorE added it to the state",
    "s_hi": "ScalarE rounded the state", "s_ready": "its rest is there too",
    "p_mul": "VectorE decayed the scores", "p_hi": "ScalarE rounded them",
    "p_ready": "their rest is there too", "o_full": "PE wrote a chunk's output",
    "o_sq": "ScalarE summed its squares", "o_free": "VectorE copied it",
    "o_diag": "diag(1 / rms) of it is there",
    "yd_in0": "two tiles of attention's output are back", "yd_in1": "", "yd_in2": "", "yd_in3": "",
    "gr_in": "raw gate tiles are back", "g_raw": "their sigmoid is there", "silu": "a gate's silu is there",
    "y_mul": "a retention tile is gated", "y_hi": "ScalarE rounded a branch's tile",
    "y_split": "its rest is there too", "mrg_hi": "ScalarE rounded half a tile of `acc`",
    "mrg_lo": "its rest is there too",
    "xt_in0": "transposed tokens are in", "xt_in1": "", "ht": "VectorE added them to the output's tile",
    "u2_hi": "ScalarE scaled and rounded the sum", "u2_lo": "its rest is there too",
    "f_sq": "VectorE squared the hidden features", "f_hi": "ScalarE rounded them",
    "f_lo": "their rest is there too", "fin": "a result tile is normalised",
}


def key_pieces(i):
    n = META + P * (i + 1)
    size = -(-n // -(-n // BANK) // META) * META
    return [(k, min(k + size, n)) for k in range(0, n, size)]


SC_PERIOD = 2 * 2 * sum(len(key_pieces(i)) for i in range(TT))


def score_bank(n):
    n %= SC_PERIOD
    return n % 3, (1 if n < 2 else 2)


DA_PEEL = 3


def y_group(s):
    return (s - 2) // 4 - 1


def block_groups(i):
    return [(k, min(k + 4, i + 2)) for k in range(0, i + 2, 4)]


def build(nc, t):
    ctx = ExitStack()
    with ctx:
        ctx.enter_context(nc.sbuf_tensor("map", [P, MAP_SIZE], F32))

        def at(name, offset, shape, dtype=F32):
            size = int(np.prod(shape))
            assert offset + size <= MAP_SIZE, (name, offset + size)
            return nc.alloc_sbuf_tensor_at(name, [P, *shape], dtype, offset=MAP_ORIGIN + 4 * offset)

        class Area:
            def __init__(self, start):
                self.at = start

            def take(self, name, shape, dtype=F32):
                here = self.at
                self.at += (int(np.prod(shape)) + 7) // 8 * 8
                return at(name, here, shape, dtype)

        keep = Area(0)
        ident = keep.take("ident", [P])
        ident_r = keep.take("ident_r", [P], F32R)
        vecs = keep.take("vecs", [2 * KT + 1])
        lamv = keep.take("lamv", [4, DH])
        small = keep.take("small", [96])
        decay = keep.take("decay", [RET_HEADS, P + 3])
        dec = keep.take("dec", [P + 3])
        raw = keep.take("raw", [2, D])
        w_hi = keep.take("w_hi", [2, D], F32R)
        w_lo = keep.take("w_lo", [2, D], F32R)
        u_at = keep.at
        u_hi = keep.take("u_hi", [KT, L], F32R)
        u_lo = keep.take("u_lo", [KT, L], F32R)
        work = keep.at

        ss = small[:, 0:9]
        rs = small[:, 9:18]
        ms = small[:, 18:27]
        nt = small[:, 27:36]
        mx = small[:, 36:42].rearrange("p (c j) -> p c j", c=2)
        mxc = small[:, 42:44]
        nb = small[:, 44:46]
        sums = small[:, 46:50].rearrange("p (b c) -> p b c", b=2)
        rec = small[:, 50:54].rearrange("p (b c) -> p b c", b=2)
        cf = small[:, 54:55]
        lam = small[:, 55:61]
        neglam = small[:, 61:62]
        g_head = small[:, 62:63]
        rs2 = small[:, 64:64 + TT]

        g_st = at("g_st", MAP_SIZE - 2 * BANK, [2, BANK])

        a = Area(work)
        x_in = a.take("x_in", [TT, D])
        x_meta = a.take("x_meta", [D])
        junk0 = a.take("junk0", [D])
        diag0 = a.take("diag0", [TT, P])
        diag_m = a.take("diag_m", [P])

        a = Area(work)
        q_hi = a.take("q_hi", [2, SEQ], F32R)
        q_lo = a.take("q_lo", [2, SEQ], F32R)
        k_hi = a.take("k_hi", [2, L], F32R)
        k_lo = a.take("k_lo", [2, L], F32R)
        v_da = a.take("v_da", [2, 9, 2, P], F32R)
        at_hi = a.take("at_hi", [9, P], F32R)
        at_lo = a.take("at_lo", [9, P], F32R)
        z = a.take("z", [2, 2, LP])
        bias = a.take("bias", [L])
        vt = a.take("vt", [LP])
        y_low = a.take("y_low", [2, P])
        y_q = a.take("y_q", [2, 4, P])
        y_st = a.take("y_st", [2, BANK])
        junk1 = a.take("junk1", [P])

        a = Area(work)
        rq_hi = a.take("rq_hi", [DKT, SEQ], F32R)
        rq_lo = a.take("rq_lo", [DKT, SEQ], F32R)
        rk_hi = a.take("rk_hi", [DKT, LP], F32R)
        rk_lo = a.take("rk_lo", [DKT, LP], F32R)
        rv_hi = a.take("rv_hi", [9, RDV], F32R)
        rv_lo = a.take("rv_lo", [9, RDV], F32R)
        kt_hi = a.take("kt_hi", [RDK], F32R)
        kt_lo = a.take("kt_lo", [RDK], F32R)
        s_hi = a.take("s_hi", [DKT, RDV], F32R)
        s_lo = a.take("s_lo", [DKT, RDV], F32R)
        p_hi = a.take("p_hi", [P], F32R)
        p_lo = a.take("p_lo", [P], F32R)
        state = a.take("state", [DKT, RDV])
        p_f = a.take("p_f", [P])
        rvt = a.take("rvt", [LP])
        o_n = a.take("o_n", [2, RDV])
        diag_o = a.take("diag_o", [2, P])
        a.at = work + 3 * KT * SEQ
        ry_st = a.take("ry_st", [2, DVT, P])
        junk3 = a.take("junk3", [RDV])

        a = Area(work)
        y_hi = a.take("y_hi", [KT, SEQ], F32R)
        y_lo = a.take("y_lo", [KT, SEQ], F32R)
        acc = a.take("acc", [KT, SEQ])
        y_in = a.take("y_in", [2, SEQ])
        g_in = a.take("g_in", [2, SEQ])
        gate = at("gate", a.at - 2 * SEQ, [4, BANK])
        g_ret = at("g_ret", work, [KT, SEQ])
        r_at = [work + KT * SEQ, u_at, u_at + KT * SEQ]
        r_hi = [at(f"r_hi{n}", r_at[n], [DVT, SEQ], F32R) for n in range(3)]
        r_lo = [at(f"r_lo{n}", r_at[n] + DVT * SEQ, [DVT, SEQ], F32R) for n in range(3)]
        m_hi = at("m_hi", u_at, [KT, SEQ], F32R)
        m_lo = at("m_lo", u_at + KT * SEQ, [KT, SEQ], F32R)

        h2 = at("h2", work + 2 * KT * SEQ, [TT, D])
        xt_in = at("xt_in", work + 3 * KT * SEQ, [2, SEQ])
        o_st = at("o_st", a.at - 2 * SEQ, [2, BANK])
        h_t = at("h_t", a.at - SEQ, [2, BANK])

        f_hi = at("f_hi", u_at, [FF_BLOCK, SEQ], F32R)
        f_lo = at("f_lo", u_at + 4096, [FF_BLOCK, SEQ], F32R)
        wd_hi = at("wd_hi", u_at + 8192, [FF_BLOCK, D], F32R)
        wd_lo = at("wd_lo", u_at + 8192 + 4096, [FF_BLOCK, D], F32R)
        f_r = at("f_r", work + 3 * KT * SEQ, [2, BANK])
        f_s = at("f_s", work + 3 * KT * SEQ + SEQ, [2, BANK])
        junk6 = at("junk6", a.at - SEQ, [D])
        g_fin = at("g_fin", work, [D])
        out_st = at("out_st", work + D, [2, D])

        psum = ctx.enter_context(nc.psum_tensor("psum", [P, 8, BANK], F32))
        PROJ, TR, SC, PV = 0, 2, 4, 7
        SK, ST, OUT = 4, 5, 7

        S = {name: ctx.enter_context(nc.semaphore(name)) for name in SIGNALS}
        block = ctx.enter_context(nc.Block())

        @block.sync
        def _(sp):
            for i in range(2):
                sp.dma_start(raw[:, i, :], t["w"][i]).then_inc(S[f"raw_in{i}"], 16)
            with sp.Fori(1, T_ALL // 2) as pair:
                for i in range(2):
                    sp.wait_ge(S["w_split"], pair * 2 + i - 1)
                    sp.dma_start(raw[:, i, :], t["w"][pair * 2 + i]).then_inc(S[f"raw_in{i}"], 16)

        @block.gpsimd
        def _(pool):
            def split(slot, landed, n, hi, lo, apart=True):
                pool.wait_ge(S[f"raw_in{slot}"], landed)
                if apart:
                    pool.nop(nofuse=True)
                nc.gpsimd.tensor_copy(hi, raw[:, slot, :]).then_inc(S["w_hi"], 1)
                pool.wait_ge(S["w_hi"], n)
                nc.gpsimd.tensor_tensor(lo, raw[:, slot, :], hi.bitcast(F32), ALU.subtract)\
                    .then_inc(S["w_split"], 1)

            for i in range(2):
                split(i, 16, i + 1, w_hi[:, i, :], w_lo[:, i, :], apart=False)
            with pool.Fori(1, T_RING // 2) as pair:
                for i in range(2):
                    pool.wait_ge(S["w_used"], pair * 2 + i - 1)
                    split(i, pair * 16 + 16, pair * 2 + i + 1, w_hi[:, i, :], w_lo[:, i, :])

            def mlp_block(b):
                for n, (kind, j) in enumerate(MLP_ORDER):
                    if kind == "up":
                        hi, lo = w_hi[:, j % 2, :], w_lo[:, j % 2, :]
                        pool.wait_ge(S["w_used"], b * FF_BLOCK + (T_RING + j - 1))
                    else:
                        hi, lo = wd_hi[:, j, :], wd_lo[:, j, :]
                        if isinstance(b, int):
                            pool.wait_ge(S["w_used"], T_RING)
                        else:
                            pool.wait_ge(S["down_used"], b)
                    split(n % 2, b * 64 + 16 * ((T_RING + n) // 2 + 1), b * 8 + (T_RING + n + 1), hi, lo,
                          apart=not isinstance(b, int))

            mlp_block(0)
            with pool.Fori(1, N_BLOCKS) as b:
                mlp_block(b)

        @block.tensor
        def _(pe):
            seen = Tallies()
            turn = [0, 0, 0]

            def product(out, st_hi, st_lo, mv_hi, mv_lo, first, last):
                nc.tensor.matmul(out, st_hi, mv_hi, start=first, stop=False)
                nc.tensor.matmul(out, st_hi, mv_lo, start=False, stop=False)
                return nc.tensor.matmul(out, st_lo, mv_hi, start=False, stop=last)

            def next_weights():
                pe.wait_ge(S["w_split"], seen["w_split"].next())

            def take_proj():
                b = turn[0] % 2
                turn[0] += 1
                free = seen[f"proj_free{b}"]
                if free.n:
                    pe.wait_ge(S[f"proj_free{b}"], free.value())
                free.next()
                return PROJ + b

            def take_tr():
                b = turn[1] % 2
                turn[1] += 1
                free = seen[f"tr_free{b}"]
                if free.n:
                    pe.wait_ge(S[f"tr_free{b}"], free.value())
                free.next()
                return TR + b

            def project(slot, mv_h, mv_l, part, first_use, between=None, at=KT // 2):
                c0, c1 = part
                b = take_proj()
                for k in range(KT):
                    if between and k == at:
                        between()
                    cols = slice(k * P, (k + 1) * P)
                    mm = nc.tensor.matmul(psum[:, b, 0:c1 - c0], w_hi[:, slot, cols], mv_h[:, k, c0:c1],
                                          start=k == 0, stop=False)
                    if first_use and k == 0:
                        mm.then_inc(S[first_use], 1)
                    nc.tensor.matmul(psum[:, b, 0:c1 - c0], w_hi[:, slot, cols], mv_l[:, k, c0:c1],
                                     start=False, stop=False)
                    mm = nc.tensor.matmul(psum[:, b, 0:c1 - c0], w_lo[:, slot, cols], mv_h[:, k, c0:c1],
                                          start=False, stop=k == KT - 1)
                mm.then_inc(S["proj_full"], 1)

            def all_free(name):
                for b in range(2):
                    pe.wait_ge(S[f"{name}{b}"], seen[f"{name}{b}"].value())

            pe.wait_ge(S["const_in"], CONST_IN)
            for part in range(2):
                pe.wait_ge(S["diag"], part + 1)
                for m in range(KT):
                    b = take_tr()
                    for j in range(4):
                        mm = nc.tensor.matmul(psum[:, b, j * P:(j + 1) * P],
                                              x_in[:, 4 * part + j, m * P:(m + 1) * P],
                                              diag0[:, 4 * part + j, :], start=True, stop=True)
                    mm.then_inc(S["tr_full"], 1)
                if part == 0:
                    b = take_tr()
                    for m in range(KT):
                        mm = nc.tensor.matmul(psum[:, b, m * META:(m + 1) * META],
                                              x_meta[0:META, m * P:(m + 1) * P],
                                              diag_m[0:META, 0:META], start=True, stop=True)
                    mm.then_inc(S["tr_full"], 1)
            all_free("tr_free")
            pe.wait_ge(S["pads"], 2)

            tile = [0]

            def da_group(g, between=None):
                if g in (0, 3, 6):
                    next_weights()
                    tile[0] += 1
                first = "w_used" if g in (0, 3, 6) and tile[0] > 1 else None
                part = KV_PARTS[g % 3] if g < 6 else Q_PARTS[g - 6]
                project((tile[0] - 1) % 2, u_hi, u_lo, part, first, between)

            def da_values(part):
                last = (turn[0] - 2) % 2
                pe.wait_ge(S[f"proj_free{last}"], seen[f"proj_free{last}"].value())
                b = take_tr()
                for j, tok in enumerate(range(*KV_TILES[part])):
                    mm = nc.tensor.transpose(psum[:, b, j * P:(j + 1) * P],
                                             vt[:, tok * P:(tok + 1) * P], ident[:, :])
                mm.then_inc(S["tr_full"], 1)

            def da_scores(s):
                i, p = s % TT, (s // TT) % 2
                if i == 0:
                    pe.wait_ge(S["proj_free0"], seen["proj_free0"].value())
                for c in range(2):
                    rows = slice(c * DH, (c + 1) * DH)
                    q = slice(i * P, (i + 1) * P)
                    for k0, k1 in key_pieces(i):
                        bank, back = score_bank(turn[2])
                        turn[2] += 1
                        free = seen["sc_free"]
                        if free.n > back:
                            pe.wait_ge(S["sc_free"], free.value(back))
                        free.next()
                        product(psum[:, SC + bank, 0:k1 - k0], q_hi[rows, p, q], q_lo[rows, p, q],
                                k_hi[rows, p, k0:k1], k_lo[rows, p, k0:k1], True, True)\
                            .then_inc(S["sc_full"], 1)

            def da_turn_probs(s, g0, g1):
                b = take_tr()
                for j in range(g0, g1):
                    mm = nc.tensor.transpose(psum[:, b, (j - g0) * P:(j - g0 + 1) * P],
                                             z[:, s % 2, 0, j * P:(j + 1) * P], ident[:, :])
                mm.then_inc(S["tr_full"], 1)

            def da_turn_y(par):
                pe.wait_ge(S["y_ready"], seen["y_ready"].next())
                b = take_tr()
                for j in range(4):
                    mm = nc.tensor.transpose(psum[:, b, j * P:(j + 1) * P], y_q[:, par, j, :],
                                             ident[:, :])
                mm.then_inc(S["tr_full"], 1)

            def da_values_sum(s):
                p, i = (s // TT) % 2, s % TT
                all_free("tr_free")
                free = seen["pv_free"]
                if free.n:
                    pe.wait_ge(S["pv_free"], free.value())
                free.next()
                for j in range(i + 2):
                    nc.tensor.matmul(psum[:, PV, 0:2 * P], at_hi[:, j, :], v_da[:, p, j, :, :],
                                     start=j == 0, stop=False)
                    mm = nc.tensor.matmul(psum[:, PV, 0:P], at_lo[:, j, :], v_da[:, p, j, 0, :],
                                          start=False, stop=j == i + 1)
                mm.then_inc(S["pv_full"], 1)

            def ret_gate(m, half, between):
                if half == 0:
                    next_weights()
                project(m % 2, u_hi, u_lo, Q_PARTS[half], None if half else "w_used", between)

            def da_step(s, more=True):
                i = s % TT
                da_scores(s)
                blocks = block_groups((s - 1) % TT) if s else []
                if s:
                    pe.wait_ge(S["a_ready"], seen["a_ready"].next())
                for g0, g1 in blocks[:2]:
                    da_turn_probs(s - 1, g0, g1)

                def middle():
                    for g0, g1 in blocks[2:]:
                        da_turn_probs(s - 1, g0, g1)
                    if i in (2, 6) and s > 4:
                        da_turn_y(y_group(s) % 2)
                    if more and i in (1, 2, 3):
                        da_values(i - 1)

                if more:
                    da_group(i, middle)
                else:
                    ret_gate(i // 2, i % 2, middle)
                if s:
                    da_values_sum(s - 1)

            for g in range(8):
                da_group(g)
                if g in (1, 2, 3):
                    da_values(g - 1)
            for s in range(DA_PEEL):
                da_step(s)
            with seen.loop(pe, 3, DA_TURN):
                for s in range(DA_PEEL, DA_PEEL + 2 * TT):
                    da_step(s)
            for s in range(DA_PEEL + 6 * TT, 8 * TT):
                da_step(s, more=s < 7 * TT)
            pe.wait_ge(S["a_ready"], seen["a_ready"].next())
            for n, (g0, g1) in enumerate(block_groups(TT - 1)):
                da_turn_probs(8 * TT - 1, g0, g1)
            da_values_sum(8 * TT - 1)
            da_turn_y(y_group(8 * TT + 2) % 2)

            def ret_values(m, part):
                last = (turn[0] - 2) % 2
                pe.wait_ge(S[f"proj_free{last}"], seen[f"proj_free{last}"].value())
                b = take_tr()
                for j, tok in enumerate(range(*KV_TILES[part])):
                    mm = nc.tensor.transpose(psum[:, b, j * P:(j + 1) * P],
                                             rvt[:, tok * P:(tok + 1) * P], ident[:, :])
                mm.then_inc(S["tr_full"], 1)

            def ret_turn_y(c):
                pe.wait_ge(S["o_diag"], seen["o_diag"].next())
                b = take_tr()
                for j in range(DVT):
                    mm = nc.tensor.matmul(psum[:, b, j * P:(j + 1) * P], o_n[:, c % 2, j * P:(j + 1) * P],
                                          diag_o[:, c % 2, :], start=True, stop=True)
                mm.then_inc(S["tr_full"], 1)

            def ret_scores(c):
                cols = slice((c + 1) * P, (c + 2) * P)
                if seen["k_ready"].n:
                    pe.wait_ge(S["k_ready"], seen["k_ready"].value())
                if c >= 0:
                    q = slice(c * P, (c + 1) * P)
                    for d in range(DKT):
                        mm = product(psum[:, SK, 0:P], rk_hi[:, d, cols], rk_lo[:, d, cols],
                                     rq_hi[:, d, q], rq_lo[:, d, q], d == 0, d == DKT - 1)
                if c < TT - 1:
                    for d in range(DKT):
                        out = psum[:, SK, (d + 1) * P:(d + 2) * P]
                        nc.tensor.matmul(out, rk_hi[:, d, cols], ident_r[:, :], start=True, stop=False)
                        mm = nc.tensor.matmul(out, rk_lo[:, d, cols], ident_r[:, :], start=False, stop=True)
                mm.then_inc(S["sk_full"], 1)

            def ret_state(c):
                pe.wait_ge(S["k_ready"], seen["k_ready"].next())
                if seen["st_free"].n:
                    pe.wait_ge(S["st_free"], seen["st_free"].value())
                seen["st_free"].next()
                for d in range(DKT):
                    cols = slice(d * P, (d + 1) * P)
                    mm = product(psum[:, ST + d, :], kt_hi[:, cols], kt_lo[:, cols],
                                 rv_hi[:, c + 1, :], rv_lo[:, c + 1, :], True, True)
                mm.then_inc(S["st_full"], 1)

            def ret_out(c):
                q = slice(c * P, (c + 1) * P)
                if seen["o_free"].n:
                    pe.wait_ge(S["o_free"], seen["o_free"].value())
                seen["o_free"].next()
                pe.wait_ge(S["s_ready"], seen["s_ready"].next())
                for d in range(DKT):
                    product(psum[:, OUT, :], rq_hi[:, d, q], rq_lo[:, d, q], s_hi[:, d, :],
                            s_lo[:, d, :], d == 0, False)
                pe.wait_ge(S["p_ready"], seen["p_ready"].next())
                product(psum[:, OUT, :], p_hi[:, :], p_lo[:, :], rv_hi[:, c + 1, :],
                        rv_lo[:, c + 1, :], False, True).then_inc(S["o_full"], 1)

            pe.wait_ge(S["pads"], 3)
            with seen.loop(pe, RET_HEADS, RET_TURN):
                late = []
                for m in range(DVT):
                    next_weights()
                    for part in range(3):
                        project(m % 2, u_hi, u_lo, KV_PARTS[part], "w_used" if part == 0 else None)
                        for m1, p1 in late:
                            ret_values(m1, p1)
                        late = [(m, part)]
                for d in range(DKT):
                    next_weights()
                    for part in range(3):
                        project(d % 2, u_hi, u_lo, KV_PARTS[part], "w_used" if part == 0 else None)
                        for m1, p1 in late:
                            ret_values(m1, p1)
                        late = []
                for d in range(DKT):
                    next_weights()
                    for part in range(2):
                        project(d % 2, u_hi, u_lo, Q_PARTS[part], "w_used" if part == 0 else None)
                all_free("proj_free")
                all_free("tr_free")
                ret_scores(-1)
                ret_state(-1)
                for c in range(TT):
                    ret_scores(c)

                    def middle(c=c):
                        ret_out(c)
                        if c < TT - 1:
                            ret_state(c)

                    ret_gate(c // 2, c % 2, middle)
                    if c:
                        ret_turn_y(c - 1)
                ret_turn_y(TT - 1)

            def operand_ready(n):
                pe.wait_ge(S["y_split"], seen["y_split"].next(n))

            HALVES = [(0, HALF), (HALF, SEQ)]

            def gate_tile(slot):
                next_weights()
                for half in range(2):
                    project(slot, u_hi, u_lo, Q_PARTS[half], None if half else "w_used")

            def da_tile(slot):
                next_weights()
                for half in range(2):
                    project(slot, y_hi, y_lo, HALVES[half], None if half else "w_used")

            gate_tile(0)
            gate_tile(1)
            operand_ready(KT)
            pair_turn = {"w_split": 2, "w_used": 2, "proj_free0": 2, "proj_free1": 2}
            with seen.loop(pe, KT - 2, pair_turn):
                da_tile(0)
                gate_tile(1)
            da_tile(0)
            da_tile(1)
            with seen.loop(pe, KT // 4, pair_turn):
                gate_tile(0)
                gate_tile(1)
            for hr in range(RET_HEADS):
                operand_ready(DVT)
                hi, lo = r_hi[hr % 3], r_lo[hr % 3]
                for mp in range(4):
                    next_weights()
                    slot = mp % 2
                    for m2 in range(2):
                        for half in range(2):
                            b = take_proj()
                            tok = slice(half * HALF, (half + 1) * HALF)
                            for k in range(DVT):
                                cols = slice((m2 * DVT + k) * P, (m2 * DVT + k + 1) * P)
                                mm = nc.tensor.matmul(psum[:, b, :], w_hi[:, slot, cols], hi[:, k, tok],
                                                      start=k == 0, stop=False)
                                if (m2, half, k) == (0, 0, 0):
                                    mm.then_inc(S["w_used"], 1)
                                nc.tensor.matmul(psum[:, b, :], w_hi[:, slot, cols], lo[:, k, tok],
                                                 start=False, stop=False)
                                mm = nc.tensor.matmul(psum[:, b, :], w_lo[:, slot, cols], hi[:, k, tok],
                                                      start=False, stop=k == DVT - 1)
                            mm.then_inc(S["proj_full"], 1)

            def turn_o():
                b = turn[0] % 2
                pe.wait_ge(S[f"proj_free{b}"], seen[f"proj_free{b}"].value())
                out = take_tr()
                for j in range(4):
                    mm = nc.tensor.transpose(psum[:, out, j * P:(j + 1) * P],
                                             o_st[:, b, j * P:(j + 1) * P], ident[:, :])
                mm.then_inc(S["tr_full"], 1)

            def until(name, count):
                return lambda: pe.wait_ge(S[name], count)

            for m in range(KT):
                next_weights()
                for half in range(2):
                    last_tile = None
                    if m == 0:
                        pe.wait_ge(S["mrg_lo"], 2 * KT - 3 + half)
                        last_tile = until("mrg_lo", 2 * KT - 1 + half)
                    project(m % 2, m_hi, m_lo, HALVES[half], None if half else "w_used", last_tile, KT - 1)
                    if m or half:
                        turn_o()

            def mlp(first):
                for j in range(FF_BLOCK):
                    pe.wait_ge(S["w_split"], seen["w_split"].next((1, 1, 3, 2)[j]))
                    before = "w_used" if first or j else "down_used"
                    for half in range(2):
                        last_tile = None
                        if first and j == 0:
                            pe.wait_ge(S["u2_lo"], 2 * KT - 3 + half)
                            last_tile = until("u2_lo", 2 * KT - 1 + half)
                        project(j % 2, y_hi, y_lo, HALVES[half], None if half else before, last_tile,
                                KT - 1)
                        if first and j == half == 0:
                            turn_o()
                def down(b, tok, half, ks):
                    out = slice(half * BANK, (half + 1) * BANK)
                    st = slice(tok * P, (tok + 1) * P)
                    for k in ks:
                        mm = nc.tensor.matmul(psum[:, b, :], f_hi[:, k, st], wd_hi[:, k, out],
                                              start=k == 0, stop=False)
                        if (tok, half, k) == (0, 0, 0):
                            mm.then_inc(S["w_used"], 1)
                        nc.tensor.matmul(psum[:, b, :], f_hi[:, k, st], wd_lo[:, k, out],
                                         start=False, stop=False)
                        mm = nc.tensor.matmul(psum[:, b, :], f_lo[:, k, st], wd_hi[:, k, out],
                                              start=False, stop=k == FF_BLOCK - 1)
                    return mm

                pe.wait_ge(S["w_split"], seen["w_split"].next())
                pe.wait_ge(S["f_lo"], seen["f_lo"].next(2 * (FF_BLOCK - 1)))
                banks = []
                for half in range(2):
                    banks.append(take_proj())
                    down(banks[half], 0, half, range(FF_BLOCK - 1))
                pe.wait_ge(S["f_lo"], seen["f_lo"].next(2))
                for half in range(2):
                    down(banks[half], 0, half, [FF_BLOCK - 1]).then_inc(S["proj_full"], 1)
                for tok in range(1, TT):
                    for half in range(2):
                        down(take_proj(), tok, half, range(FF_BLOCK)).then_inc(S["proj_full"], 1)

            mlp(True)
            with seen.loop(pe, N_BLOCKS - 2, MLP_TURN):
                mlp(False)
            mlp(False)

        @block.scalar
        def _(act):
            seen = Tallies()
            turn = [0, 0]

            def wait(name, k=1):
                act.wait_ge(S[name], seen[name].next(k))

            def bank_proj():
                b = turn[0] % 2
                turn[0] += 1
                seen["proj_full"].next()
                seen[f"proj_free{b}"].next()
                return PROJ + b

            def bank_tr():
                b = turn[1] % 2
                turn[1] += 1
                seen["tr_full"].next()
                seen[f"tr_free{b}"].next()
                return TR + b

            def filled(name):
                act.wait_ge(S[name], seen[name].value())

            def free(b):
                return S[f"proj_free{b}" if b < TR else f"tr_free{b - TR}"]

            def step(ins):
                ins.then_inc(S["act"], 1)
                seen["act"].next()

            def settle():
                act.wait_ge(S["act"], seen["act"].value())

            for name in ("y_out0", "y_out1", "ry_out0", "ry_out1"):
                act.sem_inc(S[name], 16)
                seen[name].n = 1
            for dst, src in ((ident[:, :], t["ident"]), (bias[:, :], t["dist"]), (vecs[:, :], t["vecs"]),
                             (lamv[:, :, :], t["lamv"]), (decay[:, :, :], t["decay"])):
                act.dma_start(dst, src).then_inc(S["const_in"], 16)
            act.dma_start(x_meta[0:META, :], t["meta"]).then_inc(S["x_a"], 16)
            for j in range(TT):
                act.dma_start(x_in[:, j, :], t["x"][j * P:(j + 1) * P, :])\
                    .then_inc(S["x_a" if j < 4 else "x_b"], 16)

            act.wait_ge(S["pads"], 1)
            act.wait_ge(S["const_in"], CONST_IN)
            act.wait_ge(S["x_a"], 5 * 16)
            step(nc.scalar.activation(junk0[0:META, :], x_meta[0:META, :], ACT.Square,
                                      accum_out=ss[0:META, 0:1]))
            for part in range(2):
                if part:
                    act.wait_ge(S["x_b"], 4 * 16)
                for j in range(4 * part, 4 * part + 4):
                    settle()
                    step(nc.scalar.activation(junk0[:, :], x_in[:, j, :], ACT.Square,
                                              accum_out=ss[:, j + 1:j + 2]))
            act.wait_ge(S["lam"], 1)
            nc.scalar.activation(lam[:, 2:4], lam[:, 0:2], ACT.Exp).then_inc(S["lam_e"], 1)

            def norm_turned(g0, dst, c0, groups):
                for m in groups:
                    b = bank_tr()
                    filled("tr_full")
                    nc.scalar.activation(dst[:, m, c0:c0 + BANK], psum[:, b, :], ACT.Copy,
                                         scale=vecs[:, g0 + m:g0 + m + 1]).then_inc(S["tr_hi"], 1)

            norm_turned(0, u_hi, META, range(KT))
            b = bank_tr()
            filled("tr_full")
            for m in range(KT):
                last = nc.scalar.activation(u_hi[:, m, 0:META], psum[:, b, m * META:(m + 1) * META],
                                            ACT.Copy, scale=vecs[:, m:m + 1])
            last.then_inc(S["tr_hi"], 1)
            norm_turned(0, u_hi, META + BANK, range(KT))

            def da_group(g, p):
                b = bank_proj()
                filled("proj_full")
                if g < 3:
                    c0, c1 = KV_PARTS[g]
                    nc.scalar.activation(vt[:, PAD + c0:PAD + c1], psum[:, b, 0:c1 - c0], ACT.Copy)\
                        .then_inc(free(b), 1)
                else:
                    c0, c1 = KV_PARTS[g - 3] if g < 6 else ((g - 6) * HALF, (g - 5) * HALF)
                    dst = k_hi if g < 6 else q_hi
                    nc.scalar.activation(dst[:, p, c0:c1], psum[:, b, 0:c1 - c0], ACT.Copy)\
                        .then_inc(S["proj_hi"], 1)

            def da_values(part, p):
                b = bank_tr()
                filled("tr_full")
                t0, t1 = KV_TILES[part]
                nc.scalar.activation(v_da[:, p, t0:t1, 0, :],
                                     psum[:, b, 0:(t1 - t0) * P].rearrange("p (t n) -> p t n", n=P),
                                     ACT.Copy).then_inc(S["tr_hi"], 1)

            def da_turned(g0, g1):
                b = bank_tr()
                filled("tr_full")
                nc.scalar.activation(at_hi[:, g0:g1, :],
                                     psum[:, b, 0:(g1 - g0) * P].rearrange("p (t n) -> p t n", n=P),
                                     ACT.Copy).then_inc(S["tr_hi"], 1)

            stores = [0]

            def da_y(head, half):
                b = bank_tr()
                filled("tr_full")
                slot = stores[0] % 2
                stores[0] += 1
                out = seen[f"y_out{slot}"]
                act.wait_ge(S[f"y_out{slot}"], out.value16())
                sem_b = free(b)
                nc.scalar.activation(y_st[:, slot, :], psum[:, b, :], ACT.Copy, scale=g_head)\
                    .then_inc(sem_b, 1)
                act.wait_ge(sem_b, seen[f"tr_free{b - TR}"].value())
                out.next()
                act.dma_start(t["yd"][head, :, half * HALF:(half + 1) * HALF], y_st[:, slot, :])\
                    .then_inc(S[f"y_out{slot}"], 16)

            def da_exp(s):
                wait("nb")
                nk = META + P * (s % TT + 1)
                for c in range(2):
                    zc = z[:, s % 2, c, PAD:PAD + nk]
                    nc.scalar.activation(zc, zc, ACT.Exp, bias=nb[:, c:c + 1], scale=DA_SCALE,
                                         accum_out=sums[:, s % 2, c:c + 1]).then_inc(S["expd"], 1)

            def da_low(s):
                wait("pv_full")
                nc.scalar.activation(y_low[:, s % 2, :], psum[:, PV, P:2 * P], ACT.Copy,
                                     scale=rec[:, s % 2, 0:1]).then_inc(S["pv_low"], 1)

            def da_step(s, head, more=True):
                i = s % TT
                blocks = block_groups((s - 1) % TT) if s else []
                for g0, g1 in blocks[:2]:
                    da_turned(g0, g1)
                if s > 1:
                    da_low(s - 2)
                da_exp(s)
                for g0, g1 in blocks[2:]:
                    da_turned(g0, g1)
                if i in (2, 6) and s > 4:
                    da_y(head - (1 if i == 2 else 0), 1 if i == 2 else 0)
                if more and i in (1, 2, 3):
                    da_values(i - 1, (s // TT + 1) % 2)
                if more:
                    da_group(i, (s // TT + 1) % 2)
                else:
                    raw_gate(0, i // 2, i % 2)

            def raw_gate(head, m, half):
                b = bank_proj()
                filled("proj_full")
                out = seen[f"g_out{half}"]
                if out.n:
                    act.wait_ge(S[f"g_out{half}"], out.value16())
                out.next()
                nc.scalar.activation(g_st[:, half, :], psum[:, b, :], ACT.Copy).then_inc(free(b), 1)
                act.wait_ge(free(b), seen[f"proj_free{b}"].value())
                act.dma_start(t["gr"][head, :, m, half * HALF:(half + 1) * HALF], g_st[:, half, :])\
                    .then_inc(S[f"g_out{half}"], 16)

            for g in range(8):
                da_group(g, 0)
                if g in (1, 2, 3):
                    da_values(g - 1, 0)
            for s in range(DA_PEEL):
                da_step(s, 0)
            with seen.loop(act, 3, DA_TURN) as pair:
                for s in range(DA_PEEL, DA_PEEL + 2 * TT):
                    da_step(s, pair * 2 + s // TT)
            for s in range(DA_PEEL + 6 * TT, 8 * TT):
                da_step(s, s // TT, more=s < 7 * TT)
            for g0, g1 in block_groups(TT - 1):
                da_turned(g0, g1)
            da_low(8 * TT - 2)
            da_low(8 * TT - 1)
            da_y(7, 1)
            for slot in range(2):
                act.wait_ge(S[f"y_out{slot}"], seen[f"y_out{slot}"].value16())

            def ret_values(m, part):
                b = bank_tr()
                filled("tr_full")
                t0, t1 = KV_TILES[part]
                nc.scalar.activation(rv_hi[:, t0:t1, m * P:(m + 1) * P],
                                     psum[:, b, 0:(t1 - t0) * P].rearrange("p (t n) -> p t n", n=P),
                                     ACT.Copy).then_inc(S["tr_hi"], 1)

            def ret_hi(dst):
                b = bank_proj()
                filled("proj_full")
                nc.scalar.activation(dst, psum[:, b, 0:dst.shape[-1]], ACT.Copy)\
                    .then_inc(S["proj_hi"], 1)

            def ret_keys(head):
                nc.scalar.activation(kt_hi[:, :], psum[:, SK, P:P + RDK], ACT.Copy,
                                     scale=dec[:, P + 1:P + 2]).then_inc(S["k_hi"], 1)

            def ret_state():
                wait("st_free")
                nc.scalar.activation(s_hi[:, :, :], state[:, :, :], ACT.Copy).then_inc(S["s_hi"], 1)

            def ret_y(head, c):
                b = bank_tr()
                filled("tr_full")
                slot = c % 2
                out = seen[f"ry_out{slot}"]
                act.wait_ge(S[f"ry_out{slot}"], out.value16())
                sem_b = free(b)
                nc.scalar.activation(ry_st[:, slot, :, :],
                                     psum[:, b, :].rearrange("p (t n) -> p t n", n=P), ACT.Copy)\
                    .then_inc(sem_b, 1)
                act.wait_ge(sem_b, seen[f"tr_free{b - TR}"].value())
                out.next()
                act.dma_start(t["yr"][head, :, :, c * P:(c + 1) * P], ry_st[:, slot, :, :])\
                    .then_inc(S[f"ry_out{slot}"], 16)

            with seen.loop(act, RET_HEADS, RET_TURN) as head:
                late = []
                for m in range(DVT):
                    for part in range(3):
                        b = bank_proj()
                        filled("proj_full")
                        c0, c1 = KV_PARTS[part]
                        nc.scalar.activation(rvt[:, PAD + c0:PAD + c1], psum[:, b, 0:c1 - c0], ACT.Copy)\
                            .then_inc(free(b), 1)
                        for m1, p1 in late:
                            ret_values(m1, p1)
                        late = [(m, part)]
                for d in range(DKT):
                    for part in range(3):
                        c0, c1 = KV_PARTS[part]
                        ret_hi(rk_hi[:, d, PAD + c0:PAD + c1])
                        for m1, p1 in late:
                            ret_values(m1, p1)
                        late = []
                for d in range(DKT):
                    for part in range(2):
                        ret_hi(rq_hi[:, d, part * HALF:(part + 1) * HALF])
                wait("dec")
                wait("sk_full")
                ret_keys(head)
                ret_state()
                for c in range(TT):
                    wait("p_mul")
                    seen["sk_full"].next()
                    nc.scalar.activation(p_hi[:, :], p_f[:, :], ACT.Copy).then_inc(S["p_hi"], 1)
                    if c < TT - 1:
                        ret_keys(head)
                    wait("o_free")
                    nc.scalar.activation(junk3[:, :], o_n[:, c % 2, :], ACT.Square,
                                         accum_out=ss[:, c % 2:c % 2 + 1]).then_inc(S["o_sq"], 1)
                    if c < TT - 1:
                        ret_state()
                    raw_gate(head + 1, c // 2, c % 2)
                    if c:
                        ret_y(head, c - 1)
                ret_y(head, TT - 1)

            for m in range(KT):
                act.dma_start(acc[:, m, :], t["yd"][m]).then_inc(S[f"yd_in{m // 2}"], 16)
            for slot in range(2):
                act.wait_ge(S[f"ry_out{slot}"], seen[f"ry_out{slot}"].value16())
                act.wait_ge(S[f"g_out{slot}"], seen[f"g_out{slot}"].value16())

            def split_da(m):
                act.wait_ge(S[f"yd_in{m // 2}"], 32)
                nc.scalar.activation(y_hi[:, m, :], acc[:, m, :], ACT.Copy).then_inc(S["y_hi"], 1)

            def gate_half(m, half, dst):
                b = bank_proj()
                filled("proj_full")
                nc.scalar.activation(dst, psum[:, b, :], ACT.Sigmoid).then_inc(free(b), 1)

            def gate_slot(m, half):
                return gate[:, (m % 2) * 2 + half, :]

            for m in range(KT // 2):
                split_da(m)
            gate_half(0, 0, gate_slot(0, 0))
            for m in range(KT // 2, KT):
                split_da(m)
            for m, half in ((0, 1), (1, 0), (1, 1)):
                gate_half(m, half, gate_slot(m, half))
            for m in range(KT):
                for half in range(2):
                    bank_proj()
                if m + 2 < KT:
                    for half in range(2):
                        gate_half(m + 2, half, gate_slot(m + 2, half))

            for b in range(2):
                act.wait_ge(S[f"proj_free{b}"], seen[f"proj_free{b}"].value())
            for m in range(DVT):
                act.dma_start(g_ret[:, m, :], t["gr"][RET_HEADS, :, m, :]).then_inc(S["gr_in"], 16)

            def load(n):
                slot = n % 2
                if n >= 2:
                    act.wait_ge(S["y_split"], KT + n - 1)
                act.dma_start(y_in[:, slot, :], t["yr"][n // 4, :, n % 4, :]).then_inc(S[f"y_in{slot}"], 16)
                act.dma_start(g_in[:, slot, :], t["gr"][n // 4, :, n % 4, :]).then_inc(S[f"y_in{slot}"], 16)

            def silu(n):
                slot = n % 2
                act.wait_ge(S[f"y_in{slot}"], 32 * (n // 2 + 1))
                nc.scalar.activation(g_in[:, slot, :], g_in[:, slot, :], ACT.Silu).then_inc(S["silu"], 1)

            def round_ret(n):
                wait("y_mul")
                nc.scalar.activation(r_hi[(n // 4) % 3][:, n % 4, :], y_in[:, n % 2, :], ACT.Copy)\
                    .then_inc(S["y_hi"], 1)

            def gate_ret(m, half):
                gate_half(m, half, g_ret[:, m, half * HALF:(half + 1) * HALF])

            load(0)
            load(1)
            for n in (0, 2):
                silu(n)
                silu(n + 1)
                round_ret(n)
                load(n + 2)
                gate_ret(4 + n // 2, 0)
                round_ret(n + 1)
                load(n + 3)
                gate_ret(4 + n // 2, 1)
            act.wait_ge(S["gr_in"], 16 * DVT)
            nc.scalar.activation(g_ret[:, 0:2, :], g_ret[:, 0:2, :], ACT.Sigmoid).then_inc(S["g_raw"], 1)
            gate_ret(6, 0)
            nc.scalar.activation(g_ret[:, 2:4, :], g_ret[:, 2:4, :], ACT.Sigmoid).then_inc(S["g_raw"], 1)
            for m, half in ((6, 1), (7, 0), (7, 1)):
                gate_ret(m, half)

            base_proj = seen["proj_full"].n
            for hr in range(RET_HEADS - 1):
                for n in range(4 * hr + 4, 4 * hr + 8):
                    silu(n)
                    if n == 12:
                        act.wait_ge(S["proj_full"], base_proj + 16)
                    round_ret(n)
                    if n + 2 < 16:
                        load(n + 2)
                for _ in range(16):
                    bank_proj()

            def load_xt(m):
                act.dma_start(xt_in[:, m % 2, :], t["xt"][m]).then_inc(S[f"xt_in{m % 2}"], 16)

            def load_h(j):
                act.wait_ge(S["mrg_lo"], 2 * (j + 1))
                act.dma_start(h2[:, j, :], t["x"][j * P:(j + 1) * P, :]).then_inc(S["h_in"], 16)

            act.wait_ge(S["y_split"], KT + 4 * RET_HEADS)
            for m in range(2):
                load_xt(m)
            for g in range(2 * KT):
                m, tok = g // 2, slice((g % 2) * HALF, (g % 2 + 1) * HALF)
                b = bank_proj()
                act.wait_ge(S[f"proj_free{b}"], seen[f"proj_free{b}"].value())
                nc.scalar.activation(m_hi[:, m, tok], acc[:, m, tok], ACT.Copy).then_inc(S["mrg_hi"], 1)
                if g % 2 and m:
                    load_h(m - 1)
            load_h(TT - 1)

            for g in range(2 * KT):
                m, tok = g // 2, slice((g % 2) * HALF, (g % 2 + 1) * HALF)
                b = bank_proj()
                bank_tr()
                filled("proj_full")
                nc.scalar.activation(o_st[:, b, :], psum[:, b, :], ACT.Copy).then_inc(free(b), 1)
                wait("ht")
                nc.scalar.activation(y_hi[:, m, tok], h_t[:, b, :], ACT.Copy,
                                     scale=vecs[:, KT + m:KT + m + 1]).then_inc(S["u2_hi"], 1)
                if g % 2 and m + 2 < KT:
                    load_xt(m + 2)

            def mlp(first=False):
                for g in range(2 * FF_BLOCK):
                    b = bank_proj()
                    filled("proj_full")
                    nc.scalar.activation(f_r[:, b, :], psum[:, b, :], ACT.Relu).then_inc(free(b), 1)
                    wait("f_sq")
                    nc.scalar.activation(f_hi[:, g // 2, (g % 2) * HALF:(g % 2 + 1) * HALF],
                                         f_s[:, b, :], ACT.Copy).then_inc(S["f_hi"], 1)
                    if first and g == 0:
                        for n in range(2):
                            act.wait_ge(S[f"tr_free{n}"], seen[f"tr_free{n}"].value())
                    if first:
                        if g:
                            settle()
                        step(nc.scalar.activation(junk6[:, :], h2[:, g, :], ACT.Square,
                                                  accum_out=ss[:, g:g + 1]))
                for _ in range(2 * TT):
                    bank_proj()

            mlp(first=True)
            with seen.loop(act, N_BLOCKS - 2, MLP_TURN):
                mlp()
            mlp()

            act.wait_ge(S["proj_full"], seen["proj_full"].value(2 * TT - 1))
            act.dma_start(g_fin[:, :], t["g_fin"]).then_inc(S["fin_in"], 16)

            def store_out(j):
                act.wait_ge(S["fin"], j + 1)
                act.dma_start(t["out"][0, j * P:(j + 1) * P, :], out_st[:, j % 2, :])\
                    .then_inc(S[f"out{j % 2}"], 16)

            for j in range(TT):
                for b in range(2):
                    act.wait_ge(S[f"proj_free{b}"], seen[f"proj_free{b}"].value(TT - 1 - j))
                if j:
                    settle()
                step(nc.scalar.activation(f_r[:, :, :], h2[:, j, :].rearrange("p (a n) -> p a n", a=2),
                                          ACT.Square, accum_out=ss[:, j:j + 1]))
                if j:
                    store_out(j - 1)
            store_out(TT - 1)
            for slot in range(2):
                act.wait_ge(S[f"out{slot}"], 16 * TT // 2)

        @block.vector
        def _(dve):
            seen = Tallies()
            turn = [0, 0, 0]

            def wait(name, k=1):
                dve.wait_ge(S[name], seen[name].next(k))

            def bank_proj():
                b = turn[0] % 2
                turn[0] += 1
                seen["proj_full"].next()
                seen[f"proj_free{b}"].next()
                return PROJ + b

            def bank_tr():
                b = turn[1] % 2
                turn[1] += 1
                seen["tr_full"].next()
                seen[f"tr_free{b}"].next()
                return TR + b

            def filled(name):
                dve.wait_ge(S[name], seen[name].value())

            def free(b):
                return S[f"proj_free{b}" if b < TR else f"tr_free{b - TR}"]

            def link(ins):
                ins.then_inc(S["dve"], 1)
                dve.wait_ge(S["dve"], seen["dve"].next())

            def rsqrt(c0, c1, n):
                x, y, w = ms[:, c0:c1], rs[:, c0:c1], nt[:, c0:c1]
                link(nc.vector.tensor_scalar(x, ss[:, c0:c1], 1.0 / n, EPS, ALU.mult, ALU.add))
                link(nc.vector.tensor_scalar(w.bitcast(I32), x.bitcast(I32), 1, None,
                                             ALU.logical_shift_right))
                link(nc.vector.tensor_scalar(y.bitcast(I32), w.bitcast(I32), -1.0, float(0x5F3759DF),
                                             ALU.mult, ALU.add))
                for _ in range(3):
                    link(nc.vector.tensor_tensor(w, y, y, ALU.mult))
                    link(nc.vector.scalar_tensor_tensor(w, w, -0.5, x, ALU.mult, ALU.mult))
                    link(nc.vector.scalar_tensor_tensor(y, w, 1.5, y, ALU.add, ALU.mult))

            def low(dst, b, hi, n):
                src = psum[:, b, 0:n]
                if len(dst.shape) == 3:
                    src = src.rearrange("p (t n) -> p t n", n=P)
                return nc.vector.tensor_tensor(dst, src, hi.bitcast(F32), ALU.subtract)

            nc.vector.memset(small[:, :], 0.0).then_inc(S["pads"], 1)
            dve.wait_ge(S["pads"], 1)
            dve.wait_ge(S["const_in"], CONST_IN)
            nc.vector.tensor_copy(ident_r[:, :], ident[:, :])
            for j in range(2):
                last = nc.vector.tensor_tensor_reduce(lamv[:, 2 * j, :], lamv[:, 2 * j, :], lamv[:, 2 * j + 1, :],
                                                      1.0, 0.0, ALU.mult, ALU.add, lam[:, j:j + 1])
            last.then_inc(S["lam"], 1)
            dve.wait_ge(S["lam_e"], 1)
            link(nc.vector.tensor_tensor(lam[:, 4:5], lam[:, 3:4], lam[:, 2:3], ALU.subtract))
            nc.vector.tensor_scalar(neglam, lam[:, 4:5], -LAM_INIT, None, ALU.add)
            link(nc.vector.tensor_scalar(g_head, vecs[:, 2 * KT:2 * KT + 1], 1.0 - LAM_INIT, None, ALU.mult))
            for part in range(2):
                dve.wait_ge(S["act"], 5 + 4 * part)
                c0, c1 = (0, 5) if part == 0 else (5, 9)
                rsqrt(c0, c1, D)
                if part == 0:
                    nc.vector.tensor_scalar(diag_m[:, :], ident[:, :], rs[:, 0:1], None, ALU.mult)
                for j in range(4 * part, 4 * part + 4):
                    last = nc.vector.tensor_scalar(diag0[:, j, :], ident[:, :], rs[:, j + 1:j + 2], None,
                                                   ALU.mult)
                last.then_inc(S["diag"], 1)

            def norm_turned(g0, hi, lo, c0):
                for m in range(KT):
                    b = bank_tr()
                    wait("tr_hi")
                    nc.vector.scalar_tensor_tensor(lo[:, m, c0:c0 + BANK], psum[:, b, :],
                                                   vecs[:, g0 + m:g0 + m + 1],
                                                   hi[:, m, c0:c0 + BANK].bitcast(F32),
                                                   ALU.mult, ALU.subtract).then_inc(free(b), 1)

            norm_turned(0, u_hi, u_lo, META)
            b = bank_tr()
            wait("tr_hi")
            for m in range(KT):
                last = nc.vector.scalar_tensor_tensor(u_lo[:, m, 0:META], psum[:, b, m * META:(m + 1) * META],
                                                      vecs[:, m:m + 1], u_hi[:, m, 0:META].bitcast(F32),
                                                      ALU.mult, ALU.subtract)
            last.then_inc(free(b), 1)
            norm_turned(0, u_hi, u_lo, META + BANK)

            for par in range(2):
                nc.vector.memset(z[:, par, 0, 0:PAD], 0.0)
            nc.vector.memset(vt[:, 0:PAD], 0.0).then_inc(S["pads"], 1)

            def da_group(g, p):
                b = bank_proj()
                if g < 3:
                    return
                wait("proj_hi")
                c0, c1 = KV_PARTS[g - 3] if g < 6 else ((g - 6) * HALF, (g - 5) * HALF)
                hi, lo = (k_hi, k_lo) if g < 6 else (q_hi, q_lo)
                low(lo[:, p, c0:c1], b, hi[:, p, c0:c1], c1 - c0).then_inc(free(b), 1)

            def da_values(part, p):
                b = bank_tr()
                wait("tr_hi")
                t0, t1 = KV_TILES[part]
                low(v_da[:, p, t0:t1, 1, :], b, v_da[:, p, t0:t1, 0, :], (t1 - t0) * P)\
                    .then_inc(free(b), 1)

            def da_logits(s):
                i = s % TT
                pieces = key_pieces(i)
                for c in range(2):
                    for j, (k0, k1) in enumerate(pieces):
                        b = SC + score_bank(turn[2])[0]
                        turn[2] += 1
                        wait("sc_full")
                        off = k0 + P * (TT - 1 - i)
                        dve.nop(nofuse=True)
                        nc.vector.tensor_tensor_reduce(z[:, s % 2, c, PAD + k0:PAD + k1], psum[:, b, 0:k1 - k0],
                                                       bias[:, off:off + k1 - k0], 1.0, -3e38,
                                                       ALU.add, ALU.max, mx[:, c, j:j + 1])\
                            .then_inc(S["sc_free"], 1)
                        seen["sc_free"].next()
                dve.wait_ge(S["sc_free"], seen["sc_free"].value())
                link(nc.vector.tensor_reduce(mxc[:, :], mx[:, :, 0:len(pieces)], AX_X, ALU.max))
                nc.vector.tensor_scalar(nb[:, :], mxc[:, :], -DA_SCALE, None, ALU.mult).then_inc(S["nb"], 1)
                seen["nb"].next()

            def da_turned(g0, g1):
                b = bank_tr()
                wait("tr_hi")
                low(at_lo[:, g0:g1, :], b, at_hi[:, g0:g1, :], (g1 - g0) * P).then_inc(free(b), 1)

            def da_combine(s):
                par = s % 2
                wait("expd", 2)
                link(nc.vector.reciprocal(rec[:, par, :], sums[:, par, :]))
                link(nc.vector.tensor_scalar(cf, sums[:, par, 0:1], neglam, rec[:, par, 1:2],
                                             ALU.mult, ALU.mult))
                nk = META + P * (s % TT + 1)
                z0, z1 = z[:, par, 0, PAD:PAD + nk], z[:, par, 1, PAD:PAD + nk]
                nc.vector.scalar_tensor_tensor(z0, z1, cf, z0, ALU.mult, ALU.add).then_inc(S["a_ready"], 1)

            def da_y(s):
                j, par = s % 4, (s // 4) % 2
                wait("pv_low")
                seen["pv_free"].next()
                y = y_q[:, par, j, :]
                nc.vector.scalar_tensor_tensor(y, psum[:, PV, 0:P], rec[:, s % 2, 0:1],
                                               y_low[:, s % 2, :], ALU.mult, ALU.add)\
                    .then_inc(S["pv_free"], 1)
                dve.wait_ge(S["pv_free"], seen["pv_free"].value())
                link(nc.vector.tensor_tensor_reduce(junk1[:, :], y, y, 1.0, 0.0, ALU.mult, ALU.add,
                                                    ss[:, j:j + 1]))

            def da_norm(s):
                rsqrt(0, 4, P)
                for j in range(4):
                    y = y_q[:, (s // 4) % 2, j, :]
                    last = nc.vector.tensor_scalar(y, y, rs[:, j:j + 1], None, ALU.mult)
                last.then_inc(S["y_ready"], 1)

            def next_slope():
                link(nc.vector.tensor_scalar(bias[:, :], bias[:, :], 0.5, None, ALU.mult))

            def da_step(s, more=True):
                i = s % TT
                blocks = block_groups((s - 1) % TT) if s else []
                da_logits(s)
                for g0, g1 in blocks[:2]:
                    da_turned(g0, g1)
                if s > 1:
                    da_y(s - 2)
                for g0, g1 in blocks[2:]:
                    da_turned(g0, g1)
                if i in (2, 6) and s > 4:
                    bank_tr()
                if more and i in (1, 2, 3):
                    da_values(i - 1, (s // TT + 1) % 2)
                da_combine(s)
                if i % 4 == 1 and s > 1:
                    da_norm(s - 2)
                if more:
                    da_group(i, (s // TT + 1) % 2)
                else:
                    bank_proj()
                if i == TT - 1 and more:
                    next_slope()

            next_slope()
            for g in range(8):
                da_group(g, 0)
                if g in (1, 2, 3):
                    da_values(g - 1, 0)
            for s in range(DA_PEEL):
                da_step(s)
            with seen.loop(dve, 3, DA_TURN):
                for s in range(DA_PEEL, DA_PEEL + 2 * TT):
                    da_step(s)
            for s in range(DA_PEEL + 6 * TT, 8 * TT):
                da_step(s, more=s < 7 * TT)
            for g0, g1 in block_groups(TT - 1):
                da_turned(g0, g1)
            da_y(8 * TT - 2)
            da_y(8 * TT - 1)
            da_norm(8 * TT - 1)
            bank_tr()

            for slot in range(2):
                dve.wait_ge(S[f"y_out{slot}"], 16 * (1 + DA_HEADS))
            for x in (rk_hi, rk_lo):
                for d in range(DKT):
                    nc.vector.memset(x[:, d, 0:PAD].bitcast(F32), 0.0)
            nc.vector.memset(rvt[:, 0:PAD], 0.0).then_inc(S["pads"], 1)

            def ret_values(m, part):
                b = bank_tr()
                wait("tr_hi")
                t0, t1 = KV_TILES[part]
                cols = slice(m * P, (m + 1) * P)
                low(rv_lo[:, t0:t1, cols], b, rv_hi[:, t0:t1, cols], (t1 - t0) * P).then_inc(free(b), 1)

            def ret_low(hi, lo):
                b = bank_proj()
                wait("proj_hi")
                low(lo, b, hi, lo.shape[-1]).then_inc(free(b), 1)

            def ret_keys(head):
                wait("k_hi")
                nc.vector.scalar_tensor_tensor(kt_lo[:, :], psum[:, SK, P:P + RDK], dec[:, P + 1:P + 2],
                                               kt_hi[:, :].bitcast(F32), ALU.mult, ALU.subtract)\
                    .then_inc(S["k_ready"], 1)

            def state_add(first):
                wait("st_full")
                flat = state[:, :, :].rearrange("p d n -> p (d n)")
                src = psum[:, ST:ST + DKT, :].rearrange("p d n -> p (d n)")
                if first:
                    ins = nc.vector.tensor_copy(flat, src)
                else:
                    ins = nc.vector.scalar_tensor_tensor(flat, flat, dec[:, P + 2:P + 3], src,
                                                         ALU.mult, ALU.add)
                seen["st_free"].next()
                ins.then_inc(S["st_free"], 1)

            def state_low():
                wait("s_hi")
                nc.vector.tensor_tensor(s_lo[:, :, :], state[:, :, :], s_hi[:, :, :].bitcast(F32),
                                        ALU.subtract).then_inc(S["s_ready"], 1)

            with seen.loop(dve, RET_HEADS, RET_TURN) as head:
                nc.vector.tensor_copy(dec[:, :], decay[:, head, :]).then_inc(S["dec"], 1)
                seen["dec"].next()
                dve.wait_ge(S["dec"], seen["dec"].value())
                late = []
                for m in range(DVT):
                    for part in range(3):
                        bank_proj()
                        for m1, p1 in late:
                            ret_values(m1, p1)
                        late = [(m, part)]
                for d in range(DKT):
                    for part in range(3):
                        c0, c1 = KV_PARTS[part]
                        ret_low(rk_hi[:, d, PAD + c0:PAD + c1], rk_lo[:, d, PAD + c0:PAD + c1])
                        for m1, p1 in late:
                            ret_values(m1, p1)
                        late = []
                for d in range(DKT):
                    for part in range(2):
                        cols = slice(part * HALF, (part + 1) * HALF)
                        ret_low(rq_hi[:, d, cols], rq_lo[:, d, cols])
                seen["sk_full"].next()
                ret_keys(head)
                state_add(True)
                state_low()
                for c in range(TT):
                    wait("sk_full")
                    nc.vector.tensor_tensor(p_f[:, :], psum[:, SK, 0:P], dec[:, 0:P], ALU.mult)\
                        .then_inc(S["p_mul"], 1)
                    wait("p_hi")
                    nc.vector.tensor_tensor(p_lo[:, :], p_f[:, :], p_hi[:, :].bitcast(F32), ALU.subtract)\
                        .then_inc(S["p_ready"], 1)
                    if c < TT - 1:
                        ret_keys(head)
                    wait("o_full")
                    nc.vector.tensor_scalar(o_n[:, c % 2, :], psum[:, OUT, :], dec[:, P:P + 1], None,
                                            ALU.mult).then_inc(S["o_free"], 1)
                    if c < TT - 1:
                        state_add(False)
                    wait("o_sq")
                    rsqrt(c % 2, c % 2 + 1, RDV)
                    nc.vector.tensor_scalar(diag_o[:, c % 2, :], ident[:, :], rs[:, c % 2:c % 2 + 1], None,
                                            ALU.mult).then_inc(S["o_diag"], 1)
                    if c < TT - 1:
                        state_low()
                    bank_proj()
                    bank_tr()
                dve.wait_ge(S["o_free"], seen["o_free"].next(TT))

            for m in range(KT):
                wait("y_hi")
                nc.vector.tensor_tensor(y_lo[:, m, :], acc[:, m, :], y_hi[:, m, :].bitcast(F32),
                                        ALU.subtract).then_inc(S["y_split"], 1)
            gate_at = {}

            def count_gate(m):
                for half in range(2):
                    b = bank_proj()
                    gate_at[m, half] = (b, seen[f"proj_free{b}"].value())

            count_gate(0)
            count_gate(1)
            dve.wait_ge(S["y_split"], KT)
            for m in range(KT):
                for half in range(2):
                    n, at_n = gate_at[m, half]
                    b = bank_proj()
                    filled("proj_full")
                    dve.wait_ge(S[f"proj_free{n}"], at_n)
                    nc.vector.tensor_tensor(acc[:, m, half * HALF:(half + 1) * HALF], psum[:, b, :],
                                            gate[:, (m % 2) * 2 + half, :], ALU.mult).then_inc(free(b), 1)
                if m + 2 < KT:
                    count_gate(m + 2)
            for _ in range(KT):
                bank_proj()

            def split_ret(n):
                slot = n % 2
                wait("silu")
                nc.vector.tensor_tensor(y_in[:, slot, :], y_in[:, slot, :], g_in[:, slot, :], ALU.mult)\
                    .then_inc(S["y_mul"], 1)
                wait("y_hi")
                nc.vector.tensor_tensor(r_lo[(n // 4) % 3][:, n % 4, :], y_in[:, slot, :],
                                        r_hi[(n // 4) % 3][:, n % 4, :].bitcast(F32), ALU.subtract)\
                    .then_inc(S["y_split"], 1)

            for n in range(DVT):
                split_ret(n)
            dve.wait_ge(S["g_raw"], 2)
            for b in range(2):
                dve.wait_ge(S[f"proj_free{b}"], seen[f"proj_free{b}"].value())

            def ret_add(g):
                m, tok = g // 2, slice((g % 2) * HALF, (g % 2 + 1) * HALF)
                b = bank_proj()
                filled("proj_full")
                dve.wait_ge(free(b), seen[f"proj_free{b}"].value(1))
                link(nc.vector.tensor_tensor(psum[:, b, :], psum[:, b, :], g_ret[:, m, tok], ALU.mult))
                nc.vector.tensor_tensor(acc[:, m, tok], acc[:, m, tok], psum[:, b, :], ALU.add)\
                    .then_inc(free(b), 1)

            for hr in range(RET_HEADS - 1):
                for q in range(4):
                    for g in range(4 * q, 4 * q + 4):
                        ret_add(g)
                    split_ret(4 * hr + 4 + q)

            def merge_low(g):
                m, tok = g // 2, slice((g % 2) * HALF, (g % 2 + 1) * HALF)
                wait("mrg_hi")
                nc.vector.tensor_tensor(m_lo[:, m, tok], acc[:, m, tok], m_hi[:, m, tok].bitcast(F32),
                                        ALU.subtract).then_inc(S["mrg_lo"], 1)

            for g in range(2 * KT):
                ret_add(g)
                if g:
                    merge_low(g - 1)
            merge_low(2 * KT - 1)

            def add_turned(g):
                m, half = g // 2, g % 2
                b = bank_tr()
                filled("tr_full")
                h = h2[:, 4 * half:4 * half + 4, m * P:(m + 1) * P]
                nc.vector.tensor_tensor(h, h, psum[:, b, :].rearrange("p (t n) -> p t n", n=P), ALU.add)\
                    .then_inc(free(b), 1)

            for g in range(2 * KT):
                m, tok = g // 2, slice((g % 2) * HALF, (g % 2 + 1) * HALF)
                b = bank_proj()
                dve.wait_ge(free(b), seen[f"proj_free{b}"].value())
                dve.wait_ge(S[f"xt_in{m % 2}"], 16 * (m // 2 + 1))
                nc.vector.tensor_tensor(h_t[:, b, :], o_st[:, b, :], xt_in[:, m % 2, tok], ALU.add)\
                    .then_inc(S["ht"], 1)
                wait("u2_hi")
                seen["ht"].next()
                nc.vector.scalar_tensor_tensor(y_lo[:, m, tok], h_t[:, b, :], vecs[:, KT + m:KT + m + 1],
                                               y_hi[:, m, tok].bitcast(F32), ALU.mult, ALU.subtract)\
                    .then_inc(S["u2_lo"], 1)
                if g == 1:
                    dve.wait_ge(S["h_in"], 16 * TT)
                if g:
                    add_turned(g - 1)
            add_turned(2 * KT - 1)

            def mlp(first=False, then=None):
                for g in range(2 * FF_BLOCK):
                    b = bank_proj()
                    dve.wait_ge(free(b), seen[f"proj_free{b}"].value())
                    nc.vector.tensor_tensor(f_s[:, b, :], f_r[:, b, :], f_r[:, b, :], ALU.mult)\
                        .then_inc(S["f_sq"], 1)
                    wait("f_hi")
                    seen["f_sq"].next()
                    tok = slice((g % 2) * HALF, (g % 2 + 1) * HALF)
                    nc.vector.tensor_tensor(f_lo[:, g // 2, tok], f_s[:, b, :],
                                            f_hi[:, g // 2, tok].bitcast(F32), ALU.subtract)\
                        .then_inc(S["f_lo"], 1)
                    seen["f_lo"].next()
                if first:
                    dve.wait_ge(S["act"], 9 + TT)
                    link(nc.vector.tensor_scalar(ms[:, 0:TT], ss[:, 0:TT], 1.0 / D, EPS, ALU.mult, ALU.add))
                    link(nc.vector.reciprocal(rs2, ms[:, 0:TT]))
                for tok in range(TT):
                    for half in range(2):
                        b = bank_proj()
                        filled("proj_full")
                        dve.wait_ge(free(b), seen[f"proj_free{b}"].value(1))
                        h = h2[:, tok, half * BANK:(half + 1) * BANK]
                        nc.vector.scalar_tensor_tensor(h, psum[:, b, :], rs2[:, tok:tok + 1], h, ALU.mult,
                                                       ALU.add).then_inc(free(b), 1)
                    if then and tok:
                        then(tok - 1)

            def finish(j):
                if j == 0:
                    dve.wait_ge(S["fin_in"], 16)
                dve.wait_ge(S["act"], 9 + TT + j + 1)
                rsqrt(j, j + 1, D)
                if j >= 2:
                    dve.wait_ge(S[f"out{j % 2}"], 16 * (j // 2))
                nc.vector.scalar_tensor_tensor(out_st[:, j % 2, :], h2[:, j, :], rs[:, j:j + 1],
                                               g_fin[:, :], ALU.mult, ALU.mult).then_inc(S["fin"], 1)

            mlp(first=True)
            with seen.loop(dve, N_BLOCKS - 2, MLP_TURN):
                mlp()
            mlp(then=finish)
            finish(TT - 1)


def feature_tiles(w):
    k, m = w.shape
    return w.reshape(k // P, P, m // P, P).transpose(2, 1, 0, 3).reshape(m // P, P, k)


def weight_stream(w_in, w_da, w_ret, w_out, w_up, w_down):
    tiles = feature_tiles(w_in)
    qa, ka, va, qr, kr, vr, gr, g_a, g_r = 0, 8, 16, 24, 32, 40, 56, 72, 80
    order = []
    for h in range(DA_HEADS):
        order += [va + h, ka + h, qa + h]
    gates = [gr + j for j in range(2 * D // P)] + [g_r + j for j in range(DVT)]
    order += gates[:DVT]
    for h in range(RET_HEADS):
        order += [vr + DVT * h + j for j in range(DVT)]
        order += [kr + DKT * h + j for j in range(DKT)] + [qr + DKT * h + j for j in range(DKT)]
        order += gates[DVT * (h + 1):DVT * (h + 2)]
    da, gate_a = feature_tiles(w_da), tiles[g_a:g_a + KT]
    both = np.concatenate([gate_a[:2], np.stack([da[:-2], gate_a[2:]], axis=1).reshape(-1, P, D), da[-2:]])
    ret = w_ret.reshape(RET_HEADS, DVT, P, 4, 2, P).transpose(0, 3, 2, 4, 1, 5).reshape(16, P, D)
    up, down = feature_tiles(w_up), w_down.reshape(FF // P, P, D)
    both_mlp = {"up": up.reshape(N_BLOCKS, FF_BLOCK, P, D), "down": down.reshape(N_BLOCKS, FF_BLOCK, P, D)}
    mlp = np.stack([both_mlp[kind][:, j] for kind, j in MLP_ORDER], axis=1)
    return np.concatenate([tiles[np.array(order)], both, tiles[g_r + DVT:g_r + KT], ret, feature_tiles(w_out),
                           mlp.reshape(-1, P, D)])


def decay_tables():
    j, i = np.arange(P, dtype=np.float64)[:, None], np.arange(P, dtype=np.float64)[None, :]
    out = np.zeros((P, RET_HEADS, P + 3))
    for h in range(RET_HEADS):
        g = 1.0 - 2.0 ** (-5.0 - h)
        out[:, h, 0:P] = np.where(i >= j, g ** -(j + 1.0), 0.0) * RDK ** -0.5
        out[:, h, P] = g ** (j[:, 0] + 1.0)
        out[:, h, P + 1] = g ** (P - 1.0 - j[:, 0]) * RDK ** -0.5
        out[:, h, P + 2] = g ** P
    return out.astype(np.float32)


def distance_table():
    q, k = np.arange(P)[:, None] + META + SEQ - P, np.arange(L)[None, :]
    return np.where(k <= q, (k - q) / DA_SCALE, -1e30).astype(np.float32)


def kernel(x, meta_tokens, norm_mix_g, w_in, da_lambda_q1, da_lambda_k1, da_lambda_q2, da_lambda_k2,
           da_head_g, w_proj_da, w_proj_ret, w_out, norm_mlp_g, w_up, w_down, final_norm_g):
    import concourse.bacc as bacc
    from concourse.bass_utils import run_bass_kernel_spmd

    np_in = {
        "x": np.asarray(x)[0],
        "xt": np.asarray(x)[0].T.reshape(KT, P, SEQ),
        "meta": np.asarray(meta_tokens),
        "w": weight_stream(np.asarray(w_in)[0], np.asarray(w_proj_da)[0], np.asarray(w_proj_ret)[0],
                           np.asarray(w_out)[0], np.asarray(w_up)[0], np.asarray(w_down)[0]),
        "vecs": np.concatenate([np.asarray(norm_mix_g)[0].reshape(KT, P),
                                np.asarray(norm_mlp_g)[0].reshape(KT, P),
                                np.asarray(da_head_g)[0].reshape(1, P)]).T,
        "lamv": np.broadcast_to(np.stack([np.asarray(v)[0] for v in (
            da_lambda_q1, da_lambda_k1, da_lambda_q2, da_lambda_k2)])[None], (P, 4, DH)),
        "g_fin": np.broadcast_to(np.asarray(final_norm_g)[None], (P, D)),
        "ident": np.eye(P, dtype=np.float32),
        "dist": distance_table(),
        "decay": decay_tables(),
    }
    nc = bacc.Bacc("TRN2", target_bir_lowering=False, num_devices=1)
    arrays, t = {}, {}
    for name, a in np_in.items():
        a = np.ascontiguousarray(a)
        arrays[f"in_{name}"] = a
        t[name] = nc.dram_tensor(f"in_{name}", a.shape, mybir.dt.from_np(a.dtype), kind="ExternalInput").ap()
    t["out"] = nc.dram_tensor("out_0", (1, SEQ, D), F32, kind="ExternalOutput").ap()
    t["yd"] = nc.dram_tensor("y_da_scratch", (DA_HEADS, P, SEQ), F32, kind="Internal").ap()
    t["yr"] = nc.dram_tensor("y_ret_scratch", (RET_HEADS, P, DVT, SEQ), F32, kind="Internal").ap()
    t["gr"] = nc.dram_tensor("gate_scratch", (RET_HEADS + 1, P, DVT, SEQ), F32, kind="Internal").ap()
    build(nc, t)
    r = run_bass_kernel_spmd(nc, [arrays], core_ids=[0])
    return r.results[0]["out_0"]
```

```python
import math
from contextlib import ExitStack, contextmanager

import numpy as np

import concourse.bass as bass
from concourse import mybir

F32 = mybir.dt.float32
F32R = mybir.dt.float32r
I32 = mybir.dt.int32
ALU = mybir.AluOpType
ACT = mybir.ActivationFunctionType
AX_X = mybir.AxisListType.X

P = 128
D = 1024
KT = D // P
META = 16
SEQ = 1024
L = META + SEQ
TT = SEQ // P
PAD = P - META
LP = PAD + L
BANK = 512
HALF = SEQ // 2
EPS = 1e-6
MAP_ORIGIN = 16512
MAP_SIZE = 53200
OUT_SLOTS = 4

DA_HEADS = 8
DH = 64
LAM_INIT = 0.8 - 0.6 * math.exp(-0.3 * 0)
DA_SCALE = DH ** -0.5

MAP_ROWS = [slice(c * DH, (c + 1) * DH) for c in range(2)]

RET_HEADS = 4
RDK = D // RET_HEADS
RDV = 2 * D // RET_HEADS
DKT = RDK // P
DVT = RDV // P

FF = 4 * D
FF_BLOCK = 4
N_BLOCKS = FF // P // FF_BLOCK

KV_PARTS = [(0, META + 3 * P), (META + 3 * P, META + 6 * P), (META + 6 * P, L)]
KV_TILES = [(0, 4), (4, 7), (7, 9)]
Q_PARTS = [(META, META + HALF), (META + HALF, L)]

T_DA = 3 * DA_HEADS
T_RET = DVT + 12 * RET_HEADS
T_BRANCH = 2 * KT + KT // 2 + 4 * RET_HEADS
T_RING = T_DA + T_RET + T_BRANCH + KT
T_ALL = T_RING + N_BLOCKS * 2 * FF_BLOCK
MLP_ORDER = [("up", 0), ("up", 1), ("down", 0), ("down", 1), ("up", 2), ("down", 2), ("up", 3), ("down", 3)]
MLP_FIRST = [("up", 0), ("up", 1), ("down", 0), ("up", 2), ("down", 1), ("up", 3), ("down", 2), ("down", 3)]


class Tally:

    def __init__(self):
        self.n, self.turn, self.per = 0, None, 0

    def next(self, k=1):
        self.n += k
        return self.value()

    def value(self, back=0):
        v = self.n - back
        assert v > 0
        return v if self.turn is None else self.turn * self.per + v

    def value16(self):
        v = 16 * self.n
        assert v > 0
        return v if self.turn is None else self.turn * (16 * self.per) + v


class Tallies:

    def __init__(self):
        self.of = {}

    def __getitem__(self, name):
        return self.of.setdefault(name, Tally())

    @contextmanager
    def loop(self, eng, turns, per):
        before = {}
        with eng.Fori(0, turns) as turn:
            for name in per:
                t = self[name]
                before[name] = t.n
                t.turn, t.per = turn, per[name]
            frozen = {k: t.n for k, t in self.of.items() if k not in per}
            yield turn
            for k, t in self.of.items():
                if k in before:
                    assert t.n - before[k] in (0, per[k]), (k, t.n - before[k], per[k])
                else:
                    assert t.n == frozen.get(k, 0), (k, t.n - frozen.get(k, 0), "missing")
        for name in per:
            t = self[name]
            t.turn = None
            t.n = before[name] + per[name] * turns


FIRST_SUMS = 1 + TT // 2
DA_TURN = {
    "w_split": 6, "w_used": 6, "proj_full": 16, "proj_hi": 10, "proj_free0": 8, "proj_free1": 8,
    "tr_full": 38, "tr_hi": 34, "tr_free0": 19, "tr_free1": 19, "sc_full": 56, "sc_free": 56,
    "nb": 16, "expd": 32, "a_ready": 16, "pv_full": 16, "pv_low": 16, "pv_free": 16,
    "y_ready": 4, "y_out0": 2, "y_out1": 2, "y_sq": 16, "dve": 74,
}
RET_TURN = {
    "w_split": 12, "w_used": 12, "proj_full": 30, "proj_hi": 10, "proj_free0": 15, "proj_free1": 15,
    "tr_full": 20, "tr_hi": 12, "tr_free0": 10, "tr_free1": 10, "sk_full": 9, "k_hi": 8,
    "k_ready": 8, "st_full": 8, "st_free": 8, "s_hi": 8, "s_ready": 8, "p_mul": 8, "p_hi": 8,
    "p_ready": 8, "o_full": 8, "o_sq": 8, "o_free": 8, "o_diag": 8, "ry_out0": 4, "ry_out1": 4,
    "g_out0": 4, "g_out1": 4, "dve": 96, "dec": 1,
}
MLP_TURN = {
    "w_split": 8, "w_used": 8, "proj_full": 24, "proj_free0": 12, "proj_free1": 12,
    "f_sq": 8, "f_hi": 8, "f_lo": 8,
}


SIGNALS = {
    "const_in": "ident, vecs or lamv is in", "table_in": "dist or decay is in",
    "meta_in": "meta tokens are in", **{f"x_in{j}": "token tile j is in" for j in range(TT)},
    "raw_in0": "a weight tile is in", "raw_in1": "",
    "y_out0": "attention output is stored", "y_out1": "", "ry_out0": "retention output is stored",
    "ry_out1": "", "g_out0": "retention gate is stored", "g_out1": "",
    "y_in0": "a branch's tile (or its gate) is back", "y_in1": "", "h_in": "tokens are in h2",
    "fin_in": "the final gain is in",
    **{f"out{j}": "a result tile is stored" for j in range(OUT_SLOTS)},
    "w_hi": "Pool rounded a weight tile", "w_split": "Pool split a weight tile",
    "w_used": "PE is done with a weight tile", "down_used": "PE is done with a block's down rows",
    "proj_full": "PE filled a projection bank", "proj_hi": "ScalarE rounded a projection bank",
    "proj_free0": "a projection bank has been read", "proj_free1": "",
    "tr_full": "PE filled a transpose bank", "tr_hi": "ScalarE rounded a transpose bank",
    "n_full": "PE filled a bank of the first norm", "n_hi": "ScalarE rounded it",
    "n_free": "VectorE read it", "tr_free0": "a transpose bank has been read", "tr_free1": "",
    "pads": "VectorE cleared zero columns", "lam": "lambda's exponents are there",
    "lam_e": "and their exponentials", "diag": "diag(1 / rms) of four token tiles is there",
    "diag_m": "and that of the meta tokens",
    "act": "ScalarE wrote a sum of squares", "dve": "VectorE wrote what it reads next",
    "sc_full": "PE filled a bank of scores", "sc_free": "VectorE read a bank of scores",
    "nb": "minus the rows' maxima are there", "expd": "exponentials and their sum are there",
    "a_ready": "the two maps are combined", "pv_full": "PE summed the values",
    "pv_low": "ScalarE read the low half of that sum", "pv_free": "VectorE read the high half",
    "y_sq": "ScalarE summed an output's squares",
    "y_ready": "four query tiles are normalised",
    "dec": "this head's decay is in `dec`", "sk_full": "PE wrote scores and keys by token",
    "k_hi": "ScalarE rounded the decayed keys", "k_ready": "their rest is there too",
    "st_full": "PE wrote a chunk's k^T v", "st_free": "VectorE added it to the state",
    "s_hi": "ScalarE rounded the state", "s_ready": "its rest is there too",
    "p_mul": "VectorE decayed the scores", "p_hi": "ScalarE rounded them",
    "p_ready": "their rest is there too", "o_full": "PE wrote a chunk's output",
    "o_sq": "ScalarE summed its squares", "o_free": "VectorE copied it",
    "o_diag": "diag(1 / rms) of it is there",
    "yd_in0": "two tiles of attention's output are back", "yd_in1": "", "yd_in2": "", "yd_in3": "",
    "gr_in": "raw gate tiles are back", "g_raw": "their sigmoid is there", "silu": "a gate's silu is there",
    "y_mul": "a retention tile is gated", "y_hi": "ScalarE rounded a branch's tile",
    "y_split": "its rest is there too", "mrg_hi": "ScalarE rounded half a tile of `acc`",
    "mrg_lo": "its rest is there too",
    "xt_in0": "transposed tokens are in", "xt_in1": "", "ht": "VectorE added them to the output's tile",
    "u2_hi": "ScalarE scaled and rounded the sum", "u2_lo": "its rest is there too",
    "f_sq": "VectorE squared the hidden features", "f_hi": "ScalarE rounded them",
    "f_lo": "their rest is there too", "fin": "a result tile is normalised",
}


def key_pieces(i):
    n = META + P * (i + 1)
    size = -(-n // -(-n // BANK) // META) * META
    return [(k, min(k + size, n)) for k in range(0, n, size)]


SC_PERIOD = 2 * 2 * sum(len(key_pieces(i)) for i in range(TT))


def score_bank(n):
    n %= SC_PERIOD
    return n % 3, (1 if n < 2 else 2)


DA_PEEL = TT
NORM_AT, TURN_AT = (2, 3, 4, 5, 6), (6, 7)


def block_groups(i):
    return [(k, min(k + 4, i + 2)) for k in range(0, i + 2, 4)]


def build(nc, t):
    ctx = ExitStack()
    with ctx:
        ctx.enter_context(nc.sbuf_tensor("map", [P, MAP_SIZE], F32))

        def at(name, offset, shape, dtype=F32):
            size = int(np.prod(shape))
            assert offset + size <= MAP_SIZE, (name, offset + size)
            return nc.alloc_sbuf_tensor_at(name, [P, *shape], dtype, offset=MAP_ORIGIN + 4 * offset)

        class Area:
            def __init__(self, start):
                self.at = start

            def take(self, name, shape, dtype=F32):
                here = self.at
                self.at += (int(np.prod(shape)) + 7) // 8 * 8
                return at(name, here, shape, dtype)

        keep = Area(0)
        ident = keep.take("ident", [P])
        ident_r = keep.take("ident_r", [P], F32R)
        vecs = keep.take("vecs", [2 * KT + 1])
        lamv = keep.take("lamv", [4, DH])
        small = keep.take("small", [96])
        decay = keep.take("decay", [RET_HEADS, P + 3])
        dec = keep.take("dec", [P + 3])
        raw = keep.take("raw", [2, D])
        w_hi = keep.take("w_hi", [2, D], F32R)
        w_lo = keep.take("w_lo", [2, D], F32R)
        u_at = keep.at
        u_hi = keep.take("u_hi", [KT, L], F32R)
        u_lo = keep.take("u_lo", [KT, L], F32R)
        work = keep.at

        ss = small[:, 0:9]
        rs = small[:, 9:18]
        ms = small[:, 18:27]
        nt = small[:, 27:36]
        mx = small[:, 36:42].rearrange("p (c j) -> p c j", c=2)
        mxc = small[:, 42:44]
        nb = small[:, 44:46]
        sums = small[:, 46:50].rearrange("p (b c) -> p b c", b=2)
        rec = small[:, 50:54].rearrange("p (b c) -> p b c", b=2)
        cf = small[:, 54:55]
        lam = small[:, 55:61]
        neglam = small[:, 61:62]
        g_head = small[:, 62:63]
        rs2 = small[:, 64:64 + TT]

        g_st = at("g_st", MAP_SIZE - 2 * BANK, [2, BANK])

        a = Area(work)
        x_in = a.take("x_in", [TT, D])
        x_meta = a.take("x_meta", [D])
        junk0 = a.take("junk0", [D])
        diag0 = a.take("diag0", [TT, P])
        diag_m = a.take("diag_m", [P])
        junk_v = a.take("junk_v", [D])

        a = Area(work)
        qs = a.take("qs", [2, 2, SEQ], F32R)
        ks = a.take("ks", [2, 2, L], F32R)
        k_lo = a.take("k_lo", [2, L], F32R)
        v_da = a.take("v_da", [2, 9, 2, P], F32R)
        at_hi = a.take("at_hi", [9, P], F32R)
        at_lo = a.take("at_lo", [9, P], F32R)
        z = a.take("z", [2, 2, LP])
        bias = a.take("bias", [L])
        vt = a.take("vt", [LP])
        y_low = a.take("y_low", [2, P])
        y_q = a.take("y_q", [2, TT, P])
        y_st = a.take("y_st", [2, BANK])
        junk1 = a.take("junk1", [P])

        a = Area(work)
        rq_hi = a.take("rq_hi", [DKT, SEQ], F32R)
        rq_lo = a.take("rq_lo", [DKT, SEQ], F32R)
        rk_hi = a.take("rk_hi", [DKT, LP], F32R)
        rk_lo = a.take("rk_lo", [DKT, LP], F32R)
        rv_hi = a.take("rv_hi", [9, RDV], F32R)
        rv_lo = a.take("rv_lo", [9, RDV], F32R)
        kt_hi = a.take("kt_hi", [RDK], F32R)
        kt_lo = a.take("kt_lo", [RDK], F32R)
        s_hi = a.take("s_hi", [DKT, RDV], F32R)
        s_lo = a.take("s_lo", [DKT, RDV], F32R)
        p_hi = a.take("p_hi", [P], F32R)
        p_lo = a.take("p_lo", [P], F32R)
        state = a.take("state", [DKT, RDV])
        p_f = a.take("p_f", [P])
        rvt = a.take("rvt", [LP])
        o_n = a.take("o_n", [2, RDV])
        diag_o = a.take("diag_o", [2, P])
        a.at = work + 3 * KT * SEQ
        ry_st = a.take("ry_st", [2, DVT, P])
        junk3 = a.take("junk3", [RDV])

        a = Area(work)
        y_hi = a.take("y_hi", [KT, SEQ], F32R)
        y_lo = a.take("y_lo", [KT, SEQ], F32R)
        acc = a.take("acc", [KT, SEQ])
        y_in = a.take("y_in", [2, SEQ])
        g_in = a.take("g_in", [2, SEQ])
        gate = at("gate", a.at - 2 * SEQ, [4, BANK])
        g_ret = at("g_ret", work, [KT, SEQ])
        r_at = [work + KT * SEQ, u_at, u_at + KT * SEQ]
        r_hi = [at(f"r_hi{n}", r_at[n], [DVT, SEQ], F32R) for n in range(3)]
        r_lo = [at(f"r_lo{n}", r_at[n] + DVT * SEQ, [DVT, SEQ], F32R) for n in range(3)]
        m_hi = at("m_hi", u_at, [KT, SEQ], F32R)
        m_lo = at("m_lo", u_at + KT * SEQ, [KT, SEQ], F32R)

        h2 = at("h2", work + 2 * KT * SEQ, [TT, D])
        xt_in = at("xt_in", work + 3 * KT * SEQ, [2, SEQ])
        o_st = at("o_st", a.at - 2 * SEQ, [2, BANK])
        h_t = at("h_t", a.at - SEQ, [2, BANK])

        f_hi = at("f_hi", u_at, [FF_BLOCK, SEQ], F32R)
        f_lo = at("f_lo", u_at + 4096, [FF_BLOCK, SEQ], F32R)
        wd_hi = at("wd_hi", u_at + 8192, [FF_BLOCK, D], F32R)
        wd_lo = at("wd_lo", u_at + 8192 + 4096, [FF_BLOCK, D], F32R)
        f_r = at("f_r", work + 3 * KT * SEQ, [2, BANK])
        f_s = at("f_s", work + 3 * KT * SEQ + SEQ, [2, BANK])
        junk5 = at("junk5", a.at - SEQ, [D])
        g_fin = at("g_fin", work, [D])
        out_st = at("out_st", work + D, [OUT_SLOTS, D])

        psum = ctx.enter_context(nc.psum_tensor("psum", [P, 8, BANK], F32))
        PROJ, TR, SC, PV = 0, 2, 4, 7
        SK, ST, OUT = 4, 5, 7

        S = {name: ctx.enter_context(nc.semaphore(name)) for name in SIGNALS}
        block = ctx.enter_context(nc.Block())

        @block.sync
        def _(sp):
            sp.wait_ge(S["x_in3"], 16)
            for i in range(2):
                sp.dma_start(raw[:, i, :], t["w"][i]).then_inc(S[f"raw_in{i}"], 16)
            with sp.Fori(1, T_ALL // 2) as pair:
                for i in range(2):
                    sp.wait_ge(S["w_split"], pair * 2 + i - 1)
                    sp.dma_start(raw[:, i, :], t["w"][pair * 2 + i]).then_inc(S[f"raw_in{i}"], 16)

        @block.gpsimd
        def _(pool):
            def split(slot, landed, n, hi, lo, apart=True):
                pool.wait_ge(S[f"raw_in{slot}"], landed)
                if apart:
                    pool.nop(nofuse=True)
                nc.gpsimd.tensor_copy(hi, raw[:, slot, :]).then_inc(S["w_hi"], 1)
                pool.wait_ge(S["w_hi"], n)
                nc.gpsimd.tensor_tensor(lo, raw[:, slot, :], hi.bitcast(F32), ALU.subtract)\
                    .then_inc(S["w_split"], 1)

            for i in range(2):
                split(i, 16, i + 1, w_hi[:, i, :], w_lo[:, i, :], apart=False)
            with pool.Fori(1, T_RING // 2) as pair:
                for i in range(2):
                    pool.wait_ge(S["w_used"], pair * 2 + i - 1)
                    split(i, pair * 16 + 16, pair * 2 + i + 1, w_hi[:, i, :], w_lo[:, i, :])

            def mlp_block(b):
                for n, (kind, j) in enumerate(MLP_FIRST if isinstance(b, int) else MLP_ORDER):
                    if kind == "up":
                        hi, lo = w_hi[:, j % 2, :], w_lo[:, j % 2, :]
                        pool.wait_ge(S["w_used"], b * FF_BLOCK + (T_RING + j - 1))
                    else:
                        hi, lo = wd_hi[:, j, :], wd_lo[:, j, :]
                        if isinstance(b, int):
                            pool.wait_ge(S["w_used"], T_RING)
                        else:
                            pool.wait_ge(S["down_used"], b)
                    split(n % 2, b * 64 + 16 * ((T_RING + n) // 2 + 1), b * 8 + (T_RING + n + 1), hi, lo,
                          apart=not isinstance(b, int))

            mlp_block(0)
            with pool.Fori(1, N_BLOCKS) as b:
                mlp_block(b)

        @block.tensor
        def _(pe):
            seen = Tallies()
            turn = [0, 0, 0]

            def product(out, st_hi, st_lo, mv_hi, mv_lo, first, last):
                nc.tensor.matmul(out, st_hi, mv_hi, start=first, stop=False)
                nc.tensor.matmul(out, st_hi, mv_lo, start=False, stop=False)
                return nc.tensor.matmul(out, st_lo, mv_hi, start=False, stop=last)

            def next_weights():
                pe.wait_ge(S["w_split"], seen["w_split"].next())

            def take_proj():
                b = turn[0] % 2
                turn[0] += 1
                free = seen[f"proj_free{b}"]
                if free.n:
                    pe.wait_ge(S[f"proj_free{b}"], free.value())
                free.next()
                return PROJ + b

            def take_tr():
                b = turn[1] % 2
                turn[1] += 1
                free = seen[f"tr_free{b}"]
                if free.n:
                    pe.wait_ge(S[f"tr_free{b}"], free.value())
                free.next()
                return TR + b

            def project(slot, mv_h, mv_l, part, first_use, between=None, at=KT // 2):
                c0, c1 = part
                b = take_proj()
                for k in range(KT):
                    if between and k == at:
                        between()
                    cols = slice(k * P, (k + 1) * P)
                    mm = nc.tensor.matmul(psum[:, b, 0:c1 - c0], w_hi[:, slot, cols], mv_h[:, k, c0:c1],
                                          start=k == 0, stop=False)
                    if first_use and k == 0:
                        mm.then_inc(S[first_use], 1)
                    nc.tensor.matmul(psum[:, b, 0:c1 - c0], w_hi[:, slot, cols], mv_l[:, k, c0:c1],
                                     start=False, stop=False)
                    mm = nc.tensor.matmul(psum[:, b, 0:c1 - c0], w_lo[:, slot, cols], mv_h[:, k, c0:c1],
                                          start=False, stop=k == KT - 1)
                mm.then_inc(S["proj_full"], 1)

            def all_free(name):
                for b in range(2):
                    pe.wait_ge(S[f"{name}{b}"], seen[f"{name}{b}"].value())

            groups = 0

            def norm_bank():
                nonlocal groups
                if groups >= 4:
                    pe.wait_ge(S["n_free"], groups - 3)
                groups += 1
                return TR + (groups - 1) % 4

            for part in range(2):
                pe.wait_ge(S["diag"], part + 1)
                for m in range(KT):
                    b = norm_bank()
                    for j in range(4):
                        mm = nc.tensor.matmul(psum[:, b, j * P:(j + 1) * P],
                                              x_in[:, 4 * part + j, m * P:(m + 1) * P],
                                              diag0[:, 4 * part + j, :], start=True, stop=True)
                    mm.then_inc(S["n_full"], 1)
                if part == 0:
                    pe.wait_ge(S["diag_m"], 1)
                    b = norm_bank()
                    for m in range(KT):
                        mm = nc.tensor.matmul(psum[:, b, m * META:(m + 1) * META],
                                              x_meta[0:META, m * P:(m + 1) * P],
                                              diag_m[0:META, 0:META], start=True, stop=True)
                    mm.then_inc(S["n_full"], 1)
            pe.wait_ge(S["n_free"], KT + 1)

            tile = [0]

            def da_group(g, between=None):
                if g in (0, 3, 6):
                    next_weights()
                    tile[0] += 1
                first = "w_used" if g in (0, 3, 6) and tile[0] > 1 else None
                part = KV_PARTS[g % 3] if g < 6 else Q_PARTS[g - 6]
                project((tile[0] - 1) % 2, u_hi, u_lo, part, first, between)

            def da_values(part):
                last = (turn[0] - 2) % 2
                pe.wait_ge(S[f"proj_free{last}"], seen[f"proj_free{last}"].value())
                b = take_tr()
                for j, tok in enumerate(range(*KV_TILES[part])):
                    mm = nc.tensor.transpose(psum[:, b, j * P:(j + 1) * P],
                                             vt[:, tok * P:(tok + 1) * P], ident[:, :])
                mm.then_inc(S["tr_full"], 1)

            def da_scores(s):
                i, p = s % TT, (s // TT) % 2
                if i == 0:
                    pe.wait_ge(S["proj_free0"], seen["proj_free0"].value())
                for c in range(2):
                    rows = MAP_ROWS[c]
                    q = slice(i * P, (i + 1) * P)
                    for k0, k1 in key_pieces(i):
                        bank, back = score_bank(turn[2])
                        turn[2] += 1
                        free = seen["sc_free"]
                        if free.n > back:
                            pe.wait_ge(S["sc_free"], free.value(back))
                        free.next()
                        out = psum[:, SC + bank, 0:k1 - k0]
                        nc.tensor.matmul(out, qs[:, p, c, q], ks[:, p, c, k0:k1], start=True, stop=False)
                        nc.tensor.matmul(out, qs[rows, p, c, q], k_lo[rows, p, k0:k1],
                                         start=False, stop=True).then_inc(S["sc_full"], 1)

            def da_turn_probs(s, g0, g1):
                b = take_tr()
                for j in range(g0, g1):
                    mm = nc.tensor.transpose(psum[:, b, (j - g0) * P:(j - g0 + 1) * P],
                                             z[:, s % 2, 0, j * P:(j + 1) * P], ident[:, :])
                mm.then_inc(S["tr_full"], 1)

            def da_turn_y(head, half):
                pe.wait_ge(S["y_ready"], seen["y_ready"].next())
                b = take_tr()
                for j in range(4):
                    mm = nc.tensor.transpose(psum[:, b, j * P:(j + 1) * P],
                                             y_q[:, head % 2, 4 * half + j, :], ident[:, :])
                mm.then_inc(S["tr_full"], 1)

            def da_values_sum(s):
                p, i = (s // TT) % 2, s % TT
                all_free("tr_free")
                free = seen["pv_free"]
                if free.n:
                    pe.wait_ge(S["pv_free"], free.value())
                free.next()
                for j in range(i + 2):
                    nc.tensor.matmul(psum[:, PV, 0:2 * P], at_hi[:, j, :], v_da[:, p, j, :, :],
                                     start=j == 0, stop=False)
                    mm = nc.tensor.matmul(psum[:, PV, 0:P], at_lo[:, j, :], v_da[:, p, j, 0, :],
                                          start=False, stop=j == i + 1)
                mm.then_inc(S["pv_full"], 1)

            def ret_gate(m, half, between=None):
                if half == 0:
                    next_weights()
                project(m % 2, u_hi, u_lo, Q_PARTS[half], None if half else "w_used", between)

            def da_step(s, more=True):
                i = s % TT
                da_scores(s)
                blocks = block_groups((s - 1) % TT) if s else []
                if s:
                    pe.wait_ge(S["a_ready"], seen["a_ready"].next())
                for g0, g1 in blocks[:2]:
                    da_turn_probs(s - 1, g0, g1)

                def middle():
                    for g0, g1 in blocks[2:]:
                        da_turn_probs(s - 1, g0, g1)
                    if i in TURN_AT and s > TT:
                        da_turn_y(s // TT - 1, TURN_AT.index(i))
                    if more and i in (1, 2, 3):
                        da_values(i - 1)

                if more:
                    da_group(i, middle)
                elif i < TT - 1:
                    ret_gate(i // 2, i % 2, middle)
                else:
                    middle()
                if s:
                    da_values_sum(s - 1)

            for g in range(8):
                if g == 1:
                    pe.wait_ge(S["n_free"], groups)
                    pe.wait_ge(S["pads"], 2)
                da_group(g)
                if g in (1, 2, 3):
                    da_values(g - 1)
            for s in range(DA_PEEL):
                da_step(s)
            with seen.loop(pe, 3, DA_TURN):
                for s in range(DA_PEEL, DA_PEEL + 2 * TT):
                    da_step(s)
            for s in range(DA_PEEL + 6 * TT, 8 * TT):
                da_step(s, more=s < 7 * TT)
            pe.wait_ge(S["a_ready"], seen["a_ready"].next())
            for n, (g0, g1) in enumerate(block_groups(TT - 1)):
                da_turn_probs(8 * TT - 1, g0, g1)
            da_values_sum(8 * TT - 1)
            ret_gate(DVT - 1, 1)
            for half in range(2):
                da_turn_y(DA_HEADS - 1, half)

            def ret_values(m, part):
                last = (turn[0] - 2) % 2
                pe.wait_ge(S[f"proj_free{last}"], seen[f"proj_free{last}"].value())
                b = take_tr()
                for j, tok in enumerate(range(*KV_TILES[part])):
                    mm = nc.tensor.transpose(psum[:, b, j * P:(j + 1) * P],
                                             rvt[:, tok * P:(tok + 1) * P], ident[:, :])
                mm.then_inc(S["tr_full"], 1)

            def ret_turn_y(c):
                pe.wait_ge(S["o_diag"], seen["o_diag"].next())
                b = take_tr()
                for j in range(DVT):
                    mm = nc.tensor.matmul(psum[:, b, j * P:(j + 1) * P], o_n[:, c % 2, j * P:(j + 1) * P],
                                          diag_o[:, c % 2, :], start=True, stop=True)
                mm.then_inc(S["tr_full"], 1)

            def ret_scores(c):
                cols = slice((c + 1) * P, (c + 2) * P)
                if seen["k_ready"].n:
                    pe.wait_ge(S["k_ready"], seen["k_ready"].value())
                if c >= 0:
                    q = slice(c * P, (c + 1) * P)
                    for d in range(DKT):
                        mm = product(psum[:, SK, 0:P], rk_hi[:, d, cols], rk_lo[:, d, cols],
                                     rq_hi[:, d, q], rq_lo[:, d, q], d == 0, d == DKT - 1)
                if c < TT - 1:
                    for d in range(DKT):
                        out = psum[:, SK, (d + 1) * P:(d + 2) * P]
                        nc.tensor.matmul(out, rk_hi[:, d, cols], ident_r[:, :], start=True, stop=False)
                        mm = nc.tensor.matmul(out, rk_lo[:, d, cols], ident_r[:, :], start=False, stop=True)
                mm.then_inc(S["sk_full"], 1)

            def ret_state(c):
                pe.wait_ge(S["k_ready"], seen["k_ready"].next())
                if seen["st_free"].n:
                    pe.wait_ge(S["st_free"], seen["st_free"].value())
                seen["st_free"].next()
                for d in range(DKT):
                    cols = slice(d * P, (d + 1) * P)
                    mm = product(psum[:, ST + d, :], kt_hi[:, cols], kt_lo[:, cols],
                                 rv_hi[:, c + 1, :], rv_lo[:, c + 1, :], True, True)
                mm.then_inc(S["st_full"], 1)

            def ret_out(c):
                q = slice(c * P, (c + 1) * P)
                if seen["o_free"].n:
                    pe.wait_ge(S["o_free"], seen["o_free"].value())
                seen["o_free"].next()
                pe.wait_ge(S["s_ready"], seen["s_ready"].next())
                for d in range(DKT):
                    product(psum[:, OUT, :], rq_hi[:, d, q], rq_lo[:, d, q], s_hi[:, d, :],
                            s_lo[:, d, :], d == 0, False)
                pe.wait_ge(S["p_ready"], seen["p_ready"].next())
                product(psum[:, OUT, :], p_hi[:, :], p_lo[:, :], rv_hi[:, c + 1, :],
                        rv_lo[:, c + 1, :], False, True).then_inc(S["o_full"], 1)

            with seen.loop(pe, RET_HEADS, RET_TURN):
                late = []
                for m in range(DVT):
                    next_weights()
                    for part in range(3):
                        project(m % 2, u_hi, u_lo, KV_PARTS[part], "w_used" if part == 0 else None)
                        if (m, part) == (0, 1):
                            pe.wait_ge(S["pads"], 3)
                        for m1, p1 in late:
                            ret_values(m1, p1)
                        late = [(m, part)]
                for d in range(DKT):
                    next_weights()
                    for part in range(3):
                        project(d % 2, u_hi, u_lo, KV_PARTS[part], "w_used" if part == 0 else None)
                        for m1, p1 in late:
                            ret_values(m1, p1)
                        late = []
                next_weights()
                for part in range(2):
                    project(0, u_hi, u_lo, Q_PARTS[part], None if part else "w_used")
                ret_scores(-1)
                next_weights()
                project(1, u_hi, u_lo, Q_PARTS[0], "w_used")
                all_free("tr_free")
                ret_state(-1)
                project(1, u_hi, u_lo, Q_PARTS[1], None)
                all_free("proj_free")
                for c in range(TT):
                    ret_scores(c)

                    def middle(c=c):
                        ret_out(c)
                        if c < TT - 1:
                            ret_state(c)

                    ret_gate(c // 2, c % 2, middle)
                    if c:
                        ret_turn_y(c - 1)
                ret_turn_y(TT - 1)

            def operand_ready(n):
                pe.wait_ge(S["y_split"], seen["y_split"].next(n))

            HALVES = [(0, HALF), (HALF, SEQ)]

            def gate_tile(slot):
                next_weights()
                for half in range(2):
                    project(slot, u_hi, u_lo, Q_PARTS[half], None if half else "w_used")

            def da_tile(slot):
                next_weights()
                for half in range(2):
                    project(slot, y_hi, y_lo, HALVES[half], None if half else "w_used")

            gate_tile(0)
            gate_tile(1)
            operand_ready(KT)
            pair_turn = {"w_split": 2, "w_used": 2, "proj_free0": 2, "proj_free1": 2}
            with seen.loop(pe, KT - 2, pair_turn):
                da_tile(0)
                gate_tile(1)
            da_tile(0)
            da_tile(1)
            with seen.loop(pe, KT // 4, pair_turn):
                gate_tile(0)
                gate_tile(1)
            for hr in range(RET_HEADS):
                operand_ready(DVT)
                hi, lo = r_hi[hr % 3], r_lo[hr % 3]
                for mp in range(4):
                    next_weights()
                    slot = mp % 2
                    for m2 in range(2):
                        for half in range(2):
                            b = take_proj()
                            tok = slice(half * HALF, (half + 1) * HALF)
                            for k in range(DVT):
                                cols = slice((m2 * DVT + k) * P, (m2 * DVT + k + 1) * P)
                                mm = nc.tensor.matmul(psum[:, b, :], w_hi[:, slot, cols], hi[:, k, tok],
                                                      start=k == 0, stop=False)
                                if (m2, half, k) == (0, 0, 0):
                                    mm.then_inc(S["w_used"], 1)
                                nc.tensor.matmul(psum[:, b, :], w_hi[:, slot, cols], lo[:, k, tok],
                                                 start=False, stop=False)
                                mm = nc.tensor.matmul(psum[:, b, :], w_lo[:, slot, cols], hi[:, k, tok],
                                                      start=False, stop=k == DVT - 1)
                            mm.then_inc(S["proj_full"], 1)

            def turn_o():
                b = turn[0] % 2
                pe.wait_ge(S[f"proj_free{b}"], seen[f"proj_free{b}"].value())
                out = take_tr()
                for j in range(4):
                    mm = nc.tensor.transpose(psum[:, out, j * P:(j + 1) * P],
                                             o_st[:, b, j * P:(j + 1) * P], ident[:, :])
                mm.then_inc(S["tr_full"], 1)

            def until(name, count):
                return lambda: pe.wait_ge(S[name], count)

            for m in range(KT):
                next_weights()
                for half in range(2):
                    last_tile = None
                    if m == 0:
                        pe.wait_ge(S["mrg_lo"], 2 * KT - 3 + half)
                        last_tile = until("mrg_lo", 2 * KT - 1 + half)
                    project(m % 2, m_hi, m_lo, HALVES[half], None if half else "w_used", last_tile, KT - 1)
                    if m or half:
                        turn_o()

            def mlp(first):
                order = MLP_FIRST if first else MLP_ORDER
                split = 0
                for j in range(FF_BLOCK):
                    at = order.index(("up", j)) + 1
                    pe.wait_ge(S["w_split"], seen["w_split"].next(at - split))
                    split = at
                    before = "w_used" if first or j else "down_used"
                    for half in range(2):
                        last_tile = None
                        if first and j == 0:
                            pe.wait_ge(S["u2_lo"], 2 * KT - 3 + half)
                            last_tile = until("u2_lo", 2 * KT - 1 + half)
                        project(j % 2, y_hi, y_lo, HALVES[half], None if half else before, last_tile,
                                KT - 1)
                        if first and j == half == 0:
                            turn_o()
                def down(b, tok, half, ks):
                    out = slice(half * BANK, (half + 1) * BANK)
                    st = slice(tok * P, (tok + 1) * P)
                    for k in ks:
                        mm = nc.tensor.matmul(psum[:, b, :], f_hi[:, k, st], wd_hi[:, k, out],
                                              start=k == 0, stop=False)
                        if (tok, half, k) == (0, 0, 0):
                            mm.then_inc(S["w_used"], 1)
                        nc.tensor.matmul(psum[:, b, :], f_hi[:, k, st], wd_lo[:, k, out],
                                         start=False, stop=False)
                        mm = nc.tensor.matmul(psum[:, b, :], f_lo[:, k, st], wd_hi[:, k, out],
                                              start=False, stop=k == FF_BLOCK - 1)
                    return mm

                pe.wait_ge(S["w_split"], seen["w_split"].next(len(order) - split))
                pe.wait_ge(S["f_lo"], seen["f_lo"].next(2 * (FF_BLOCK - 1)))
                banks = []
                for half in range(2):
                    banks.append(take_proj())
                    down(banks[half], 0, half, range(FF_BLOCK - 1))
                pe.wait_ge(S["f_lo"], seen["f_lo"].next(2))
                for half in range(2):
                    down(banks[half], 0, half, [FF_BLOCK - 1]).then_inc(S["proj_full"], 1)
                for tok in range(1, TT):
                    for half in range(2):
                        down(take_proj(), tok, half, range(FF_BLOCK)).then_inc(S["proj_full"], 1)

            mlp(True)
            with seen.loop(pe, N_BLOCKS - 2, MLP_TURN):
                mlp(False)
            mlp(False)

        @block.scalar
        def _(act):
            seen = Tallies()
            turn = [0, 0]

            def wait(name, k=1):
                act.wait_ge(S[name], seen[name].next(k))

            def bank_proj():
                b = turn[0] % 2
                turn[0] += 1
                seen["proj_full"].next()
                seen[f"proj_free{b}"].next()
                return PROJ + b

            def bank_tr():
                b = turn[1] % 2
                turn[1] += 1
                seen["tr_full"].next()
                seen[f"tr_free{b}"].next()
                return TR + b

            def filled(name):
                act.wait_ge(S[name], seen[name].value())

            def free(b):
                return S[f"proj_free{b}" if b < TR else f"tr_free{b - TR}"]

            def step(ins):
                ins.then_inc(S["act"], 1)
                seen["act"].next()

            def settle():
                act.wait_ge(S["act"], seen["act"].value())

            for name in ("y_out0", "y_out1", "ry_out0", "ry_out1"):
                act.sem_inc(S[name], 16)
                seen[name].n = 1
            for dst, src in ((lamv[:, :, :], t["lamv"]), (vecs[:, :], t["vecs"]), (ident[:, :], t["ident"])):
                act.dma_start(dst, src).then_inc(S["const_in"], 16)
            act.dma_start(x_meta[0:META, :], t["meta"]).then_inc(S["meta_in"], 16)
            for j in range(TT):
                act.dma_start(x_in[:, j, :], t["x"][j * P:(j + 1) * P, :]).then_inc(S[f"x_in{j}"], 16)
            for dst, src in ((bias[:, :], t["dist"]), (decay[:, :, :], t["decay"])):
                act.dma_start(dst, src).then_inc(S["table_in"], 16)

            act.wait_ge(S["lam"], 1)
            nc.scalar.activation(lam[:, 2:4], lam[:, 0:2], ACT.Exp).then_inc(S["lam_e"], 1)
            act.wait_ge(S["meta_in"], 16)
            step(nc.scalar.activation(junk0[0:META, :], x_meta[0:META, :], ACT.Square,
                                      accum_out=ss[0:META, 0:1]))

            def square(j):
                act.wait_ge(S[f"x_in{j}"], 16)
                settle()
                step(nc.scalar.activation(junk0[:, :], x_in[:, j, :], ACT.Square,
                                          accum_out=ss[:, j + 1:j + 2]))

            groups = 0

            def norm_turned(part, m):
                nonlocal groups
                groups += 1
                c0 = META + part * BANK
                act.wait_ge(S["n_full"], groups)
                nc.scalar.activation(u_hi[:, m, c0:c0 + BANK], psum[:, TR + (groups - 1) % 4, :], ACT.Copy,
                                     scale=vecs[:, m:m + 1]).then_inc(S["n_hi"], 1)

            square(0)
            square(2)
            for m in range(KT):
                norm_turned(0, m)
                if m in (0, 2):
                    square(m + 4)
            groups += 1
            act.wait_ge(S["n_full"], groups)
            for m in range(KT):
                last = nc.scalar.activation(u_hi[:, m, 0:META],
                                            psum[:, TR + (groups - 1) % 4, m * META:(m + 1) * META],
                                            ACT.Copy, scale=vecs[:, m:m + 1])
            last.then_inc(S["n_hi"], 1)
            for m in range(KT):
                norm_turned(1, m)

            def da_group(g, p):
                b = bank_proj()
                filled("proj_full")
                if g < 3:
                    c0, c1 = KV_PARTS[g]
                    nc.scalar.activation(vt[:, PAD + c0:PAD + c1], psum[:, b, 0:c1 - c0], ACT.Copy)\
                        .then_inc(free(b), 1)
                else:
                    c0, c1 = KV_PARTS[g - 3] if g < 6 else ((g - 6) * HALF, (g - 5) * HALF)
                    dst = ks if g < 6 else qs
                    for c in range(2):
                        src = psum[MAP_ROWS[c], b, 0:c1 - c0]
                        last = nc.scalar.activation(dst[MAP_ROWS[c], p, c, c0:c1], src, ACT.Copy)
                        if g < 6:
                            last = nc.scalar.activation(dst[MAP_ROWS[1 - c], p, c, c0:c1], src, ACT.Copy)
                    last.then_inc(S["proj_hi"], 1)

            def da_values(part, p):
                b = bank_tr()
                filled("tr_full")
                t0, t1 = KV_TILES[part]
                nc.scalar.activation(v_da[:, p, t0:t1, 0, :],
                                     psum[:, b, 0:(t1 - t0) * P].rearrange("p (t n) -> p t n", n=P),
                                     ACT.Copy).then_inc(S["tr_hi"], 1)

            def da_turned(g0, g1):
                b = bank_tr()
                filled("tr_full")
                nc.scalar.activation(at_hi[:, g0:g1, :],
                                     psum[:, b, 0:(g1 - g0) * P].rearrange("p (t n) -> p t n", n=P),
                                     ACT.Copy).then_inc(S["tr_hi"], 1)

            stores = [0]

            def da_y(head, half):
                b = bank_tr()
                filled("tr_full")
                slot = stores[0] % 2
                stores[0] += 1
                out = seen[f"y_out{slot}"]
                act.wait_ge(S[f"y_out{slot}"], out.value16())
                sem_b = free(b)
                nc.scalar.activation(y_st[:, slot, :], psum[:, b, :], ACT.Copy, scale=g_head)\
                    .then_inc(sem_b, 1)
                act.wait_ge(sem_b, seen[f"tr_free{b - TR}"].value())
                out.next()
                act.dma_start(t["yd"][head, :, half * HALF:(half + 1) * HALF], y_st[:, slot, :])\
                    .then_inc(S[f"y_out{slot}"], 16)

            def da_exp(s):
                wait("nb")
                nk = META + P * (s % TT + 1)
                for c in range(2):
                    zc = z[:, s % 2, c, PAD:PAD + nk]
                    nc.scalar.activation(zc, zc, ACT.Exp, bias=nb[:, c:c + 1], scale=DA_SCALE,
                                         accum_out=sums[:, s % 2, c:c + 1]).then_inc(S["expd"], 1)

            def da_low(s):
                wait("pv_full")
                nc.scalar.activation(y_low[:, s % 2, :], psum[:, PV, P:2 * P], ACT.Copy,
                                     scale=rec[:, s % 2, 0:1]).then_inc(S["pv_low"], 1)

            def da_square(s):
                wait("pv_free")
                nc.scalar.activation(junk1[:, :], y_q[:, (s // TT) % 2, s % TT, :], ACT.Square,
                                     accum_out=ss[:, s % TT:s % TT + 1]).then_inc(S["y_sq"], 1)

            def da_step(s, head, more=True):
                i = s % TT
                blocks = block_groups((s - 1) % TT) if s else []
                for g0, g1 in blocks[:2]:
                    da_turned(g0, g1)
                if s > 1:
                    da_low(s - 2)
                da_exp(s)
                if s > 1:
                    da_square(s - 2)
                for g0, g1 in blocks[2:]:
                    da_turned(g0, g1)
                if i in TURN_AT and s > TT:
                    da_y(head - 1, TURN_AT.index(i))
                if more and i in (1, 2, 3):
                    da_values(i - 1, (s // TT + 1) % 2)
                if more:
                    da_group(i, (s // TT + 1) % 2)
                elif i < TT - 1:
                    raw_gate(0, i // 2, i % 2)

            def raw_gate(head, m, half):
                b = bank_proj()
                filled("proj_full")
                out = seen[f"g_out{half}"]
                if out.n:
                    act.wait_ge(S[f"g_out{half}"], out.value16())
                out.next()
                nc.scalar.activation(g_st[:, half, :], psum[:, b, :], ACT.Copy).then_inc(free(b), 1)
                act.wait_ge(free(b), seen[f"proj_free{b}"].value())
                act.dma_start(t["gr"][head, :, m, half * HALF:(half + 1) * HALF], g_st[:, half, :])\
                    .then_inc(S[f"g_out{half}"], 16)

            for g in range(8):
                da_group(g, 0)
                if g in (1, 2, 3):
                    da_values(g - 1, 0)
            for s in range(DA_PEEL):
                da_step(s, 0)
            with seen.loop(act, 3, DA_TURN) as pair:
                for s in range(DA_PEEL, DA_PEEL + 2 * TT):
                    da_step(s, pair * 2 + s // TT)
            for s in range(DA_PEEL + 6 * TT, 8 * TT):
                da_step(s, s // TT, more=s < 7 * TT)
            for g0, g1 in block_groups(TT - 1):
                da_turned(g0, g1)
            da_low(8 * TT - 2)
            da_square(8 * TT - 2)
            da_low(8 * TT - 1)
            da_square(8 * TT - 1)
            raw_gate(0, DVT - 1, 1)
            for half in range(2):
                da_y(DA_HEADS - 1, half)

            def ret_values(m, part):
                b = bank_tr()
                filled("tr_full")
                t0, t1 = KV_TILES[part]
                nc.scalar.activation(rv_hi[:, t0:t1, m * P:(m + 1) * P],
                                     psum[:, b, 0:(t1 - t0) * P].rearrange("p (t n) -> p t n", n=P),
                                     ACT.Copy).then_inc(S["tr_hi"], 1)

            def ret_hi(dst):
                b = bank_proj()
                filled("proj_full")
                nc.scalar.activation(dst, psum[:, b, 0:dst.shape[-1]], ACT.Copy)\
                    .then_inc(S["proj_hi"], 1)

            def ret_keys(head):
                nc.scalar.activation(kt_hi[:, :], psum[:, SK, P:P + RDK], ACT.Copy,
                                     scale=dec[:, P + 1:P + 2]).then_inc(S["k_hi"], 1)

            def ret_state():
                wait("st_free")
                nc.scalar.activation(s_hi[:, :, :], state[:, :, :], ACT.Copy).then_inc(S["s_hi"], 1)

            def ret_y(head, c):
                b = bank_tr()
                filled("tr_full")
                slot = c % 2
                out = seen[f"ry_out{slot}"]
                act.wait_ge(S[f"ry_out{slot}"], out.value16())
                sem_b = free(b)
                nc.scalar.activation(ry_st[:, slot, :, :],
                                     psum[:, b, :].rearrange("p (t n) -> p t n", n=P), ACT.Copy)\
                    .then_inc(sem_b, 1)
                act.wait_ge(sem_b, seen[f"tr_free{b - TR}"].value())
                out.next()
                act.dma_start(t["yr"][head, :, :, c * P:(c + 1) * P], ry_st[:, slot, :, :])\
                    .then_inc(S[f"ry_out{slot}"], 16)

            with seen.loop(act, RET_HEADS, RET_TURN) as head:
                late = []
                for m in range(DVT):
                    for part in range(3):
                        b = bank_proj()
                        filled("proj_full")
                        c0, c1 = KV_PARTS[part]
                        nc.scalar.activation(rvt[:, PAD + c0:PAD + c1], psum[:, b, 0:c1 - c0], ACT.Copy)\
                            .then_inc(free(b), 1)
                        for m1, p1 in late:
                            ret_values(m1, p1)
                        late = [(m, part)]
                for d in range(DKT):
                    for part in range(3):
                        c0, c1 = KV_PARTS[part]
                        ret_hi(rk_hi[:, d, PAD + c0:PAD + c1])
                        for m1, p1 in late:
                            ret_values(m1, p1)
                        late = []
                for part in range(2):
                    ret_hi(rq_hi[:, 0, part * HALF:(part + 1) * HALF])
                wait("dec")
                wait("sk_full")
                ret_keys(head)
                ret_hi(rq_hi[:, 1, 0:HALF])
                ret_state()
                ret_hi(rq_hi[:, 1, HALF:SEQ])
                for c in range(TT):
                    wait("p_mul")
                    seen["sk_full"].next()
                    nc.scalar.activation(p_hi[:, :], p_f[:, :], ACT.Copy).then_inc(S["p_hi"], 1)
                    if c < TT - 1:
                        ret_keys(head)
                    wait("o_free")
                    nc.scalar.activation(junk3[:, :], o_n[:, c % 2, :], ACT.Square,
                                         accum_out=ss[:, c % 2:c % 2 + 1]).then_inc(S["o_sq"], 1)
                    if c < TT - 1:
                        ret_state()
                    raw_gate(head + 1, c // 2, c % 2)
                    if c:
                        ret_y(head, c - 1)
                ret_y(head, TT - 1)

            for slot in range(2):
                act.wait_ge(S[f"y_out{slot}"], seen[f"y_out{slot}"].value16())
            for m in range(KT):
                act.dma_start(acc[:, m, :], t["yd"][m]).then_inc(S[f"yd_in{m // 2}"], 16)
            for slot in range(2):
                act.wait_ge(S[f"ry_out{slot}"], seen[f"ry_out{slot}"].value16())
                act.wait_ge(S[f"g_out{slot}"], seen[f"g_out{slot}"].value16())

            def split_da(m):
                act.wait_ge(S[f"yd_in{m // 2}"], 32)
                nc.scalar.activation(y_hi[:, m, :], acc[:, m, :], ACT.Copy).then_inc(S["y_hi"], 1)

            def gate_half(m, half, dst):
                b = bank_proj()
                filled("proj_full")
                nc.scalar.activation(dst, psum[:, b, :], ACT.Sigmoid).then_inc(free(b), 1)

            def gate_slot(m, half):
                return gate[:, (m % 2) * 2 + half, :]

            for half in range(2):
                gate_half(0, half, gate_slot(0, half))
                for m in range(half * KT // 2, (half + 1) * KT // 2):
                    split_da(m)
            for half in range(2):
                gate_half(1, half, gate_slot(1, half))
            for m in range(KT):
                for half in range(2):
                    bank_proj()
                if m + 2 < KT:
                    for half in range(2):
                        gate_half(m + 2, half, gate_slot(m + 2, half))

            for b in range(2):
                act.wait_ge(S[f"proj_free{b}"], seen[f"proj_free{b}"].value())
            def load(n):
                slot = n % 2
                if n >= 2:
                    act.wait_ge(S["y_split"], KT + n - 1)
                act.dma_start(y_in[:, slot, :], t["yr"][n // 4, :, n % 4, :]).then_inc(S[f"y_in{slot}"], 16)
                act.dma_start(g_in[:, slot, :], t["gr"][n // 4, :, n % 4, :]).then_inc(S[f"y_in{slot}"], 16)

            def silu(n):
                slot = n % 2
                act.wait_ge(S[f"y_in{slot}"], 32 * (n // 2 + 1))
                nc.scalar.activation(g_in[:, slot, :], g_in[:, slot, :], ACT.Silu).then_inc(S["silu"], 1)

            def round_ret(n):
                wait("y_mul")
                nc.scalar.activation(r_hi[(n // 4) % 3][:, n % 4, :], y_in[:, n % 2, :], ACT.Copy)\
                    .then_inc(S["y_hi"], 1)

            def gate_ret(m, half):
                gate_half(m, half, g_ret[:, m, half * HALF:(half + 1) * HALF])

            load(0)
            load(1)
            for m in range(DVT):
                act.dma_start(g_ret[:, m, :], t["gr"][RET_HEADS, :, m, :]).then_inc(S["gr_in"], 16)
            gate_ret(4, 0)
            for n in (0, 2):
                silu(n)
                silu(n + 1)
                round_ret(n)
                gate_ret(4 + n, 1 if n == 0 else 0)
                round_ret(n + 1)
                load(n + 2)
                load(n + 3)
                if n == 0:
                    for half in range(2):
                        gate_ret(5, half)
            gate_ret(6, 1)
            act.wait_ge(S["gr_in"], 16 * DVT)
            nc.scalar.activation(g_ret[:, 0:2, :], g_ret[:, 0:2, :], ACT.Sigmoid).then_inc(S["g_raw"], 1)
            gate_ret(7, 0)
            nc.scalar.activation(g_ret[:, 2:4, :], g_ret[:, 2:4, :], ACT.Sigmoid).then_inc(S["g_raw"], 1)
            gate_ret(7, 1)

            base_proj = seen["proj_full"].n
            for hr in range(RET_HEADS - 1):
                for n in range(4 * hr + 4, 4 * hr + 8):
                    silu(n)
                    if n == 12:
                        act.wait_ge(S["proj_full"], base_proj + 16)
                    round_ret(n)
                    if n + 2 < 16:
                        load(n + 2)
                for _ in range(16):
                    bank_proj()

            def load_xt(m):
                act.dma_start(xt_in[:, m % 2, :], t["xt"][m]).then_inc(S[f"xt_in{m % 2}"], 16)

            def load_h(j):
                act.wait_ge(S["mrg_lo"], 2 * (j + 1))
                act.dma_start(h2[:, j, :], t["x"][j * P:(j + 1) * P, :]).then_inc(S["h_in"], 16)

            act.wait_ge(S["y_split"], KT + 4 * RET_HEADS)
            for m in range(2):
                load_xt(m)
            for g in range(2 * KT):
                m, tok = g // 2, slice((g % 2) * HALF, (g % 2 + 1) * HALF)
                b = bank_proj()
                act.wait_ge(S[f"proj_free{b}"], seen[f"proj_free{b}"].value())
                nc.scalar.activation(m_hi[:, m, tok], acc[:, m, tok], ACT.Copy).then_inc(S["mrg_hi"], 1)
                if g % 2 and m:
                    load_h(m - 1)
            load_h(TT - 1)

            for g in range(2 * KT):
                m, tok = g // 2, slice((g % 2) * HALF, (g % 2 + 1) * HALF)
                b = bank_proj()
                bank_tr()
                filled("proj_full")
                nc.scalar.activation(o_st[:, b, :], psum[:, b, :], ACT.Copy).then_inc(free(b), 1)
                wait("ht")
                nc.scalar.activation(y_hi[:, m, tok], h_t[:, b, :], ACT.Copy,
                                     scale=vecs[:, KT + m:KT + m + 1]).then_inc(S["u2_hi"], 1)
                if g % 2 and m + 2 < KT:
                    load_xt(m + 2)

            def mlp(first=False):
                for g in range(2 * FF_BLOCK):
                    b = bank_proj()
                    filled("proj_full")
                    nc.scalar.activation(f_r[:, b, :], psum[:, b, :], ACT.Relu).then_inc(free(b), 1)
                    wait("f_sq")
                    nc.scalar.activation(f_hi[:, g // 2, (g % 2) * HALF:(g % 2 + 1) * HALF],
                                         f_s[:, b, :], ACT.Copy).then_inc(S["f_hi"], 1)
                    if first and g == 0:
                        for n in range(2):
                            act.wait_ge(S[f"tr_free{n}"], seen[f"tr_free{n}"].value())
                    if first:
                        if g:
                            settle()
                        step(nc.scalar.activation(junk5[:, :], h2[:, g, :], ACT.Square,
                                                  accum_out=ss[:, g:g + 1]))
                for _ in range(2 * TT):
                    bank_proj()

            mlp(first=True)
            with seen.loop(act, N_BLOCKS - 2, MLP_TURN):
                mlp()
            mlp()

            act.wait_ge(S["proj_full"], seen["proj_full"].value(2 * TT - 1))
            act.dma_start(g_fin[:, :], t["g_fin"]).then_inc(S["fin_in"], 16)

            def store_out(j):
                act.wait_ge(S["fin"], j + 1)
                act.dma_start(t["out"][0, j * P:(j + 1) * P, :], out_st[:, j % OUT_SLOTS, :])\
                    .then_inc(S[f"out{j % OUT_SLOTS}"], 16)

            for j in range(TT):
                for b in range(2):
                    act.wait_ge(S[f"proj_free{b}"], seen[f"proj_free{b}"].value(TT - 1 - j))
                if j:
                    settle()
                step(nc.scalar.activation(f_r[:, :, :], h2[:, j, :].rearrange("p (a n) -> p a n", a=2),
                                          ACT.Square, accum_out=ss[:, j:j + 1]))
                if j:
                    store_out(j - 1)
            store_out(TT - 1)
            for slot in range(OUT_SLOTS):
                act.wait_ge(S[f"out{slot}"], 16 * TT // OUT_SLOTS)

        @block.vector
        def _(dve):
            seen = Tallies()
            turn = [0, 0, 0]

            def wait(name, k=1):
                dve.wait_ge(S[name], seen[name].next(k))

            def bank_proj():
                b = turn[0] % 2
                turn[0] += 1
                seen["proj_full"].next()
                seen[f"proj_free{b}"].next()
                return PROJ + b

            def bank_tr():
                b = turn[1] % 2
                turn[1] += 1
                seen["tr_full"].next()
                seen[f"tr_free{b}"].next()
                return TR + b

            def filled(name):
                dve.wait_ge(S[name], seen[name].value())

            def free(b):
                return S[f"proj_free{b}" if b < TR else f"tr_free{b - TR}"]

            def link(ins):
                ins.then_inc(S["dve"], 1)
                dve.wait_ge(S["dve"], seen["dve"].next())

            def mean(c0, c1, n):
                link(nc.vector.tensor_scalar(ms[:, c0:c1], ss[:, c0:c1], 1.0 / n, EPS, ALU.mult, ALU.add))

            def rsqrt_guess(c0, c1):
                x, y, w = ms[:, c0:c1], rs[:, c0:c1], nt[:, c0:c1]
                link(nc.vector.tensor_scalar(w.bitcast(I32), x.bitcast(I32), 1, None,
                                             ALU.logical_shift_right))
                link(nc.vector.tensor_scalar(y.bitcast(I32), w.bitcast(I32), -1.0, float(0x5F3759DF),
                                             ALU.mult, ALU.add))

            def rsqrt_steps(c0, c1, steps):
                x, y, w = ms[:, c0:c1], rs[:, c0:c1], nt[:, c0:c1]
                for _ in range(steps):
                    link(nc.vector.tensor_tensor(w, y, y, ALU.mult))
                    link(nc.vector.scalar_tensor_tensor(w, w, -0.5, x, ALU.mult, ALU.mult))
                    link(nc.vector.scalar_tensor_tensor(y, w, 1.5, y, ALU.add, ALU.mult))

            def rsqrt(c0, c1, n):
                mean(c0, c1, n)
                rsqrt_guess(c0, c1)
                rsqrt_steps(c0, c1, 3)

            def low(dst, b, hi, n):
                src = psum[:, b, 0:n]
                if len(dst.shape) == 3:
                    src = src.rearrange("p (t n) -> p t n", n=P)
                return nc.vector.tensor_tensor(dst, src, hi.bitcast(F32), ALU.subtract)

            nc.vector.memset(small[:, :], 0.0).then_inc(S["pads"], 1)
            dve.wait_ge(S["pads"], 1)
            dve.wait_ge(S["const_in"], 16 * 3)
            for j in range(2):
                q, k = lamv[:, 2 * j, :], lamv[:, 2 * j + 1, :]
                last = nc.vector.tensor_tensor_reduce(q, q, k, 1.0, 0.0, ALU.mult, ALU.add, lam[:, j:j + 1])
            last.then_inc(S["lam"], 1)
            nc.vector.tensor_copy(ident_r[:, :], ident[:, :])

            def square(j):
                dve.wait_ge(S[f"x_in{j}"], 16)
                link(nc.vector.tensor_tensor_reduce(junk_v[:, :], x_in[:, j, :], x_in[:, j, :], 1.0, 0.0,
                                                    ALU.mult, ALU.add, ss[:, j + 1:j + 2]))

            def diagonals(part):
                dve.wait_ge(S["act"], 3 + 2 * part)
                c0, c1 = (0, 5) if part == 0 else (5, 9)
                rsqrt(c0, c1, D)
                for j in range(4 * part, 4 * part + 4):
                    last = nc.vector.tensor_scalar(diag0[:, j, :], ident[:, :], rs[:, j + 1:j + 2], None,
                                                   ALU.mult)
                last.then_inc(S["diag"], 1)

            groups = 0

            def norm_turned(part, m):
                nonlocal groups
                groups += 1
                c0 = META + part * BANK
                wait("n_hi")
                nc.vector.scalar_tensor_tensor(u_lo[:, m, c0:c0 + BANK], psum[:, TR + (groups - 1) % 4, :],
                                               vecs[:, m:m + 1], u_hi[:, m, c0:c0 + BANK].bitcast(F32),
                                               ALU.mult, ALU.subtract).then_inc(S["n_free"], 1)

            square(1)
            square(3)
            diagonals(0)
            nc.vector.tensor_scalar(diag_m[:, :], ident[:, :], rs[:, 0:1], None, ALU.mult)\
                .then_inc(S["diag_m"], 1)
            for m in range(KT):
                norm_turned(0, m)
                if m in (0, 2):
                    square(m + 5)
                if m == 4:
                    diagonals(1)
            groups += 1
            wait("n_hi")
            for m in range(KT):
                last = nc.vector.scalar_tensor_tensor(u_lo[:, m, 0:META],
                                                      psum[:, TR + (groups - 1) % 4, m * META:(m + 1) * META],
                                                      vecs[:, m:m + 1], u_hi[:, m, 0:META].bitcast(F32),
                                                      ALU.mult, ALU.subtract)
            last.then_inc(S["n_free"], 1)
            for m in range(KT):
                norm_turned(1, m)

            dve.wait_ge(S["lam_e"], 1)
            link(nc.vector.tensor_tensor(lam[:, 4:5], lam[:, 3:4], lam[:, 2:3], ALU.subtract))
            nc.vector.tensor_scalar(neglam, lam[:, 4:5], -LAM_INIT, None, ALU.add)
            link(nc.vector.tensor_scalar(g_head, vecs[:, 2 * KT:2 * KT + 1], 1.0 - LAM_INIT, None, ALU.mult))
            dve.wait_ge(S["table_in"], 32)

            for par in range(2):
                nc.vector.memset(z[:, par, 0, 0:PAD], 0.0)
            nc.vector.memset(vt[:, 0:PAD], 0.0).then_inc(S["pads"], 1)

            def da_group(g, p):
                b = bank_proj()
                if g < 3:
                    return
                wait("proj_hi")
                c0, c1 = KV_PARTS[g - 3] if g < 6 else ((g - 6) * HALF, (g - 5) * HALF)
                for c in range(2):
                    rows, other = MAP_ROWS[c], MAP_ROWS[1 - c]
                    if g < 6:
                        hi, lo = ks[rows, p, c, c0:c1], k_lo[rows, p, c0:c1]
                    else:
                        hi, lo = qs[rows, p, c, c0:c1], qs[other, p, c, c0:c1]
                    last = nc.vector.tensor_tensor(lo, psum[rows, b, 0:c1 - c0], hi.bitcast(F32), ALU.subtract)
                last.then_inc(free(b), 1)

            def da_values(part, p):
                b = bank_tr()
                wait("tr_hi")
                t0, t1 = KV_TILES[part]
                low(v_da[:, p, t0:t1, 1, :], b, v_da[:, p, t0:t1, 0, :], (t1 - t0) * P)\
                    .then_inc(free(b), 1)

            def da_logits(s):
                i = s % TT
                pieces = key_pieces(i)
                for c in range(2):
                    for j, (k0, k1) in enumerate(pieces):
                        b = SC + score_bank(turn[2])[0]
                        turn[2] += 1
                        wait("sc_full")
                        off = k0 + P * (TT - 1 - i)
                        dve.nop(nofuse=True)
                        nc.vector.tensor_tensor_reduce(z[:, s % 2, c, PAD + k0:PAD + k1], psum[:, b, 0:k1 - k0],
                                                       bias[:, off:off + k1 - k0], 1.0, -3e38,
                                                       ALU.add, ALU.max, mx[:, c, j:j + 1])\
                            .then_inc(S["sc_free"], 1)
                        seen["sc_free"].next()
                dve.wait_ge(S["sc_free"], seen["sc_free"].value())
                link(nc.vector.tensor_reduce(mxc[:, :], mx[:, :, 0:len(pieces)], AX_X, ALU.max))
                nc.vector.tensor_scalar(nb[:, :], mxc[:, :], -DA_SCALE, None, ALU.mult).then_inc(S["nb"], 1)
                seen["nb"].next()

            def da_turned(g0, g1):
                b = bank_tr()
                wait("tr_hi")
                low(at_lo[:, g0:g1, :], b, at_hi[:, g0:g1, :], (g1 - g0) * P).then_inc(free(b), 1)

            def da_combine(s):
                par = s % 2
                if s > 1:
                    dve.wait_ge(S["pv_free"], seen["pv_free"].value())
                wait("expd", 2)
                link(nc.vector.reciprocal(rec[:, par, :], sums[:, par, :]))
                link(nc.vector.tensor_scalar(cf, sums[:, par, 0:1], neglam, rec[:, par, 1:2],
                                             ALU.mult, ALU.mult))
                nk = META + P * (s % TT + 1)
                z0, z1 = z[:, par, 0, PAD:PAD + nk], z[:, par, 1, PAD:PAD + nk]
                nc.vector.scalar_tensor_tensor(z0, z1, cf, z0, ALU.mult, ALU.add).then_inc(S["a_ready"], 1)

            def da_y(s):
                j, par = s % TT, (s // TT) % 2
                wait("pv_low")
                seen["pv_free"].next()
                y = y_q[:, par, j, :]
                nc.vector.scalar_tensor_tensor(y, psum[:, PV, 0:P], rec[:, s % 2, 0:1],
                                               y_low[:, s % 2, :], ALU.mult, ALU.add)\
                    .then_inc(S["pv_free"], 1)

            def da_norm(head, part):
                if part == 0:
                    wait("y_sq", TT)
                    mean(0, TT, P)
                if part == 1:
                    rsqrt_guess(0, TT)
                if part in (2, 3, 4):
                    rsqrt_steps(0, TT, 1)
                if part >= 4:
                    for j in range(4 * (part - 4), 4 * (part - 3)):
                        y = y_q[:, head % 2, j, :]
                        last = nc.vector.tensor_scalar(y, y, rs[:, j:j + 1], None, ALU.mult)
                    last.then_inc(S["y_ready"], 1)

            def group_of(s):
                if s < 7 * TT:
                    da_group(s % TT, (s // TT + 1) % 2)
                else:
                    bank_proj()

            def next_slope():
                link(nc.vector.tensor_scalar(bias[:, :], bias[:, :], 0.5, None, ALU.mult))

            def da_step(s, more=True):
                i = s % TT
                blocks = block_groups((s - 1) % TT) if s else []
                if i == NORM_AT[0] and s > TT:
                    da_norm(s // TT - 1, 0)
                da_logits(s)
                for g0, g1 in blocks[:2]:
                    da_turned(g0, g1)
                if s > 1:
                    da_y(s - 2)
                for g0, g1 in blocks[2:]:
                    da_turned(g0, g1)
                if i in TURN_AT and s > TT:
                    bank_tr()
                if more and i in (1, 2, 3):
                    da_values(i - 1, (s // TT + 1) % 2)
                if s:
                    group_of(s - 1)
                da_combine(s)
                if i in NORM_AT and s > TT:
                    da_norm(s // TT - 1, 1 + NORM_AT.index(i))
                if i == TT - 1 and more:
                    next_slope()

            next_slope()
            for g in range(8):
                da_group(g, 0)
                if g in (1, 2, 3):
                    da_values(g - 1, 0)
            for s in range(DA_PEEL):
                da_step(s)
            with seen.loop(dve, 3, DA_TURN):
                for s in range(DA_PEEL, DA_PEEL + 2 * TT):
                    da_step(s)
            for s in range(DA_PEEL + 6 * TT, 8 * TT):
                da_step(s, more=s < 7 * TT)
            for g0, g1 in block_groups(TT - 1):
                da_turned(g0, g1)
            da_y(8 * TT - 2)
            da_y(8 * TT - 1)
            for part in range(6):
                da_norm(DA_HEADS - 1, part)
            group_of(8 * TT - 1)
            for _ in range(2):
                bank_tr()

            for slot in range(2):
                dve.wait_ge(S[f"y_out{slot}"], 16 * (1 + DA_HEADS))
            for x in (rk_hi, rk_lo):
                for d in range(DKT):
                    nc.vector.memset(x[:, d, 0:PAD].bitcast(F32), 0.0)
            nc.vector.memset(rvt[:, 0:PAD], 0.0).then_inc(S["pads"], 1)

            def ret_values(m, part):
                b = bank_tr()
                wait("tr_hi")
                t0, t1 = KV_TILES[part]
                cols = slice(m * P, (m + 1) * P)
                low(rv_lo[:, t0:t1, cols], b, rv_hi[:, t0:t1, cols], (t1 - t0) * P).then_inc(free(b), 1)

            def ret_low(hi, lo):
                b = bank_proj()
                wait("proj_hi")
                low(lo, b, hi, lo.shape[-1]).then_inc(free(b), 1)

            def ret_keys(head):
                wait("k_hi")
                nc.vector.scalar_tensor_tensor(kt_lo[:, :], psum[:, SK, P:P + RDK], dec[:, P + 1:P + 2],
                                               kt_hi[:, :].bitcast(F32), ALU.mult, ALU.subtract)\
                    .then_inc(S["k_ready"], 1)

            def state_add(first):
                wait("st_full")
                flat = state[:, :, :].rearrange("p d n -> p (d n)")
                src = psum[:, ST:ST + DKT, :].rearrange("p d n -> p (d n)")
                if first:
                    ins = nc.vector.tensor_copy(flat, src)
                else:
                    ins = nc.vector.scalar_tensor_tensor(flat, flat, dec[:, P + 2:P + 3], src,
                                                         ALU.mult, ALU.add)
                seen["st_free"].next()
                ins.then_inc(S["st_free"], 1)

            def state_low():
                wait("s_hi")
                nc.vector.tensor_tensor(s_lo[:, :, :], state[:, :, :], s_hi[:, :, :].bitcast(F32),
                                        ALU.subtract).then_inc(S["s_ready"], 1)

            with seen.loop(dve, RET_HEADS, RET_TURN) as head:
                nc.vector.tensor_copy(dec[:, :], decay[:, head, :]).then_inc(S["dec"], 1)
                seen["dec"].next()
                dve.wait_ge(S["dec"], seen["dec"].value())
                late = []
                for m in range(DVT):
                    for part in range(3):
                        bank_proj()
                        for m1, p1 in late:
                            ret_values(m1, p1)
                        late = [(m, part)]
                for d in range(DKT):
                    for part in range(3):
                        c0, c1 = KV_PARTS[part]
                        ret_low(rk_hi[:, d, PAD + c0:PAD + c1], rk_lo[:, d, PAD + c0:PAD + c1])
                        for m1, p1 in late:
                            ret_values(m1, p1)
                        late = []
                for part in range(2):
                    cols = slice(part * HALF, (part + 1) * HALF)
                    ret_low(rq_hi[:, 0, cols], rq_lo[:, 0, cols])
                seen["sk_full"].next()
                ret_keys(head)
                ret_low(rq_hi[:, 1, 0:HALF], rq_lo[:, 1, 0:HALF])
                state_add(True)
                state_low()
                ret_low(rq_hi[:, 1, HALF:SEQ], rq_lo[:, 1, HALF:SEQ])
                for c in range(TT):
                    wait("sk_full")
                    nc.vector.tensor_tensor(p_f[:, :], psum[:, SK, 0:P], dec[:, 0:P], ALU.mult)\
                        .then_inc(S["p_mul"], 1)
                    wait("p_hi")
                    nc.vector.tensor_tensor(p_lo[:, :], p_f[:, :], p_hi[:, :].bitcast(F32), ALU.subtract)\
                        .then_inc(S["p_ready"], 1)
                    if c < TT - 1:
                        ret_keys(head)
                    wait("o_full")
                    nc.vector.tensor_scalar(o_n[:, c % 2, :], psum[:, OUT, :], dec[:, P:P + 1], None,
                                            ALU.mult).then_inc(S["o_free"], 1)
                    if c < TT - 1:
                        state_add(False)
                    wait("o_sq")
                    rsqrt(c % 2, c % 2 + 1, RDV)
                    nc.vector.tensor_scalar(diag_o[:, c % 2, :], ident[:, :], rs[:, c % 2:c % 2 + 1], None,
                                            ALU.mult).then_inc(S["o_diag"], 1)
                    if c < TT - 1:
                        state_low()
                    bank_proj()
                    bank_tr()
                dve.wait_ge(S["o_free"], seen["o_free"].next(TT))

            for m in range(KT):
                wait("y_hi")
                nc.vector.tensor_tensor(y_lo[:, m, :], acc[:, m, :], y_hi[:, m, :].bitcast(F32),
                                        ALU.subtract).then_inc(S["y_split"], 1)
            gate_at = {}

            def count_gate(m):
                for half in range(2):
                    b = bank_proj()
                    gate_at[m, half] = (b, seen[f"proj_free{b}"].value())

            count_gate(0)
            count_gate(1)
            dve.wait_ge(S["y_split"], KT)
            for m in range(KT):
                for half in range(2):
                    n, at_n = gate_at[m, half]
                    b = bank_proj()
                    filled("proj_full")
                    dve.wait_ge(S[f"proj_free{n}"], at_n)
                    nc.vector.tensor_tensor(acc[:, m, half * HALF:(half + 1) * HALF], psum[:, b, :],
                                            gate[:, (m % 2) * 2 + half, :], ALU.mult).then_inc(free(b), 1)
                if m + 2 < KT:
                    count_gate(m + 2)
            for _ in range(KT):
                bank_proj()

            def gate_y(n):
                wait("silu")
                nc.vector.tensor_tensor(y_in[:, n % 2, :], y_in[:, n % 2, :], g_in[:, n % 2, :], ALU.mult)\
                    .then_inc(S["y_mul"], 1)

            def split_low(n):
                wait("y_hi")
                nc.vector.tensor_tensor(r_lo[(n // 4) % 3][:, n % 4, :], y_in[:, n % 2, :],
                                        r_hi[(n // 4) % 3][:, n % 4, :].bitcast(F32), ALU.subtract)\
                    .then_inc(S["y_split"], 1)

            for n in range(DVT):
                gate_y(n)
                split_low(n)
            dve.wait_ge(S["g_raw"], 2)
            for b in range(2):
                dve.wait_ge(S[f"proj_free{b}"], seen[f"proj_free{b}"].value())

            def ret_add(g):
                m, tok = g // 2, slice((g % 2) * HALF, (g % 2 + 1) * HALF)
                b = bank_proj()
                filled("proj_full")
                dve.wait_ge(free(b), seen[f"proj_free{b}"].value(1))
                link(nc.vector.tensor_tensor(psum[:, b, :], psum[:, b, :], g_ret[:, m, tok], ALU.mult))
                nc.vector.tensor_tensor(acc[:, m, tok], acc[:, m, tok], psum[:, b, :], ALU.add)\
                    .then_inc(free(b), 1)

            for hr in range(RET_HEADS - 1):
                for g in range(2 * KT):
                    ret_add(g)
                    n = 4 * hr + 4 + g // 3
                    if g < 12 and g % 3 == 0:
                        gate_y(n)
                    if g < 12 and g % 3 == 1:
                        split_low(n)

            def merge_low(g):
                m, tok = g // 2, slice((g % 2) * HALF, (g % 2 + 1) * HALF)
                wait("mrg_hi")
                nc.vector.tensor_tensor(m_lo[:, m, tok], acc[:, m, tok], m_hi[:, m, tok].bitcast(F32),
                                        ALU.subtract).then_inc(S["mrg_lo"], 1)

            for g in range(2 * KT):
                ret_add(g)
                if g:
                    merge_low(g - 1)
            merge_low(2 * KT - 1)

            def add_turned(g):
                m, half = g // 2, g % 2
                b = bank_tr()
                filled("tr_full")
                h = h2[:, 4 * half:4 * half + 4, m * P:(m + 1) * P]
                nc.vector.tensor_tensor(h, h, psum[:, b, :].rearrange("p (t n) -> p t n", n=P), ALU.add)\
                    .then_inc(free(b), 1)

            for g in range(2 * KT):
                m, tok = g // 2, slice((g % 2) * HALF, (g % 2 + 1) * HALF)
                b = bank_proj()
                dve.wait_ge(free(b), seen[f"proj_free{b}"].value())
                dve.wait_ge(S[f"xt_in{m % 2}"], 16 * (m // 2 + 1))
                nc.vector.tensor_tensor(h_t[:, b, :], o_st[:, b, :], xt_in[:, m % 2, tok], ALU.add)\
                    .then_inc(S["ht"], 1)
                wait("u2_hi")
                seen["ht"].next()
                nc.vector.scalar_tensor_tensor(y_lo[:, m, tok], h_t[:, b, :], vecs[:, KT + m:KT + m + 1],
                                               y_hi[:, m, tok].bitcast(F32), ALU.mult, ALU.subtract)\
                    .then_inc(S["u2_lo"], 1)
                if g == 1:
                    dve.wait_ge(S["h_in"], 16 * TT)
                if g:
                    add_turned(g - 1)
            add_turned(2 * KT - 1)

            def mlp(first=False, then=None):
                for g in range(2 * FF_BLOCK):
                    b = bank_proj()
                    dve.wait_ge(free(b), seen[f"proj_free{b}"].value())
                    nc.vector.tensor_tensor(f_s[:, b, :], f_r[:, b, :], f_r[:, b, :], ALU.mult)\
                        .then_inc(S["f_sq"], 1)
                    wait("f_hi")
                    seen["f_sq"].next()
                    tok = slice((g % 2) * HALF, (g % 2 + 1) * HALF)
                    nc.vector.tensor_tensor(f_lo[:, g // 2, tok], f_s[:, b, :],
                                            f_hi[:, g // 2, tok].bitcast(F32), ALU.subtract)\
                        .then_inc(S["f_lo"], 1)
                    seen["f_lo"].next()
                if first:
                    dve.wait_ge(S["act"], FIRST_SUMS + TT)
                    link(nc.vector.tensor_scalar(ms[:, 0:TT], ss[:, 0:TT], 1.0 / D, EPS, ALU.mult, ALU.add))
                    link(nc.vector.reciprocal(rs2, ms[:, 0:TT]))
                for tok in range(TT):
                    for half in range(2):
                        b = bank_proj()
                        filled("proj_full")
                        dve.wait_ge(free(b), seen[f"proj_free{b}"].value(1))
                        h = h2[:, tok, half * BANK:(half + 1) * BANK]
                        nc.vector.scalar_tensor_tensor(h, psum[:, b, :], rs2[:, tok:tok + 1], h, ALU.mult,
                                                       ALU.add).then_inc(free(b), 1)
                    if then and tok:
                        then(tok - 1)

            def finish(j):
                if j == 0:
                    dve.wait_ge(S["fin_in"], 16)
                dve.wait_ge(S["act"], FIRST_SUMS + TT + j + 1)
                rsqrt(j, j + 1, D)
                if j >= OUT_SLOTS:
                    dve.wait_ge(S[f"out{j % OUT_SLOTS}"], 16 * (j // OUT_SLOTS))
                nc.vector.scalar_tensor_tensor(out_st[:, j % OUT_SLOTS, :], h2[:, j, :], rs[:, j:j + 1],
                                               g_fin[:, :], ALU.mult, ALU.mult).then_inc(S["fin"], 1)

            mlp(first=True)
            with seen.loop(dve, N_BLOCKS - 2, MLP_TURN):
                mlp()
            mlp(then=finish)
            finish(TT - 1)


def feature_tiles(w):
    k, m = w.shape
    return w.reshape(k // P, P, m // P, P).transpose(2, 1, 0, 3).reshape(m // P, P, k)


def weight_stream(w_in, w_da, w_ret, w_out, w_up, w_down):
    tiles = feature_tiles(w_in)
    qa, ka, va, qr, kr, vr, gr, g_a, g_r = 0, 8, 16, 24, 32, 40, 56, 72, 80
    order = []
    for h in range(DA_HEADS):
        order += [va + h, ka + h, qa + h]
    gates = [gr + j for j in range(2 * D // P)] + [g_r + j for j in range(DVT)]
    order += gates[:DVT]
    for h in range(RET_HEADS):
        order += [vr + DVT * h + j for j in range(DVT)]
        order += [kr + DKT * h + j for j in range(DKT)] + [qr + DKT * h + j for j in range(DKT)]
        order += gates[DVT * (h + 1):DVT * (h + 2)]
    da, gate_a = feature_tiles(w_da), tiles[g_a:g_a + KT]
    both = np.concatenate([gate_a[:2], np.stack([da[:-2], gate_a[2:]], axis=1).reshape(-1, P, D), da[-2:]])
    ret = w_ret.reshape(RET_HEADS, DVT, P, 4, 2, P).transpose(0, 3, 2, 4, 1, 5).reshape(16, P, D)
    up, down = feature_tiles(w_up), w_down.reshape(FF // P, P, D)
    both_mlp = {"up": up.reshape(N_BLOCKS, FF_BLOCK, P, D), "down": down.reshape(N_BLOCKS, FF_BLOCK, P, D)}
    mlp = np.stack([both_mlp[kind][:, j] for kind, j in MLP_ORDER], axis=1)
    mlp[0] = np.stack([both_mlp[kind][0, j] for kind, j in MLP_FIRST])
    return np.concatenate([tiles[np.array(order)], both, tiles[g_r + DVT:g_r + KT], ret, feature_tiles(w_out),
                           mlp.reshape(-1, P, D)])


def decay_tables():
    j, i = np.arange(P, dtype=np.float64)[:, None], np.arange(P, dtype=np.float64)[None, :]
    out = np.zeros((P, RET_HEADS, P + 3))
    for h in range(RET_HEADS):
        g = 1.0 - 2.0 ** (-5.0 - h)
        out[:, h, 0:P] = np.where(i >= j, g ** -(j + 1.0), 0.0) * RDK ** -0.5
        out[:, h, P] = g ** (j[:, 0] + 1.0)
        out[:, h, P + 1] = g ** (P - 1.0 - j[:, 0]) * RDK ** -0.5
        out[:, h, P + 2] = g ** P
    return out.astype(np.float32)


def distance_table():
    q, k = np.arange(P)[:, None] + META + SEQ - P, np.arange(L)[None, :]
    return np.where(k <= q, (k - q) / DA_SCALE, -1e30).astype(np.float32)


def kernel(x, meta_tokens, norm_mix_g, w_in, da_lambda_q1, da_lambda_k1, da_lambda_q2, da_lambda_k2,
           da_head_g, w_proj_da, w_proj_ret, w_out, norm_mlp_g, w_up, w_down, final_norm_g):
    import concourse.bacc as bacc
    from concourse.bass_utils import run_bass_kernel_spmd

    np_in = {
        "x": np.asarray(x)[0],
        "xt": np.asarray(x)[0].T.reshape(KT, P, SEQ),
        "meta": np.asarray(meta_tokens),
        "w": weight_stream(np.asarray(w_in)[0], np.asarray(w_proj_da)[0], np.asarray(w_proj_ret)[0],
                           np.asarray(w_out)[0], np.asarray(w_up)[0], np.asarray(w_down)[0]),
        "vecs": np.concatenate([np.asarray(norm_mix_g)[0].reshape(KT, P),
                                np.asarray(norm_mlp_g)[0].reshape(KT, P),
                                np.asarray(da_head_g)[0].reshape(1, P)]).T,
        "lamv": np.broadcast_to(np.stack([np.asarray(v)[0] for v in (
            da_lambda_q1, da_lambda_k1, da_lambda_q2, da_lambda_k2)])[None], (P, 4, DH)),
        "g_fin": np.broadcast_to(np.asarray(final_norm_g)[None], (P, D)),
        "ident": np.eye(P, dtype=np.float32),
        "dist": distance_table(),
        "decay": decay_tables(),
    }
    nc = bacc.Bacc("TRN2", target_bir_lowering=False, num_devices=1)
    arrays, t = {}, {}
    for name, a in np_in.items():
        a = np.ascontiguousarray(a)
        arrays[f"in_{name}"] = a
        t[name] = nc.dram_tensor(f"in_{name}", a.shape, mybir.dt.from_np(a.dtype), kind="ExternalInput").ap()
    t["out"] = nc.dram_tensor("out_0", (1, SEQ, D), F32, kind="ExternalOutput").ap()
    t["yd"] = nc.dram_tensor("y_da_scratch", (DA_HEADS, P, SEQ), F32, kind="Internal").ap()
    t["yr"] = nc.dram_tensor("y_ret_scratch", (RET_HEADS, P, DVT, SEQ), F32, kind="Internal").ap()
    t["gr"] = nc.dram_tensor("gate_scratch", (RET_HEADS + 1, P, DVT, SEQ), F32, kind="Internal").ap()
    build(nc, t)
    r = run_bass_kernel_spmd(nc, [arrays], core_ids=[0])
    return r.results[0]["out_0"]
```
